# Optimizing a Trainium2 kernel written in Bass

```python
import jax, jax.numpy as jnp
from jax import lax
import numpy as np

D_MODEL = 1024
BATCH = 1
SEQ = 512
DEPTH = 2
DEC_BATCH = 1
DEC_SEQ = 64
PAST_LEN = 1024

CHUNK = 64
Q_BLOCK = 128
N_HEADS = 8
QK_NOPE = 64
QK_ROPE = 32
QK_HEAD = QK_NOPE + QK_ROPE
V_HEAD = 64
Q_LORA = 256
KV_LORA = 128
ROPE_THETA = 10000.0
ATTN_WIDTH = N_HEADS * V_HEAD
GMLP_GROUPS = 8
GMLP_GROUP_DIM = 64
GMLP_WIDTH = GMLP_GROUPS * GMLP_GROUP_DIM
GMLP_CHUNK = 128
MIX_WIDTH = ATTN_WIDTH + GMLP_WIDTH
IN_COLS = Q_LORA + KV_LORA + QK_ROPE + 2 * GMLP_WIDTH
SPLITS = (Q_LORA, Q_LORA + KV_LORA, Q_LORA + KV_LORA + QK_ROPE,
          Q_LORA + KV_LORA + QK_ROPE + GMLP_WIDTH)
D_FF = ((-(-8 * D_MODEL // 3) + 255) // 256) * 256
EPS = 1e-6
NEG_INF = -1e30

kernel_name = 'hybrid_mla_gmlp_stream_step'

def rms_norm(x, g):
    xf = x.astype(jnp.float32)
    y = xf * lax.rsqrt(jnp.mean(jnp.square(xf), axis=-1, keepdims=True) + EPS)
    return (y * g.astype(jnp.float32)).astype(x.dtype)

def layer_norm(x, g, b):
    xf = x.astype(jnp.float32)
    mu = jnp.mean(xf, axis=-1, keepdims=True)
    xc = xf - mu
    y = xc * lax.rsqrt(jnp.mean(jnp.square(xc), axis=-1, keepdims=True) + EPS)
    return (y * g.astype(jnp.float32) + b.astype(jnp.float32)).astype(x.dtype)

def rope_angles(pos):
    half = QK_ROPE // 2
    inv = ROPE_THETA ** (-jnp.arange(half, dtype=jnp.float32) / half)
    ang = pos.astype(jnp.float32)[:, None] * inv[None, :]
    return jnp.cos(ang), jnp.sin(ang)

def apply_rope(x, cos, sin):
    half = QK_ROPE // 2
    xf = x.astype(jnp.float32)
    x1, x2 = xf[..., :half], xf[..., half:]
    return jnp.concatenate([x1 * cos - x2 * sin, x1 * sin + x2 * cos], axis=-1).astype(x.dtype)

def attend_block(qb, qpos_b, k, v, kpos):
    s = jnp.einsum('bqhe,bkhe->bhqk', qb, k, preferred_element_type=jnp.float32) * (QK_HEAD ** -0.5)
    vis = (kpos[None, :] // CHUNK) <= (qpos_b[:, None] // CHUNK)
    s = jnp.where(vis[None, None], s, NEG_INF)
    p = jax.nn.softmax(s, axis=-1)
    return jnp.einsum('bhqk,bkhd->bqhd', p.astype(v.dtype), v)

def block_causal_attention(q, k, v, qpos, kpos):
    B, S, H, E = q.shape
    if S <= Q_BLOCK:
        return attend_block(q, qpos, k, v, kpos)
    nb = S // Q_BLOCK
    qb = q.reshape(B, nb, Q_BLOCK, H, E).transpose(1, 0, 2, 3, 4)
    ob = lax.map(lambda a: attend_block(a[0], a[1], k, v, kpos), (qb, qpos.reshape(nb, Q_BLOCK)))
    return ob.transpose(1, 0, 2, 3, 4).reshape(B, S, H, V_HEAD)

def spatial_gating(u, v, ln_g, ln_b, w_s, b_s):
    B, S, _ = u.shape
    L = min(S, GMLP_CHUNK)
    nc = S // L
    ug = jax.nn.gelu(u).reshape(B, S, GMLP_GROUPS, GMLP_GROUP_DIM)
    vn = layer_norm(jax.nn.gelu(v).reshape(B, S, GMLP_GROUPS, GMLP_GROUP_DIM), ln_g, ln_b)
    idx = jnp.arange(L)
    causal = (idx[:, None] // CHUNK) >= (idx[None, :] // CHUNK)
    ws = jnp.where(causal[None], w_s[:, :L, :L], 0.0)
    mixed = jnp.einsum('gij,bcjgd->bcigd', ws, vn.reshape(B, nc, L, GMLP_GROUPS, GMLP_GROUP_DIM))
    mixed = mixed + b_s[:, :L].T[None, None, :, :, None]
    out = ug * mixed.reshape(B, S, GMLP_GROUPS, GMLP_GROUP_DIM)
    return out, vn.reshape(B, S, GMLP_WIDTH)

def hybrid_layer(x, pos, ckv_past, kr_past, p):
    B, S, _ = x.shape
    h = rms_norm(x, p['g_mix'])
    z = h @ p['w_in']
    q_lat, c_kv, k_r, u, v = jnp.split(z, SPLITS, axis=-1)
    cos, sin = rope_angles(pos)
    q = (rms_norm(q_lat, p['g_q_lora']) @ p['w_q_up']).reshape(B, S, N_HEADS, QK_HEAD)
    q_nope = rms_norm(q[..., :QK_NOPE], p['g_qn'])
    q_rope = apply_rope(rms_norm(q[..., QK_NOPE:], p['g_qr']), cos[:, None, :], sin[:, None, :])
    q = jnp.concatenate([q_nope, q_rope], axis=-1)
    c_kv = rms_norm(c_kv, p['g_kv_lora'])
    k_r = apply_rope(rms_norm(k_r, p['g_kr']), cos, sin)
    if ckv_past is None:
        ckv_all, kr_all, kpos = c_kv, k_r, pos
    else:
        ckv_all = jnp.concatenate([ckv_past, c_kv], axis=1)
        kr_all = jnp.concatenate([kr_past, k_r], axis=1)
        kpos = jnp.arange(ckv_all.shape[1])
    T = ckv_all.shape[1]
    kv = (ckv_all @ p['w_kv_up']).reshape(B, T, N_HEADS, QK_NOPE + V_HEAD)
    k_nope = rms_norm(kv[..., :QK_NOPE], p['g_kn'])
    v_att = kv[..., QK_NOPE:]
    k = jnp.concatenate([k_nope, jnp.broadcast_to(kr_all[:, :, None, :], (B, T, N_HEADS, QK_ROPE))], axis=-1)
    o_att = block_causal_attention(q, k, v_att, pos, kpos)
    o_gm, v_rows = spatial_gating(u, v, p['gm_ln_g'], p['gm_ln_b'], p['gm_w_s'], p['gm_b_s'])
    merged = jnp.concatenate([rms_norm(o_att, p['g_out_att']).reshape(B, S, ATTN_WIDTH),
                              rms_norm(o_gm, p['g_out_gm']).reshape(B, S, GMLP_WIDTH)], axis=-1)
    x = x + merged @ p['w_o']
    h2 = rms_norm(x, p['g_ffn'])
    x = x + (jax.nn.silu(h2 @ p['w_gate']) * (h2 @ p['w_up'])) @ p['w_down']
    return x, c_kv, k_r, v_rows

def setup_inputs(seed: int = 0) -> dict:
    key = jax.random.key(seed)
    ks = jax.random.split(key, 26)

    def nrm(k, shape, scale):
        return scale * jax.random.normal(k, shape, jnp.float32)

    def gain(k, shape):
        return 1.0 + 0.02 * jax.random.normal(k, shape, jnp.float32)

    return {
        'x_prompt': nrm(ks[0], (BATCH, SEQ, D_MODEL), 1.0),
        'x_sample': nrm(ks[1], (DEC_BATCH, DEC_SEQ, D_MODEL), 1.0),
        'cache_ckv': nrm(ks[2], (DEPTH, DEC_BATCH, PAST_LEN, KV_LORA), 1.0),
        'cache_krope': nrm(ks[3], (DEPTH, DEC_BATCH, PAST_LEN, QK_ROPE), 1.0),
        'g_mix': gain(ks[4], (DEPTH, D_MODEL)),
        'w_in': nrm(ks[5], (DEPTH, D_MODEL, IN_COLS), D_MODEL ** -0.5),
        'g_q_lora': gain(ks[6], (DEPTH, Q_LORA)),
        'w_q_up': nrm(ks[7], (DEPTH, Q_LORA, N_HEADS * QK_HEAD), Q_LORA ** -0.5),
        'g_qn': gain(ks[8], (DEPTH, QK_NOPE)),
        'g_qr': gain(ks[9], (DEPTH, QK_ROPE)),
        'g_kv_lora': gain(ks[10], (DEPTH, KV_LORA)),
        'g_kr': gain(ks[11], (DEPTH, QK_ROPE)),
        'w_kv_up': nrm(ks[12], (DEPTH, KV_LORA, N_HEADS * (QK_NOPE + V_HEAD)), KV_LORA ** -0.5),
        'g_kn': gain(ks[13], (DEPTH, QK_NOPE)),
        'gm_ln_g': gain(ks[14], (DEPTH, GMLP_GROUPS, GMLP_GROUP_DIM)),
        'gm_ln_b': nrm(ks[15], (DEPTH, GMLP_GROUPS, GMLP_GROUP_DIM), 0.02),
        'gm_w_s': nrm(ks[16], (DEPTH, GMLP_GROUPS, GMLP_CHUNK, GMLP_CHUNK), GMLP_CHUNK ** -0.5),
        'gm_b_s': 1.0 + nrm(ks[17], (DEPTH, GMLP_GROUPS, GMLP_CHUNK), 0.1),
        'g_out_att': gain(ks[18], (DEPTH, N_HEADS, V_HEAD)),
        'g_out_gm': gain(ks[19], (DEPTH, GMLP_GROUPS, GMLP_GROUP_DIM)),
        'w_o': nrm(ks[20], (DEPTH, MIX_WIDTH, D_MODEL), MIX_WIDTH ** -0.5),
        'g_ffn': gain(ks[21], (DEPTH, D_MODEL)),
        'w_gate': nrm(ks[22], (DEPTH, D_MODEL, D_FF), D_MODEL ** -0.5),
        'w_up': nrm(ks[23], (DEPTH, D_MODEL, D_FF), D_MODEL ** -0.5),
        'w_down': nrm(ks[24], (DEPTH, D_FF, D_MODEL), D_FF ** -0.5),
    }

def reference(x_prompt, x_sample, cache_ckv, cache_krope, g_mix, w_in, g_q_lora, w_q_up,
              g_qn, g_qr, g_kv_lora, g_kr, w_kv_up, g_kn, gm_ln_g, gm_ln_b, gm_w_s, gm_b_s,
              g_out_att, g_out_gm, w_o, g_ffn, w_gate, w_up, w_down):
    past = cache_ckv.shape[2]
    pos_p = jnp.arange(x_prompt.shape[1])
    pos_s = past + jnp.arange(x_sample.shape[1])
    yp, ys = x_prompt, x_sample
    ckv_p, kr_p, ckv_s, kr_s, gv_s = [], [], [], [], []
    for l in range(DEPTH):
        p = {'g_mix': g_mix[l], 'w_in': w_in[l], 'g_q_lora': g_q_lora[l], 'w_q_up': w_q_up[l],
             'g_qn': g_qn[l], 'g_qr': g_qr[l], 'g_kv_lora': g_kv_lora[l], 'g_kr': g_kr[l],
             'w_kv_up': w_kv_up[l], 'g_kn': g_kn[l], 'gm_ln_g': gm_ln_g[l], 'gm_ln_b': gm_ln_b[l],
             'gm_w_s': gm_w_s[l], 'gm_b_s': gm_b_s[l], 'g_out_att': g_out_att[l],
             'g_out_gm': g_out_gm[l], 'w_o': w_o[l], 'g_ffn': g_ffn[l], 'w_gate': w_gate[l],
             'w_up': w_up[l], 'w_down': w_down[l]}
        yp, c, r, _ = hybrid_layer(yp, pos_p, None, None, p)
        ckv_p.append(c)
        kr_p.append(r)
        ys, c, r, gv = hybrid_layer(ys, pos_s, cache_ckv[l], cache_krope[l], p)
        ckv_s.append(c)
        kr_s.append(r)
        gv_s.append(gv)
    return (yp, ys, jnp.stack(ckv_p), jnp.stack(kr_p), jnp.stack(ckv_s), jnp.stack(kr_s), jnp.stack(gv_s))


_drawn_inputs = setup_inputs


def setup_inputs(seed=0):
    import zlib

    import numpy as np

    out = dict(_drawn_inputs(seed))
    spreads = {}
    factors = {'g_q_lora': 3.794,
     'g_qn': 3.848,
     'g_qr': 8.0,
     'g_kr': 2.697,
     'g_kn': 4.231,
     'gm_ln_g': 2.796,
     'gm_ln_b': 2.779,
     'g_out_att': 3.657,
     'g_out_gm': 3.891,
     'g_ffn': 3.585}
    for name, (base, spread) in spreads.items():
        noise = np.random.default_rng([zlib.crc32(name.encode()), seed]).standard_normal(out[name].shape)
        drawn = base * np.exp(spread * noise) if base else spread * noise
        out[name] = __import__('jax').numpy.asarray(drawn.astype(out[name].dtype))
    for name, factor in factors.items():
        out[name] = (out[name] * factor).astype(out[name].dtype)
    return out
```

```python
from contextlib import ExitStack

import numpy as np

import concourse.bass as bass
from concourse import mybir

D_MODEL, SEQ, DEC, DEPTH, PAST = 1024, 512, 64, 2, 1024
HEADS, NOPE, ROPE, VDIM = 8, 64, 32, 64
QK = NOPE + ROPE
Q_LORA, KV_LORA = 256, 128
GROUPS, GDIM = 8, 64
WIDTH = GROUPS * GDIM
D_FF = 2816
CHUNK = 64
EPS = 1e-6
SCALE = float(QK) ** -0.5
NEG_INF = -1e30
THETA = 10000.0

P = 128
TOK = SEQ + DEC
HALF = TOK // 2
KT = D_MODEL // P
TILE_AT = [0, 128, 256, 384, TOK - P]
NT = len(TILE_AT)
PT_ = SEQ // P
CACHE_TILES = PAST // P
S_KEYS = PAST + DEC
ALL_KEYS = S_KEYS + SEQ
KV_KR = KV_LORA + ROPE
BLOCK = 2048
COLS = BLOCK // KT
FPAIRS = D_FF // COLS
BODIES = (FPAIRS - 1) // 2
assert FPAIRS == 1 + 2 * BODIES

F32 = mybir.dt.float32
F32R = mybir.dt.float32r
ALU = mybir.AluOpType
ACT = mybir.ActivationFunctionType
AX = mybir.AxisListType

G_MIX, G_FFN, G_QL, G_BS, G_OUT = 0, 16, 32, 36, 52
G_QN, G_KN = 68, 70
G_BS_S = 72
G_ROWS = 88


class Unit:

    def __init__(self, n, done, before, freed):
        self.n, self.bank, self.done, self.before, self.freed = n, n % 8, done, before, freed


class Ring:

    def __init__(self):
        self.units, self.values, self.done = [], {}, 0

    def before(self):
        return self.units[-8].freed if len(self.units) >= 8 else None

    def add(self, sem, with_last=False):
        if not with_last:
            self.values[sem] = self.values.get(sem, 0) + 1
        self.done += 1
        u = Unit(len(self.units), self.done, self.before(), (sem, self.values[sem]))
        self.units.append(u)
        return u

    def skip(self):
        self.units.append(Unit(len(self.units), self.done, None, self.before()))

    def repeat(self, first, times):
        body = self.units[first:]
        size = len(body)
        sem = body[0].freed[0]
        assert size % 8 == 0 and all(u.freed[0] == sem for u in body)
        per = len({u.freed[1] for u in body})
        for t in range(1, times):
            for u in body:
                self.units.append(Unit(len(self.units), u.done + size * t, self.before(),
                                       (sem, u.freed[1] + per * t)))
        self.done += size * (times - 1)
        self.values[sem] += per * (times - 1)
        for j, u in enumerate(body):
            steady = self.units[first + size + j].before
            u.before = (sem, steady[1] - per)
            assert u.before[1] > 0
        return size, per


class Slots:

    def __init__(self):
        self.raw, self.n_split, self.last = [], 0, {}

    def load(self, split=True):
        self.raw.append(self.n_split if split else None)
        self.n_split += split
        return len(self.raw) - 1

    def used(self, n, unit):
        self.last[n] = unit


def batches():
    cache = [("k", [j, j + 1]) for j in range(0, CACHE_TILES, 2)]
    own = CACHE_TILES
    return ([("q", [PT_])] + cache + [("k", [own])],
            [("q", [0, 1]), ("q", [2, 3]), ("k", [own + 1, own + 2]), ("k", [own + 3, own + 4])])


def key_tile(j):
    if j < CACHE_TILES:
        return j * P, P
    if j == CACHE_TILES:
        return PAST, DEC
    return S_KEYS + (j - CACHE_TILES - 1) * P, P


S_BATCHES, P_BATCHES = batches()
NB = len(S_BATCHES) + len(P_BATCHES)
S_SPANS = [(0, 512), (512, 512), (1024, 64)]
S_TRANS = [(0, 4), (4, 4), (8, 1)]
HEAD_PAIRS = HEADS // 2
P_STEPS = [(i, h, n) for i, n in ((0, 4), (1, 2), (2, 1), (3, 1)) for h in range(0, HEADS, n)]
STEPS = HEAD_PAIRS + len(P_STEPS)
O_GROUPS = (PT_ * WIDTH + HEAD_PAIRS * VDIM) // VDIM
SMALL, GAIN_LOADS = 8, 11
ROOTS = (["r1", "kv", "q", "ln"] + [f"b{n}" for n in range(len(S_BATCHES))] + ["gm"]
         + [f"b{n}" for n in range(len(S_BATCHES), NB)] + ["o", "r2"])


def root_no(l, name):
    return l * len(ROOTS) + ROOTS.index(name) + 1


def build_plan():
    ring, slots, plan = Ring(), Slots(), []
    gains = ring.add("gains_turned")
    xt = [[ring.add("x_turned_dve"), ring.add("x_turned_act")] for _ in range(NT)]
    for l in range(DEPTH):
        L = {}
        L["w_in"] = w = [slots.load() for _ in range(6)]
        L["kv"] = [ring.add("kv_out") for _ in range(NT)]
        slots.used(w[0], L["kv"][-1])
        L["ss1"] = ring.add("sumsq_out")
        L["q"] = [[ring.add("qlat_out") for _ in range(2)] for _ in range(2)]
        slots.used(w[1], L["q"][-1][-1])
        L["v0"] = [ring.add("gelu_out") for _ in range(NT)]
        L["ssq"] = ring.add("sumsq_out")
        for name in ("v1", "u0", "u1"):
            L[name] = [ring.add("gelu_out") for _ in range(NT)]
        for j, name in enumerate(("v0", "v1", "u0", "u1")):
            slots.used(w[2 + j], L[name][-1])
        L["wq"], L["wkv"] = slots.load(False), slots.load(False)
        L["ct"] = [ring.add("ckvt_act" if j % 2 else "ckvt_dve") for j in range(4)]
        L["wst"] = [ring.add("wst_out") for _ in range(3)]

        def turn(b):
            b["turn"] = [(ring.add("qkt_dve"), ring.add("qkt_act")) for _ in b["tiles"]]

        def group(todo, seq):
            out = []
            for what, tiles in todo:
                b = {"what": what, "tiles": tiles, "seq": seq + len(out)}
                b["up"] = [(ring.add("qz_out" if what == "q" else "k_scaled"),
                            ring.add("qz_out" if what == "q" else "v_out")) for _ in tiles]
                out.append(b)
                if len(out) > 1:
                    turn(out[-2])
            turn(out[-1])
            return out

        L["s_batches"] = group(S_BATCHES, 0)
        L["mix"] = [ring.add("mix_out") for _ in range(5)]
        L["s_steps"] = steps = [{} for _ in range(HEAD_PAIRS)]
        for n in range(HEAD_PAIRS + 2):
            if n < HEAD_PAIRS:
                steps[n]["s"] = [ring.add("s_exp") for _ in S_SPANS]
            if 1 <= n <= HEAD_PAIRS:
                steps[n - 1]["t"] = [ring.add("pt_dve"), ring.add("pt_act"), ring.add("pt_dve")]
            if n >= 2:
                steps[n - 2]["o"] = ring.add("o_out")
        L["p_batches"] = group(P_BATCHES, len(S_BATCHES))
        L["batches"] = L["s_batches"] + L["p_batches"]
        slots.used(L["wq"], L["p_batches"][1]["up"][-1][1])
        slots.used(L["wkv"], L["p_batches"][3]["up"][-1][1])
        L["p_steps"] = steps = [{} for _ in P_STEPS]
        for n in range(len(P_STEPS) + 2):
            if n < len(P_STEPS):
                steps[n]["s"] = ring.add("s_exp")
            if 1 <= n <= len(P_STEPS):
                steps[n - 1]["t"] = ring.add("pt_act" if (n - 1) % 2 == 0 else "pt_dve")
            if n >= 2:
                steps[n - 2]["o"] = ring.add("o_out")
        L["mt"] = [ring.add("merged_out") for _ in range(KT + 1)]
        L["w_o"] = [slots.load() for _ in range(4)]
        if len(ring.units) % 2:
            ring.skip()
        L["wo"] = [[ring.add("wo_added", with_last=h > 0) for h in range(2)] for _ in range(KT)]
        for j, n in enumerate(L["w_o"]):
            slots.used(n, L["wo"][2 * j + 1][1])

        def pair_units(n):
            out = [[ring.add("ffn_out", with_last=h > 0) for h in range(2)] for _ in range(2)]
            slots.used(n, out[1][1])
            return out

        def down_units(n):
            out = [[ring.add("ffn_out", with_last=h > 0) for h in range(2)] for _ in range(KT)]
            slots.used(n, out[-1][1])
            return out

        L["ffn_in"] = [slots.load() for _ in range(2)]
        L["g0"] = pair_units(L["ffn_in"][0])
        L["ss2"] = ring.add("sumsq_out")
        L["rb"] = [ring.add("rb_out") for _ in range(2)]
        ring.skip()
        L["u0f"] = pair_units(L["ffn_in"][1])
        first = len(ring.units)
        L["body_slots"] = n = [slots.load() for _ in range(6)]
        L["body"] = [(pair_units(n[3 * s]), down_units(n[3 * s + 1]), pair_units(n[3 * s + 2]))
                     for s in range(2)]
        size, per = L["body_size"], L["body_per"] = ring.repeat(first, BODIES)
        for j in range(6 * (BODIES - 1)):
            m = slots.load()
            slots.used(m, ring.units[slots.last[m - 6].n + size])
        L["last_u"] = [ring.units[u[0].n + size * (BODIES - 1)] for u in L["body"][1][2]]
        L["last_slot"] = slots.load()
        L["last"] = down_units(L["last_slot"])
        plan.append(L)
    y = [[ring.add("y_dve"), ring.add("y_act")] for _ in range(NT)]
    return ring, slots, gains, xt, plan, y


def trunk(nc, a, out):
    ring, slots, gains_unit, xt_units, plan, y_units = build_plan()
    sems = ExitStack()
    with sems:
        place_at = {}

        def place(name, shape, dtype, at):
            size = 4 * int(np.prod(shape[1:]))
            place_at[name] = (at, at + size)
            assert at % 32 == 0 and at + size <= nc.sbuf_top, (name, at, size)
            return nc.alloc_sbuf_tensor_at(name, shape, dtype, offset=at)

        at = -(-nc.sbuf_base // 32) * 32
        xT = place("xT", [P, KT, TOK], F32, at)
        at += 4 * KT * TOK
        r0 = at
        hs_hi = place("hs_hi", [P, KT, TOK], F32R, at)
        at += 4 * KT * TOK
        hs_lo = place("hs_lo", [P, KT, TOK], F32R, at)
        at += 4 * KT * TOK
        act_hi = place("act_hi", [P, 2, TOK], F32R, at)
        at += 8 * TOK
        act_lo = place("act_lo", [P, 2, TOK], F32R, at)
        at += 8 * TOK
        gate = place("gate", [P, 2, TOK], F32, at)
        at += 8 * TOK
        hid = place("hid", [P, 2, TOK], F32, at)
        at += 8 * TOK
        kT_s = place("kT_s", [QK, HEADS, S_KEYS], F32, r0)
        v_s = place("v_s", [P, CACHE_TILES + 1, WIDTH], F32, r0 + 4 * HEADS * S_KEYS)
        qT_s = place("qT_s", [QK, HEADS, DEC], F32, at - 4 * HEADS * DEC)
        assert r0 + 4 * HEADS * S_KEYS + 4 * (CACHE_TILES + 1) * WIDTH <= at - 4 * HEADS * DEC
        kT_p = place("kT_p", [QK, HEADS, SEQ], F32, r0)
        v_p = place("v_p", [P, PT_, WIDTH], F32, r0 + 4 * HEADS * SEQ)
        qT_p = place("qT_p", [QK, HEADS, SEQ], F32, r0 + 4 * HEADS * SEQ + 4 * PT_ * WIDTH)
        raw = place("raw", [P, 2, BLOCK], F32, at)
        at += 8 * BLOCK
        w_hi = place("w_hi", [P, 2, BLOCK], F32R, at)
        at += 8 * BLOCK
        w_lo = place("w_lo", [P, 2, BLOCK], F32R, at)
        at += 8 * BLOCK
        qlatT = place("qlatT", [P, 2, TOK], F32, at)
        sumsq = place("sumsq", [P, TOK], F32, at)
        rb = place("rb", [P, TOK], F32, at + 4 * TOK)
        at += 8 * TOK
        ug = place("ug", [P, NT, WIDTH], F32, at)
        x_tm = place("x_tm", [P, NT, D_MODEL], F32, at)
        at += 4 * NT * WIDTH
        gv = place("gv", [P, NT, WIDTH], F32, at)
        o_tm = place("o_tm", [P, PT_ * WIDTH + HEAD_PAIRS * VDIM], F32, at)
        o_s = o_tm[:, PT_ * WIDTH:].rearrange("p (m d) -> p m d", d=VDIM)
        at += 4 * NT * WIDTH
        ckv_n = place("ckv_n", [P, NT, KV_LORA], F32, at)
        at += 4 * NT * KV_LORA
        kr_n = place("kr_n", [P, NT, ROPE], F32, at)
        at += 4 * NT * ROPE
        ckvT = place("ckvT", [P, ALL_KEYS], F32, at)
        at += 4 * ALL_KEYS
        wsT = place("wsT", [P, GROUPS, P], F32, at)
        at += 4 * GROUPS * P
        wsT_s = place("wsT_s", [P, GROUPS, DEC], F32, at)
        at += 4 * GROUPS * DEC
        tm = place("tm", [P, 2, 2, HEADS, QK], F32, at)
        wide = place("wide", [P, 5 * WIDTH], F32, at)
        wide_o = place("wide_o", [P, PT_ * WIDTH + HEAD_PAIRS * VDIM], F32, at)
        at += 16 * HEADS * QK
        sq = place("sq", [P, 2, HEADS, QK], F32, at)
        at += 8 * HEADS * QK
        p_sb = place("p_sb", [P, 2, S_KEYS], F32, at)
        wide_g = place("wide_g", [P, NT * WIDTH], F32, at)
        ws_in = place("ws_in", [P, GROUPS, P], F32, at)
        cache_in = place("cache_in", [P, CACHE_TILES, KV_LORA], F32, at + 4 * GROUPS * P)
        at += 8 * S_KEYS
        pT = place("pT", [P, 2, CACHE_TILES + 1, P], F32, at)
        kvz = place("kvz", [P, NT, KV_KR], F32, at)
        kvsq = place("kvsq", [P, NT, KV_KR], F32, at + 4 * NT * KV_KR)
        ms_sb = place("ms_sb", [P, KT, DEC], F32, at)
        at += 8 * (CACHE_TILES + 1) * P
        cache_kr = place("cache_kr", [P, CACHE_TILES, ROPE], F32, at)
        at += 4 * CACHE_TILES * ROPE
        ln_gb = place("ln_gb", [P, 2, WIDTH], F32, at)
        at += 8 * WIDTH
        g_tm = place("g_tm", [P, KV_LORA + 2 * ROPE], F32, at)
        at += 4 * (KV_LORA + 2 * ROPE)
        trig = place("trig", [P, NT, ROPE], F32, at)
        at += 4 * NT * ROPE
        gT = place("gT", [P, G_ROWS], F32, at)
        at += 4 * G_ROWS
        gq = place("gq", [P, 8], F32, at)
        at += 32
        ident = place("ident", [P, P], F32, at)
        g_in = place("g_in", [P, P], F32, at + 512)
        at += 1024
        ones = place("ones", [P, 8], F32, at)
        at += 32
        mhalf = place("mhalf", [P, 64], F32, at)
        at += 256
        ms = place("ms", [P, 64], F32, at)
        at += 256
        rs = place("rs", [P, 64], F32, at)
        at += 256
        mu = place("mu", [P, 64], F32, at)
        at += 256
        r_tok = place("r_tok", [P, 8], F32, at)
        at += 32
        r_q = place("r_q", [P, 8], F32, at)
        at += 32
        mx = place("mx", [P, 8], F32, at)
        at += 32
        nm = place("nm", [P, 2, 8], F32, at)
        at += 64
        lsum = place("lsum", [P, 4, 8], F32, at)
        at += 128
        linv = place("linv", [P, 2, 8], F32, at)
        at += 64

        ps = sems.enter_context(nc.psum_tensor("ps", [P, 8, 512], F32))

        S = {}

        def sem(name):
            S[name] = sems.enter_context(nc.semaphore(name))
            return S[name]

        full = sem("full")
        for name in ring.values:
            sem(name)
        g_zeroed, ident_ready, const_ready = sem("g_zeroed"), sem("ident_ready"), sem("const_ready")
        gains_loaded, trig_loaded = sem("gains_loaded"), sem("trig_loaded")
        x_loaded = [sem(f"x_loaded{t}") for t in range(NT)]
        raw_loaded = [sem(f"raw_loaded{s}") for s in range(2)]
        layer_loaded = sem("layer_loaded")
        hi_split, lo_split = sem("hi_split"), sem("lo_split")
        gq_ready = sem("gq_ready")
        hs_hi_done, hs_lo_done = sem("hs_hi_done"), sem("hs_lo_done")
        squared, summed = sem("squared"), sem("summed")
        ms_ready, rs_ready = sem("ms_ready"), sem("rs_ready")
        r_ready, rq_ready = sem("r_ready"), sem("rq_ready")
        ckv_normed, kr_turned = sem("ckv_normed"), sem("kr_turned")
        v_centred, v_squared, v_scaled, vn_done = (sem("v_centred"), sem("v_squared"), sem("v_scaled"),
                                                   sem("vn_done"))
        sq_free, q_normed, kr_spread = sem("sq_free"), sem("q_normed"), sem("kr_spread")
        nm_ready, wsT_masked = sem("nm_ready"), sem("wsT_masked")
        gm_squared, gm_normed = sem("gm_squared"), sem("gm_normed")
        o_squared, o_normed = sem("o_squared"), sem("o_normed")
        m_hi, m_lo = sem("m_hi"), sem("m_lo")
        silu_done, gate_done = sem("silu_done"), sem("gate_done")
        act_hi_done, act_lo_done = sem("act_hi_done"), sem("act_lo_done")
        dve_chain, pool_chain = sem("dve_chain"), sem("pool_chain")
        rows_stored, v_stored, y_stored = sem("rows_stored"), sem("v_stored"), sem("y_stored")

        def bank(u, rows=slice(0, P), cols=512):
            return ps[rows, u.bank, 0:cols]

        def halves(t):
            return t.rearrange("p (h c) -> p h c", h=2)

        def in_cols(l, c0, c1):
            return a["w_in"][l][:, c0:c1].rearrange("(k p) n -> p k n", p=P)

        w_in_cols = [(Q_LORA, Q_LORA + KV_KR), (0, Q_LORA)]
        for c in (Q_LORA + KV_KR + WIDTH, Q_LORA + KV_KR):
            w_in_cols += [(c, c + COLS), (c + COLS, c + 2 * COLS)]

        raw_of = [n for n, k in enumerate(slots.raw) if k is not None]

        def emptied(eng, u):
            eng.wait_ge(S[u.freed[0]], u.freed[1])

        def filled(eng, u):
            eng.wait_ge(full, u.done)

        block = sems.enter_context(nc.Block())

        @block.sync
        def _(sp):
            def load(n, dst, src):
                if n >= 2:
                    k = slots.raw[n - 2]
                    if k is None:
                        filled(sp, slots.last[n - 2])
                    else:
                        sp.wait_ge(lo_split, k + 1)
                sp.dma_start(dst, src).then_inc(raw_loaded[n % 2], 16)

            def by_k(n, cols):
                return raw[:, n % 2, 0:KT * cols].rearrange("p (k n) -> p k n", k=KT)

            def by_f(n):
                return raw[:, n % 2, :].rearrange("p (f n) -> p f n", f=2)

            def small(l):
                if l:
                    sp.wait_ge(m_lo, l)
                loads = [(ws_in[:, :, :], a["gm_w_s"][l].rearrange("g i j -> i g j")),
                         (cache_in[:, :, :], a["cache_ckv"][l, 0].rearrange("(j p) c -> p j c", p=P)),
                         (cache_kr[:, :, :], a["cache_krope"][l, 0].rearrange("(j p) c -> p j c", p=P)),
                         (ln_gb[:, 0, :], a["gm_ln_g"][l].rearrange("g d -> (g d)").partition_broadcast(P)),
                         (ln_gb[:, 1, :], a["gm_ln_b"][l].rearrange("g d -> (g d)").partition_broadcast(P))]
                c = 0
                for name, n in (("g_kv_lora", KV_LORA), ("g_kr", ROPE), ("g_qr", ROPE)):
                    loads.append((g_tm[:, c:c + n], a[name][l].partition_broadcast(P)))
                    c += n
                assert len(loads) == SMALL
                for dst, src in loads:
                    sp.dma_start(dst, src).then_inc(layer_loaded, 16)

            for t, c in enumerate(TILE_AT[:PT_]):
                sp.dma_start(x_tm[:, t, :], a["x_prompt"][0, c:c + P, :]).then_inc(x_loaded[t], 16)
            sp.dma_start(x_tm[DEC:P, PT_, :], a["x_sample"][0]).then_inc(x_loaded[PT_], 16)
            for l, L in enumerate(plan):
                for n, (c0, c1) in zip(L["w_in"], w_in_cols):
                    load(n, by_k(n, c1 - c0), in_cols(l, c0, c1))
                    if l == 0 and n == L["w_in"][1]:
                        small(0)
                n = L["wq"]
                load(n, raw[:, n % 2, 0:2 * HEADS * QK].rearrange("p (m n) -> p m n", m=2),
                     a["w_q_up"][l].rearrange("(m p) n -> p m n", p=P))
                n = L["wkv"]
                load(n, raw[:, n % 2, 0:2 * WIDTH], a["w_kv_up"][l])
                for j, n in enumerate(L["w_o"]):
                    load(n, by_k(n, COLS), a["w_o"][l][:, j * COLS:(j + 1) * COLS].rearrange("(k p) n -> p k n", p=P))
                gate_src = a["w_gate"][l].rearrange("(k p) (g n) -> g p k n", p=P, n=COLS)
                up_src = a["w_up"][l].rearrange("(k p) (g n) -> g p k n", p=P, n=COLS)
                down_src = a["w_down"][l].rearrange("(g f p) n -> g p f n", p=P, f=2)
                for n, src in zip(L["ffn_in"], (gate_src, up_src)):
                    load(n, by_k(n, COLS), src[0])
                if l + 1 < DEPTH:
                    small(l + 1)
                n0 = L["body_slots"][0]
                with sp.Fori(0, BODIES) as b:
                    for s in range(2):
                        for j, src in enumerate((gate_src, down_src, up_src)):
                            n = n0 + 3 * s + j
                            sp.wait_ge(lo_split, b * 6 + (slots.raw[n - 2] + 1))
                            sp.dma_start(by_f(n) if j == 1 else by_k(n, COLS),
                                         src[b * 2 + (s if j == 1 else s + 1)]).then_inc(raw_loaded[n % 2], 16)
                n = L["last_slot"]
                load(n, by_f(n), down_src[FPAIRS - 1])
            for t in range(NT):
                for u in y_units[t]:
                    emptied(sp, u)
                if t < PT_:
                    sp.dma_start(out["y_prompt"][0, t * P:(t + 1) * P, :], x_tm[:, t, :]).then_inc(y_stored, 16)
                else:
                    sp.dma_start(out["y_sample"][0], x_tm[0:DEC, t, :]).then_inc(y_stored, 16)
            sp.wait_ge(y_stored, 16 * NT)
            sp.wait_ge(rows_stored, 16 * 4 * DEPTH)
            sp.wait_ge(v_stored, 16 * DEPTH)

        @block.gpsimd
        def _(pool):
            chain = [0]

            def link(ins):
                chain[0] += 1
                ins.then_inc(pool_chain, 1)
                pool.wait_ge(pool_chain, chain[0])

            def w_low(n, size=BLOCK):
                k = slots.raw[n]
                pool.wait_ge(hi_split, k + 1)
                pool.tensor_tensor(w_lo[:, k % 2, 0:size], raw[:, n % 2, 0:size],
                                   w_hi[:, k % 2, 0:size].bitcast(F32), ALU.subtract).then_inc(lo_split, 1)

            def root(l, name, n):
                no = root_no(l, name)
                pool.wait_ge(ms_ready, no)
                pool.tensor_tensor(rs[:, 0:n], ms[:, 0:n], mhalf[:, 0:n], ALU.pow).then_inc(rs_ready, 1)

            def sum_squares(m):
                for k in range(KT):
                    n = m * KT + k + 1
                    pool.wait_ge(squared, n)
                    if k:
                        pool.wait_ge(summed, n - 1)
                        ins = pool.tensor_tensor(sumsq[:, :], sumsq[:, :], gate[:, k % 2, :], ALU.add)
                    else:
                        ins = pool.tensor_copy(sumsq[:, :], gate[:, 0, :])
                    ins.then_inc(summed, 1)

            pool.memset(g_in[:, :], 0.0).then_inc(g_zeroed, 1)
            link(pool.memset(ident[:, :], 0.0))
            pool.affine_select(out=ident[:, :], in_=ident[:, :], compare_op=ALU.not_equal, fill=1.0, base=0,
                               pattern=[[-1, P]], channel_multiplier=1).then_inc(ident_ready, 1)
            pool.memset(ones[:, :], 1.0)
            pool.memset(ms[:, :], 1.0)
            pool.memset(mhalf[:, :], -0.5)
            pool.memset(gq[:, :], 1.0).then_inc(const_ready, 1)
            pool.wait_ge(const_ready, 1)
            for l, L in enumerate(plan):
                w_low(L["w_in"][0], KT * KV_KR)
                sum_squares(2 * l)
                w_low(L["w_in"][1])
                root(l, "r1", NT)
                w_low(L["w_in"][2])
                root(l, "kv", 2 * NT)
                pool.wait_ge(ckv_normed, l + 1)
                if l == 0:
                    pool.wait_ge(trig_loaded, 16 * NT)
                h = ROPE // 2
                x1, x2 = kvz[:, :, KV_LORA:KV_LORA + h], kvz[:, :, KV_LORA + h:KV_KR]
                c, s = trig[:, :, 0:h], trig[:, :, h:ROPE]
                t1, t2 = kvsq[:, :, 0:h], kvsq[:, :, h:2 * h]
                link(pool.tensor_tensor(t1, x1, c, ALU.mult))
                link(pool.tensor_tensor(t2, x2, s, ALU.mult))
                link(pool.tensor_tensor(kr_n[:, :, 0:h], t1, t2, ALU.subtract))
                link(pool.tensor_tensor(t1, x1, s, ALU.mult))
                link(pool.tensor_tensor(t2, x2, c, ALU.mult))
                pool.tensor_tensor(kr_n[:, :, h:ROPE], t1, t2, ALU.add).then_inc(kr_turned, 1)
                w_low(L["w_in"][3])
                root(l, "q", NT)
                w_low(L["w_in"][4])
                w_low(L["w_in"][5])
                root(l, "ln", NT * GROUPS)
                pool.wait_ge(v_scaled, l + 1)
                pool.wait_ge(layer_loaded, 16 * SMALL * (l + 1))
                link(pool.tensor_tensor(gv[:, :, :], gv[:, :, :], ln_gb[:, 0:1, :].to_broadcast([P, NT, WIDTH]),
                                        ALU.mult))
                pool.tensor_tensor(gv[:, :, :], gv[:, :, :], ln_gb[:, 1:2, :].to_broadcast([P, NT, WIDTH]), ALU.add
                                   ).then_inc(vn_done, 1)

                def batch(b):
                    nt, seq = len(b["tiles"]), b["seq"]
                    if b["what"] == "q":
                        root(l, f"b{seq}", nt * HEADS * 2)
                        return
                    for jj, j in enumerate(b["tiles"]):
                        if j == CACHE_TILES:
                            continue
                        if jj == 0 and seq >= 2:
                            filled(pool, L["batches"][seq - 2]["turn"][-1][1])
                        src = cache_kr[:, j, :] if j < CACHE_TILES else kr_n[:, j - CACHE_TILES - 1, :]
                        pool.tensor_copy(tm[:, seq % 2, jj, :, NOPE:QK],
                                         src.unsqueeze(1).to_broadcast([P, HEADS, ROPE])).then_inc(kr_spread, 1)
                    root(l, f"b{seq}", nt * HEADS)

                for b in L["s_batches"]:
                    batch(b)
                root(l, "gm", NT * GROUPS)
                for b in L["p_batches"]:
                    batch(b)
                w_low(L["w_o"][0])
                w_low(L["w_o"][1])
                root(l, "o", O_GROUPS)
                w_low(L["w_o"][2])
                w_low(L["w_o"][3])
                w_low(L["ffn_in"][0])
                sum_squares(2 * l + 1)
                root(l, "r2", NT)
                w_low(L["ffn_in"][1])

                def scale_gate(no, f):
                    pool.wait_ge(silu_done, no)
                    pool.tensor_tensor(gate[:, f, :], gate[:, f, :], rb[:, :], ALU.mult).then_inc(gate_done, 1)

                pairs = 2 * FPAIRS * l
                for f in range(2):
                    scale_gate(pairs + f + 1, f)
                n0 = L["body_slots"][0]
                with pool.Fori(0, BODIES) as i:
                    for s in range(2):
                        for j in range(3):
                            n = n0 + 3 * s + j
                            k = slots.raw[n]
                            pool.wait_ge(hi_split, i * 6 + (k + 1))
                            pool.tensor_tensor(w_lo[:, k % 2, :], raw[:, n % 2, :], w_hi[:, k % 2, :].bitcast(F32),
                                               ALU.subtract).then_inc(lo_split, 1)
                            if j == 1:
                                for f in range(2):
                                    scale_gate(i * 4 + (pairs + 3 + 2 * s + f), f)
                w_low(L["last_slot"])

        @block.scalar
        def _(act):
            def w_high(n, size=BLOCK):
                k = slots.raw[n]
                act.wait_ge(raw_loaded[n % 2], 16 * (n // 2 + 1))
                if k >= 2:
                    filled(act, slots.last[raw_of[k - 2]])
                act.activation(w_hi[:, k % 2, 0:size], raw[:, n % 2, 0:size], ACT.Copy).then_inc(hi_split, 1)

            act.wait_ge(g_zeroed, 1)
            loads = [(row, slice(0, P), a[name].rearrange("l (k p) -> (l k) p", p=P))
                     for row, name in ((G_MIX, "g_mix"), (G_FFN, "g_ffn"), (G_QL, "g_q_lora"))]
            loads.append((G_BS, slice(0, P), a["gm_b_s"].rearrange("l g i -> (l g) i")))
            loads.append((G_BS_S, slice(DEC, P), a["gm_b_s"][:, :, 0:DEC].rearrange("l g i -> (l g) i")))
            for l in range(DEPTH):
                for j, name in enumerate(("g_out_att", "g_out_gm")):
                    loads.append((G_OUT + 8 * l + 4 * j, slice(0, P), a[name][l].rearrange("(k e) d -> k (e d)", e=2)))
            loads += [(G_QN, slice(0, NOPE), a["g_qn"]), (G_KN, slice(0, NOPE), a["g_kn"])]
            assert len(loads) == GAIN_LOADS
            for row, cols, src in loads:
                act.dma_start(g_in[row:row + src.shape[0], cols], src).then_inc(gains_loaded, 16)
            for t, c in enumerate(TILE_AT):
                act.dma_start(trig[:, t, :], a["trig"][c:c + P, :]).then_inc(trig_loaded, 16)
            for t in range(NT):
                u = xt_units[t][1]
                filled(act, u)
                w = P if t < PT_ else DEC
                act.activation(xT[:, 4:8, t * P:t * P + w], bank(u).rearrange("p (k c) -> p k c", k=4)[:, :, 0:w],
                               ACT.Copy).then_inc(S["x_turned_act"], 1)

            def split_high(l, gcol, ready):
                for k in range(KT):
                    ready(k)
                    act.activation(hs_hi[:, k, :], xT[:, k, :], ACT.Copy,
                                   scale=gT[:, gcol + k:gcol + k + 1]).then_inc(hs_hi_done, 1)

            def squares(m):
                for k in range(KT):
                    if k >= 2:
                        act.wait_ge(summed, m * KT + k - 1)
                    act.activation(gate[:, k % 2, :], xT[:, k, :], ACT.Square).then_inc(squared, 1)

            for l, L in enumerate(plan):
                w_high(L["w_in"][0], KT * KV_KR)
                if l == 0:
                    emptied(act, gains_unit)
                    emptied(act, xt_units[-1][0])
                    emptied(act, xt_units[-1][1])
                    split_high(l, G_MIX, lambda k: None)
                else:
                    last = plan[l - 1]["last"]
                    split_high(l, G_MIX + KT * l, lambda k: emptied(act, last[k][0]))
                w_high(L["w_in"][1])
                squares(2 * l)
                w_high(L["w_in"][2])
                act.wait_ge(summed, (2 * l + 1) * KT)
                for m in range(2):
                    for h in range(2):
                        u = L["q"][m][h]
                        filled(act, u)
                        cols = slice(h * HALF, (h + 1) * HALF)
                        act.activation(gate[:, m, cols], bank(u, cols=HALF), ACT.Square)
                        act.activation(qlatT[:, m, cols], bank(u, cols=HALF), ACT.Copy,
                                       scale=gT[:, G_QL + 2 * l + m:G_QL + 2 * l + m + 1]).then_inc(S["qlat_out"], 1)
                w_high(L["w_in"][3])
                act.wait_ge(r_ready, 2 * l + 1)
                for j, (name, dst) in enumerate((("v0", gv), ("v1", gv), ("u0", ug), ("u1", ug))):
                    for t in range(NT):
                        u = L[name][t]
                        filled(act, u)
                        act.activation(dst[:, t, (j % 2) * COLS:(j % 2 + 1) * COLS], bank(u, cols=COLS),
                                       ACT.Gelu_apprx_tanh, scale=r_tok[:, t:t + 1]).then_inc(S["gelu_out"], 1)
                    if j < 2:
                        w_high(L["w_in"][4 + j])
                act.wait_ge(v_centred, l + 1)
                act.activation(wide[:, :], gv[:, :, :].rearrange("p t c -> p (t c)"), ACT.Square).then_inc(v_squared, 1)
                filled(act, L["ct"][1])
                act.activation(ckvT[:, PAST:S_KEYS], ps[:, L["ct"][1].bank, DEC:P], ACT.Copy).then_inc(S["ckvt_act"], 1)
                filled(act, L["ct"][3])
                act.activation(ckvT[:, PAST // 2:PAST], bank(L["ct"][3]), ACT.Copy).then_inc(S["ckvt_act"], 1)
                act.wait_ge(ckv_normed, l + 1)
                act.dma_start(out["ckv_prompt"][l, 0].rearrange("(t p) c -> p t c", p=P), ckv_n[:, 0:PT_, :]
                              ).then_inc(rows_stored, 16)
                act.dma_start(out["ckv_sample"][l, 0], ckv_n[DEC:P, PT_, :]).then_inc(rows_stored, 16)
                act.wait_ge(kr_turned, l + 1)
                act.dma_start(out["krope_prompt"][l, 0].rearrange("(t p) c -> p t c", p=P), kr_n[:, 0:PT_, :]
                              ).then_inc(rows_stored, 16)
                act.dma_start(out["krope_sample"][l, 0], kr_n[DEC:P, PT_, :]).then_inc(rows_stored, 16)

                def batch_first(b):
                    seq = b["seq"]
                    if seq or l:
                        act.wait_ge(sq_free, NB * l + seq)
                    for jj, j in enumerate(b["tiles"]):
                        if b["what"] == "q":
                            if not jj:
                                act.wait_ge(rq_ready, l + 1)
                                act.wait_ge(v_squared, l + 1)
                                if seq >= 2:
                                    filled(act, L["batches"][seq - 2]["turn"][-1][1])
                                else:
                                    act.wait_ge(v_scaled, l + 1)
                            for e, u in enumerate(b["up"][jj]):
                                filled(act, u)
                                src = bank(u, cols=4 * QK).rearrange("p (h c) -> p h c", c=QK)
                                act.activation(sq[:, jj, 4 * e:4 * e + 4, :], src, ACT.Square, scale=r_q[:, j:j + 1])
                                act.activation(tm[:, seq % 2, jj, 4 * e:4 * e + 4, :], src, ACT.Copy,
                                               scale=r_q[:, j:j + 1]).then_inc(S["qz_out"], 1)
                        else:
                            uk, uv = b["up"][jj]
                            rows = slice(0, key_tile(j)[1])
                            filled(act, uk)
                            act.activation(sq[rows, jj, :, 0:NOPE], bank(uk, rows).rearrange("p (h c) -> p h c", c=NOPE),
                                           ACT.Square)
                            filled(act, uv)
                            dst = v_s[rows, j, :] if j <= CACHE_TILES else v_p[:, j - CACHE_TILES - 1, :]
                            act.activation(dst, bank(uv, rows), ACT.Copy).then_inc(S["v_out"], 1)

                def batch_turned(b):
                    for jj, j in enumerate(b["tiles"]):
                        u = b["turn"][jj][1]
                        filled(act, u)
                        src = ps[0:QK, u.bank, :].rearrange("p (h c) -> p h c", h=4)
                        if b["what"] == "q":
                            act.wait_ge(gq_ready, 2)
                            scale = gq[0:QK, l:l + 1]
                            if j == PT_:
                                dst, src = qT_s[:, 4:8, :], src[:, :, DEC:P]
                            else:
                                dst = qT_p[:, 4:8, j * P:(j + 1) * P]
                        else:
                            scale = 1.0
                            c, w = key_tile(j)
                            src = src[:, :, 0:w]
                            dst = kT_s[:, 4:8, c:c + w] if j <= CACHE_TILES else kT_p[:, 4:8, c - S_KEYS:c - S_KEYS + w]
                        act.activation(dst, src, ACT.Copy, scale=scale).then_inc(S["qkt_act"], 1)

                def batches_run(todo):
                    for n, b in enumerate(todo):
                        batch_first(b)
                        if n:
                            batch_turned(todo[n - 1])
                    batch_turned(todo[-1])

                batches_run(L["s_batches"])
                act.wait_ge(vn_done, l + 1)
                act.dma_start(out["gmlp_v_sample"][l, 0], gv[DEC:P, PT_, :]).then_inc(v_stored, 16)

                def sample_pt(n):
                    u = L["s_steps"][n]["t"][1]
                    filled(act, u)
                    if n >= 2:
                        filled(act, L["s_steps"][n - 2]["o"])
                    act.activation(pT[:, n % 2, 4:8, :], bank(u).rearrange("p (j c) -> p j c", j=4),
                                   ACT.Copy).then_inc(S["pt_act"], 1)

                for n, st in enumerate(L["s_steps"]):
                    act.wait_ge(nm_ready, STEPS * l + n + 1)
                    if n >= 2:
                        filled(act, L["s_steps"][n - 2]["t"][-1])
                    for e, ((c, w), u) in enumerate(zip(S_SPANS, st["s"])):
                        act.activation(p_sb[:, n % 2, c:c + w], bank(u, cols=w), ACT.Exp, bias=nm[:, n % 2, 0:1],
                                       scale=SCALE, accum_out=lsum[:, n % 4, e:e + 1]).then_inc(S["s_exp"], 1)
                    if n >= 1:
                        sample_pt(n - 1)
                sample_pt(HEAD_PAIRS - 1)
                emptied(act, L["s_steps"][-1]["o"])
                emptied(act, L["mix"][-1])
                act.activation(wide_g[:, :], ug[:, :, :].rearrange("p t c -> p (t c)"), ACT.Square).then_inc(gm_squared, 1)
                batches_run(L["p_batches"])
                w_high(L["w_o"][0])
                w_high(L["w_o"][1])

                def prompt_pt(m):
                    if m % 2:
                        return
                    i, _, nh = P_STEPS[m]
                    u = L["p_steps"][m]["t"]
                    filled(act, u)
                    if m >= 2:
                        filled(act, L["p_steps"][m - 2]["o"])
                    w = nh * (i + 1)
                    act.activation(pT[:, 0, 0:w, :], bank(u, cols=w * P).rearrange("p (j c) -> p j c", j=w),
                                   ACT.Copy).then_inc(S["pt_act"], 1)

                for m, (i, _, nh) in enumerate(P_STEPS):
                    st = L["p_steps"][m]
                    act.wait_ge(nm_ready, STEPS * l + HEAD_PAIRS + m + 1)
                    if m >= 2:
                        filled(act, L["p_steps"][m - 2]["t"])
                    if m < 2:
                        act.wait_ge(gm_normed, l + 1)
                    w = (i + 1) * P
                    for e in range(nh):
                        ins = act.activation(p_sb[:, m % 2, e * w:(e + 1) * w], ps[:, st["s"].bank, e * w:(e + 1) * w],
                                             ACT.Exp, bias=nm[:, m % 2, e:e + 1], scale=SCALE,
                                             accum_out=lsum[:, m % 4, e:e + 1])
                    ins.then_inc(S["s_exp"], 1)
                    if m >= 1:
                        prompt_pt(m - 1)
                prompt_pt(len(P_STEPS) - 1)
                emptied(act, L["p_steps"][-1]["o"])
                act.activation(wide_o[:, :], o_tm[:, :], ACT.Square).then_inc(o_squared, 1)
                for k in range(KT):
                    u = L["mt"][k]
                    filled(act, u)
                    g = G_OUT + 8 * l + k
                    act.activation(hs_hi[:, k, 0:SEQ], bank(u), ACT.Copy, scale=gT[:, g:g + 1]).then_inc(m_hi, 1)
                emptied(act, L["mt"][KT])
                act.activation(hs_hi[:, :, SEQ:TOK], ms_sb[:, :, :], ACT.Copy).then_inc(m_hi, 1)
                w_high(L["w_o"][2])
                w_high(L["w_o"][3])
                w_high(L["ffn_in"][0])
                filled(act, L["wo"][-1][1])
                split_high(l, G_FFN + KT * l, lambda k: emptied(act, L["wo"][k][0]))
                w_high(L["ffn_in"][1])
                squares(2 * l + 1)

                def silu(f, no):
                    act.wait_ge(S["ffn_out"], no)
                    act.activation(gate[:, f, :], gate[:, f, :], ACT.Silu).then_inc(silu_done, 1)

                def hidden_high(f, no):
                    act.wait_ge(S["ffn_out"], no)
                    act.activation(act_hi[:, f, :], hid[:, f, :], ACT.Copy).then_inc(act_hi_done, 1)

                for f in range(2):
                    silu(f, L["g0"][f][0].freed[1])
                n0 = L["body_slots"][0]
                size, per = L["body_size"], L["body_per"]
                with act.Fori(0, BODIES) as i:
                    def high(n):
                        k = slots.raw[n]
                        act.wait_ge(raw_loaded[n % 2], i * 48 + 16 * (n // 2 + 1))
                        act.wait_ge(full, i * size + (slots.last[raw_of[k - 2] + 6].done - size))
                        act.activation(w_hi[:, k % 2, :], raw[:, n % 2, :], ACT.Copy).then_inc(hi_split, 1)

                    for s in range(2):
                        before = L["u0f"] if s == 0 else L["body"][0][2]
                        high(n0 + 3 * s)
                        for f in range(2):
                            hidden_high(f, i * per + before[f][0].freed[1])
                        high(n0 + 3 * s + 1)
                        for f in range(2):
                            silu(f, i * per + L["body"][s][0][f][0].freed[1])
                        high(n0 + 3 * s + 2)
                for f in range(2):
                    hidden_high(f, L["last_u"][f].freed[1])
                w_high(L["last_slot"])
            for t in range(NT):
                u = y_units[t][1]
                rows = slice(0, P if t < PT_ else DEC)
                filled(act, u)
                act.activation(x_tm[rows, t, WIDTH:2 * WIDTH], bank(u, rows), ACT.Copy).then_inc(S["y_act"], 1)

        @block.vector
        def _(dve):
            chain = [0]

            def link(ins):
                chain[0] += 1
                ins.then_inc(dve_chain, 1)
                dve.wait_ge(dve_chain, chain[0])

            def root(l, name, n, rows, scale, ins_in=None):
                src = ms[rows, 0:n] if ins_in is None else ins_in
                dve.tensor_scalar(ms[rows, 0:n], src, scale, EPS, ALU.mult, ALU.add).then_inc(ms_ready, 1)
                dve.wait_ge(rs_ready, root_no(l, name))

            def low(dst, src, gain, hi):
                return dve.scalar_tensor_tensor(out=dst, in0=src, scalar=gain, in1=hi.bitcast(F32), op0=ALU.mult,
                                                op1=ALU.subtract)

            ALL = slice(0, P)
            filled(dve, gains_unit)
            dve.tensor_copy(gT[:, :], bank(gains_unit, cols=G_ROWS)).then_inc(S["gains_turned"], 1)
            emptied(dve, gains_unit)
            dve.wait_ge(const_ready, 1)
            dve.tensor_tensor(gq[0:NOPE, 0:DEPTH], gT[0:NOPE, G_QN:G_QN + DEPTH], gT[0:NOPE, G_KN:G_KN + DEPTH],
                              ALU.mult).then_inc(gq_ready, 2)
            for t in range(NT):
                u = xt_units[t][0]
                filled(dve, u)
                w = P if t < PT_ else DEC
                dve.tensor_copy(xT[:, 0:4, t * P:t * P + w], bank(u).rearrange("p (k c) -> p k c", k=4)[:, :, 0:w]
                                ).then_inc(S["x_turned_dve"], 1)

            def split_low(m, gcol):
                for k in range(KT):
                    dve.wait_ge(hs_hi_done, m * KT + k + 1)
                    low(hs_lo[:, k, :], xT[:, k, :], gT[:, gcol + k:gcol + k + 1], hs_hi[:, k, :]).then_inc(hs_lo_done, 1)

            def r_by_token(l, name, u, no):
                filled(dve, u)
                dve.tensor_scalar(ms[:, 0:NT], bank(u, cols=NT), 1.0 / D_MODEL, EPS, ALU.mult, ALU.add
                                  ).then_inc(S["sumsq_out"], 1)
                emptied(dve, u)
                dve.tensor_copy(ms[:, 0:NT], ms[:, 0:NT]).then_inc(ms_ready, 1)
                dve.wait_ge(rs_ready, root_no(l, name))
                dve.tensor_copy(r_tok[:, 0:NT], rs[:, 0:NT]).then_inc(r_ready, 1)
                dve.wait_ge(r_ready, no)

            for l, L in enumerate(plan):
                split_low(2 * l, G_MIX + KT * l)
                r_by_token(l, "r1", L["ss1"], 2 * l + 1)
                for t in range(NT):
                    u = L["kv"][t]
                    filled(dve, u)
                    dve.tensor_scalar(kvz[:, t, :], bank(u, cols=KV_KR), r_tok[:, t:t + 1], None, ALU.mult
                                      ).then_inc(S["kv_out"], 1)
                emptied(dve, L["kv"][-1])
                link(dve.tensor_tensor(kvsq[:, :, :], kvz[:, :, :], kvz[:, :, :], ALU.mult))
                dve.tensor_reduce(ms[:, 0:NT], kvsq[:, :, 0:KV_LORA], AX.X, ALU.add)
                link(dve.tensor_reduce(ms[:, NT:2 * NT], kvsq[:, :, KV_LORA:KV_KR], AX.X, ALU.add))
                link(dve.tensor_scalar(ms[:, 0:NT], ms[:, 0:NT], ROPE / KV_LORA, None, ALU.mult))
                root(l, "kv", 2 * NT, ALL, 1.0 / ROPE)
                link(dve.tensor_tensor(kvz[:, :, 0:KV_LORA], kvz[:, :, 0:KV_LORA],
                                       rs[:, 0:NT].unsqueeze(2).to_broadcast([P, NT, KV_LORA]), ALU.mult))
                link(dve.tensor_tensor(kvz[:, :, KV_LORA:KV_KR], kvz[:, :, KV_LORA:KV_KR],
                                       rs[:, NT:2 * NT].unsqueeze(2).to_broadcast([P, NT, ROPE]), ALU.mult))
                dve.wait_ge(layer_loaded, 16 * SMALL * (l + 1))
                if l:
                    dve.wait_ge(rows_stored, 64 * l)
                dve.tensor_tensor(ckv_n[:, :, :], kvz[:, :, 0:KV_LORA],
                                  g_tm[:, 0:KV_LORA].unsqueeze(1).to_broadcast([P, NT, KV_LORA]), ALU.mult)
                dve.tensor_tensor(kvz[:, :, KV_LORA:KV_KR], kvz[:, :, KV_LORA:KV_KR],
                                  g_tm[:, KV_LORA:KV_KR].unsqueeze(1).to_broadcast([P, NT, ROPE]), ALU.mult
                                  ).then_inc(ckv_normed, 1)
                link(dve.tensor_tensor(r_q[:, 0:NT], r_tok[:, 0:NT], r_tok[:, 0:NT], ALU.mult))
                filled(dve, L["ssq"])
                dve.tensor_tensor(ms[:, 0:NT], bank(L["ssq"], cols=NT), r_q[:, 0:NT], ALU.mult).then_inc(S["sumsq_out"], 1)
                emptied(dve, L["ssq"])
                root(l, "q", NT, ALL, 1.0 / Q_LORA)
                dve.tensor_tensor(r_q[:, 0:NT], r_tok[:, 0:NT], rs[:, 0:NT], ALU.mult).then_inc(rq_ready, 1)
                emptied(dve, L["v1"][-1])
                gvg = gv[:, :, :].rearrange("p t (g d) -> p (t g) d", d=GDIM)
                n = NT * GROUPS
                link(dve.tensor_reduce(mu[:, 0:n], gvg, AX.X, ALU.add))
                link(dve.tensor_scalar(mu[:, 0:n], mu[:, 0:n], 1.0 / GDIM, None, ALU.mult))
                dve.tensor_tensor(gvg, gvg, mu[:, 0:n].unsqueeze(2).to_broadcast([P, n, GDIM]), ALU.subtract
                                  ).then_inc(v_centred, 1)
                dve.wait_ge(v_squared, l + 1)
                link(dve.tensor_reduce(ms[:, 0:n], wide[:, :].rearrange("p (n d) -> p n d", d=GDIM), AX.X, ALU.add))
                root(l, "ln", n, ALL, 1.0 / GDIM)
                dve.tensor_tensor(gvg, gvg, rs[:, 0:n].unsqueeze(2).to_broadcast([P, n, GDIM]), ALU.mult
                                  ).then_inc(v_scaled, 1)
                filled(dve, L["ct"][0])
                dve.tensor_copy(ckvT[:, S_KEYS:ALL_KEYS], bank(L["ct"][0])).then_inc(S["ckvt_dve"], 1)
                filled(dve, L["ct"][2])
                dve.tensor_copy(ckvT[:, 0:PAST // 2], bank(L["ct"][2])).then_inc(S["ckvt_dve"], 1)
                for j in range(2):
                    filled(dve, L["wst"][j])
                    dve.tensor_copy(wsT[:, 4 * j:4 * j + 4, :], bank(L["wst"][j]).rearrange("p (g i) -> p g i", g=4)
                                    ).then_inc(S["wst_out"], 1)
                filled(dve, L["wst"][2])
                dve.tensor_copy(wsT_s[DEC:P, :, :], bank(L["wst"][2], slice(DEC, P)).rearrange("p (g i) -> p g i", g=GROUPS)
                                ).then_inc(S["wst_out"], 1)
                emptied(dve, L["wst"][1])
                dve.memset(wsT[CHUNK:P, :, 0:CHUNK], 0.0).then_inc(wsT_masked, 1)

                def batch_first(b):
                    seq, tiles = b["seq"], b["tiles"]
                    nt = len(tiles)
                    n = nt * HEADS
                    if b["what"] == "q":
                        emptied(dve, b["up"][-1][1])
                        sqv = sq[:, 0:nt, :, :].rearrange("p t h c -> p (t h) c")
                        x = tm[:, seq % 2, 0:nt, :, :].rearrange("p t h c -> p (t h) c")
                        dve.tensor_reduce(ms[:, n:2 * n], sqv[:, :, NOPE:QK], AX.X, ALU.add)
                        link(dve.tensor_reduce(ms[:, 0:n], sqv[:, :, 0:NOPE], AX.X, ALU.add))
                        link(dve.tensor_scalar(ms[:, 0:n], ms[:, 0:n], ROPE / NOPE, None, ALU.mult))
                        root(l, f"b{seq}", 2 * n, ALL, 1.0 / ROPE)
                        dve.tensor_tensor(x[:, :, 0:NOPE], x[:, :, 0:NOPE],
                                          rs[:, 0:n].unsqueeze(2).to_broadcast([P, n, NOPE]), ALU.mult)
                        xr = x[:, :, NOPE:QK]
                        link(dve.tensor_tensor(xr, xr, rs[:, n:2 * n].unsqueeze(2).to_broadcast([P, n, ROPE]), ALU.mult))
                        link(dve.tensor_tensor(xr, xr, g_tm[:, KV_KR:KV_KR + ROPE].unsqueeze(1).to_broadcast([P, n, ROPE]),
                                               ALU.mult))
                        h = ROPE // 2
                        for jj, j in enumerate(tiles):
                            x1, x2 = (tm[:, seq % 2, jj, :, NOPE + e * h:NOPE + (e + 1) * h] for e in range(2))
                            c, s = (trig[:, j:j + 1, e * h:(e + 1) * h].to_broadcast([P, HEADS, h]) for e in range(2))
                            t1, t2, t3, t4 = (sq[:, jj, :, e * h:(e + 1) * h] for e in range(4))
                            dve.tensor_tensor(t1, x1, c, ALU.mult)
                            dve.tensor_tensor(t2, x2, s, ALU.mult)
                            dve.tensor_tensor(t3, x1, s, ALU.mult)
                            link(dve.tensor_tensor(t4, x2, c, ALU.mult))
                            dve.tensor_tensor(x1, t1, t2, ALU.subtract)
                            ins = dve.tensor_tensor(x2, t3, t4, ALU.add)
                            if jj < nt - 1:
                                link(ins)
                        ins.then_inc(sq_free, 1)
                        return
                    rows = slice(0, key_tile(tiles[0])[1])
                    emptied(dve, b["up"][-1][1])
                    sqv = sq[rows, 0:nt, :, :].rearrange("p t h c -> p (t h) c")
                    dve.tensor_reduce(ms[rows, 0:n], sqv[:, :, 0:NOPE], AX.X, ALU.add).then_inc(sq_free, 1)
                    dve.wait_ge(sq_free, NB * l + seq + 1)
                    if seq >= 2:
                        filled(dve, L["batches"][seq - 2]["turn"][-1][1])
                    if tiles[0] == CACHE_TILES:
                        dve.wait_ge(kr_turned, l + 1)
                        dve.tensor_copy(tm[rows, seq % 2, 0, :, NOPE:QK],
                                        kr_n[DEC:P, PT_:PT_ + 1, :].to_broadcast([DEC, HEADS, ROPE]))
                    root(l, f"b{seq}", n, rows, 1.0 / NOPE)
                    for jj, j in enumerate(tiles):
                        u = b["up"][jj][0]
                        dve.tensor_tensor(tm[rows, seq % 2, jj, :, 0:NOPE], bank(u, rows).rearrange("p (h c) -> p h c", c=NOPE),
                                          rs[rows, jj * HEADS:(jj + 1) * HEADS].unsqueeze(2).to_broadcast([rows.stop, HEADS, NOPE]),
                                          ALU.mult).then_inc(S["k_scaled"], 1)

                def batch_turned(b):
                    for jj, j in enumerate(b["tiles"]):
                        u = b["turn"][jj][0]
                        filled(dve, u)
                        src = ps[0:QK, u.bank, :].rearrange("p (h c) -> p h c", h=4)
                        if b["what"] == "q":
                            if j == PT_:
                                dst, src = qT_s[:, 0:4, :], src[:, :, DEC:P]
                            else:
                                dst = qT_p[:, 0:4, j * P:(j + 1) * P]
                            dve.tensor_scalar(dst, src, gq[0:QK, l:l + 1], None, ALU.mult).then_inc(S["qkt_dve"], 1)
                        else:
                            c, w = key_tile(j)
                            src = src[:, :, 0:w]
                            dst = kT_s[:, 0:4, c:c + w] if j <= CACHE_TILES else kT_p[:, 0:4, c - S_KEYS:c - S_KEYS + w]
                            dve.tensor_copy(dst, src).then_inc(S["qkt_dve"], 1)

                def batches_run(todo):
                    for n, b in enumerate(todo):
                        batch_first(b)
                        if n:
                            batch_turned(todo[n - 1])
                    batch_turned(todo[-1])

                batches_run(L["s_batches"])

                for g2 in range(4):
                    u = L["mix"][g2]
                    filled(dve, u)
                    for e in range(2):
                        g = 2 * g2 + e
                        dst = ug[:, 0:PT_, g * GDIM:(g + 1) * GDIM]
                        ins = dve.scalar_tensor_tensor(
                            out=dst, in0=ps[:, u.bank, e * 256:(e + 1) * 256].rearrange("p (t d) -> p t d", t=PT_),
                            scalar=gT[:, G_BS + GROUPS * l + g:G_BS + GROUPS * l + g + 1], in1=dst, op0=ALU.add, op1=ALU.mult)
                    ins.then_inc(S["mix_out"], 1)
                u = L["mix"][4]
                filled(dve, u)
                for g in range(GROUPS):
                    dst = ug[DEC:P, PT_, g * GDIM:(g + 1) * GDIM]
                    ins = dve.scalar_tensor_tensor(
                        out=dst, in0=ps[DEC:P, u.bank, g * GDIM:(g + 1) * GDIM],
                        scalar=gT[DEC:P, G_BS_S + GROUPS * l + g:G_BS_S + GROUPS * l + g + 1], in1=dst,
                        op0=ALU.add, op1=ALU.mult)
                ins.then_inc(S["mix_out"], 1)
                dve.wait_ge(v_stored, 16 * (l + 1))
                for n in range(HEAD_PAIRS + 2):
                    if n < HEAD_PAIRS:
                        st = L["s_steps"][n]
                        for e, ((c, w), u) in enumerate(zip(S_SPANS, st["s"])):
                            filled(dve, u)
                            ins = dve.tensor_reduce(mx[:, e:e + 1], bank(u, cols=w), AX.X, ALU.max)
                        link(ins)
                        link(dve.tensor_reduce(mx[:, 3:4], mx[:, 0:3], AX.X, ALU.max))
                        dve.tensor_scalar(nm[:, n % 2, 0:1], mx[:, 3:4], -SCALE, None, ALU.mult).then_inc(nm_ready, 1)
                    if 1 <= n <= HEAD_PAIRS:
                        m = n - 1
                        for j in (0, 2):
                            u = L["s_steps"][m]["t"][j]
                            filled(dve, u)
                            if m >= 2 and not j:
                                filled(dve, L["s_steps"][m - 2]["o"])
                            first, count = S_TRANS[j]
                            rows = slice(0, P if j < 2 else DEC)
                            dve.tensor_copy(pT[rows, m % 2, first:first + count, :],
                                            bank(u, rows, count * P).rearrange("p (j c) -> p j c", j=count)
                                            ).then_inc(S["pt_dve"], 1)
                    if n >= 2:
                        m = n - 2
                        emptied(dve, L["s_steps"][m]["s"][-1])
                        link(dve.tensor_reduce(linv[:, m % 2, 0:1], lsum[:, m % 4, 0:3], AX.X, ALU.add))
                        link(dve.reciprocal(linv[:, m % 2, 0:1], linv[:, m % 2, 0:1]))
                        u = L["s_steps"][m]["o"]
                        filled(dve, u)
                        dve.tensor_scalar(o_s[:, m, :], bank(u, cols=VDIM), linv[:, m % 2, 0:1], None, ALU.mult
                                          ).then_inc(S["o_out"], 1)
                dve.wait_ge(gm_squared, l + 1)
                n = NT * GROUPS
                link(dve.tensor_reduce(ms[:, 0:n], wide_g[:, :].rearrange("p (n d) -> p n d", d=GDIM), AX.X, ALU.add))
                root(l, "gm", n, ALL, 1.0 / GDIM)
                ugg = ug[:, :, :].rearrange("p t (g d) -> p (t g) d", d=GDIM)
                dve.tensor_tensor(ugg, ugg, rs[:, 0:n].unsqueeze(2).to_broadcast([P, n, GDIM]), ALU.mult
                                  ).then_inc(gm_normed, 1)

                batches_run(L["p_batches"])

                for n in range(len(P_STEPS) + 2):
                    if n < len(P_STEPS):
                        i, _, nh = P_STEPS[n]
                        u = L["p_steps"][n]["s"]
                        w = (i + 1) * P
                        sc = ps[:, u.bank, 0:nh * w].rearrange("p (h c) -> p h c", h=nh)
                        filled(dve, u)
                        link(dve.memset(ps[0:CHUNK, u.bank, 0:nh * w].rearrange("p (h c) -> p h c", h=nh)[:, :, w - CHUNK:w],
                                        NEG_INF))
                        link(dve.tensor_reduce(mx[:, 0:nh], sc, AX.X, ALU.max))
                        dve.tensor_scalar(nm[:, n % 2, 0:nh], mx[:, 0:nh], -SCALE, None, ALU.mult).then_inc(nm_ready, 1)
                    if 1 <= n <= len(P_STEPS) and (n - 1) % 2:
                        m = n - 1
                        i, _, nh = P_STEPS[m]
                        u = L["p_steps"][m]["t"]
                        filled(dve, u)
                        if m >= 2:
                            filled(dve, L["p_steps"][m - 2]["o"])
                        w = nh * (i + 1)
                        dve.tensor_copy(pT[:, 1, 0:w, :], bank(u, cols=w * P).rearrange("p (j c) -> p j c", j=w)
                                        ).then_inc(S["pt_dve"], 1)
                    if n >= 2:
                        m = n - 2
                        i, h0, nh = P_STEPS[m]
                        emptied(dve, L["p_steps"][m]["s"])
                        link(dve.reciprocal(linv[:, m % 2, 0:nh], lsum[:, m % 4, 0:nh]))
                        u = L["p_steps"][m]["o"]
                        filled(dve, u)
                        c = i * WIDTH + h0 * VDIM
                        dve.tensor_tensor(o_tm[:, c:c + nh * VDIM].rearrange("p (h d) -> p h d", h=nh),
                                          bank(u, cols=nh * VDIM).rearrange("p (h d) -> p h d", h=nh),
                                          linv[:, m % 2, 0:nh].unsqueeze(2).to_broadcast([P, nh, VDIM]), ALU.mult
                                          ).then_inc(S["o_out"], 1)
                dve.wait_ge(o_squared, l + 1)
                link(dve.tensor_reduce(ms[:, 0:O_GROUPS], wide_o[:, :].rearrange("p (n d) -> p n d", d=VDIM), AX.X, ALU.add))
                root(l, "o", O_GROUPS, ALL, 1.0 / VDIM)
                og = o_tm[:, :].rearrange("p (n d) -> p n d", d=VDIM)
                dve.tensor_tensor(og, og, rs[:, 0:O_GROUPS].unsqueeze(2).to_broadcast([P, O_GROUPS, VDIM]), ALU.mult
                                  ).then_inc(o_normed, 1)
                for k in range(KT):
                    u = L["mt"][k]
                    g = G_OUT + 8 * l + k
                    dve.wait_ge(m_hi, (KT + 1) * l + k + 1)
                    low(hs_lo[:, k, 0:SEQ], bank(u), gT[:, g:g + 1], hs_hi[:, k, 0:SEQ]).then_inc(S["merged_out"], 1)
                u = L["mt"][KT]
                filled(dve, u)
                g = G_OUT + 8 * l
                dve.tensor_tensor(ms_sb[:, :, :], bank(u).rearrange("p (k c) -> p k c", k=KT),
                                  gT[:, g:g + KT].unsqueeze(2).to_broadcast([P, KT, DEC]), ALU.mult
                                  ).then_inc(S["merged_out"], 1)
                dve.wait_ge(m_hi, (KT + 1) * (l + 1))
                dve.tensor_tensor(hs_lo[:, :, SEQ:TOK], ms_sb[:, :, :], hs_hi[:, :, SEQ:TOK].bitcast(F32), ALU.subtract
                                  ).then_inc(m_lo, 1)

                def add_to_x(m, u):
                    x = halves(xT[:, m, :])
                    return dve.tensor_tensor(x, ps[:, u.bank:u.bank + 2, 0:HALF], x, ALU.add)

                for m in range(KT):
                    filled(dve, L["wo"][m][1])
                    add_to_x(m, L["wo"][m][0]).then_inc(S["wo_added"], 1)
                split_low(2 * l + 1, G_FFN + KT * l)
                r_by_token(l, "r2", L["ss2"], 2 * l + 2)
                filled(dve, L["rb"][0])
                dve.tensor_copy(rb[:, 0:SEQ], bank(L["rb"][0])).then_inc(S["rb_out"], 1)
                filled(dve, L["rb"][1])
                dve.tensor_copy(rb[:, SEQ:TOK], ps[:, L["rb"][1].bank, DEC:P]).then_inc(S["rb_out"], 1)
                emptied(dve, L["rb"][1])

                def gate_in(f, u, off):
                    dve.wait_ge(full, off[0] + u[1].done)
                    dve.tensor_tensor(halves(gate[:, f, :]), ps[:, u[0].bank:u[0].bank + 2, 0:HALF], halves(rb[:, :]),
                                      ALU.mult).then_inc(S["ffn_out"], 1)

                def hidden(f, u, off, no):
                    dve.wait_ge(full, off[0] + u[1].done)
                    dve.wait_ge(gate_done, no)
                    dve.tensor_tensor(halves(hid[:, f, :]), ps[:, u[0].bank:u[0].bank + 2, 0:HALF], halves(gate[:, f, :]),
                                      ALU.mult).then_inc(S["ffn_out"], 1)
                    dve.wait_ge(act_hi_done, no)
                    dve.tensor_tensor(act_lo[:, f, :], hid[:, f, :], act_hi[:, f, :].bitcast(F32), ALU.subtract
                                      ).then_inc(act_lo_done, 1)

                def down(units, off):
                    for m, u in enumerate(units):
                        dve.wait_ge(full, off[0] + u[1].done)
                        add_to_x(m, u[0]).then_inc(S["ffn_out"], 1)

                pairs = 2 * FPAIRS * l
                for f in range(2):
                    gate_in(f, L["g0"][f], (0, 0))
                for f in range(2):
                    hidden(f, L["u0f"][f], (0, 0), pairs + f + 1)
                with dve.Fori(0, BODIES) as i:
                    off = (i * L["body_size"], i * L["body_per"])
                    for s in range(2):
                        g, d, u = L["body"][s]
                        for f in range(2):
                            gate_in(f, g[f], off)
                        dve.wait_ge(S["ffn_out"], off[1] + g[1][0].freed[1])
                        down(d, off)
                        for f in range(2):
                            hidden(f, u[f], off, i * 4 + (pairs + 3 + 2 * s + f))
                dve.wait_ge(S["ffn_out"], L["last_u"][1].freed[1])
                down(L["last"], (0, 0))
                emptied(dve, L["last"][-1][0])
            for t in range(NT):
                u = y_units[t][0]
                rows = slice(0, P if t < PT_ else DEC)
                filled(dve, u)
                dve.tensor_copy(x_tm[rows, t, 0:WIDTH], bank(u, rows)).then_inc(S["y_dve"], 1)

        @block.tensor
        def _(pe):
            def free(u):
                if u.before:
                    pe.wait_ge(S[u.before[0]], u.before[1])

            def split_ready(n):
                pe.wait_ge(lo_split, slots.raw[n] + 1)

            def turn(dst, src, n):
                return pe.transpose(dst, src, ident[0:n, 0:n])

            pe.wait_ge(ident_ready, 1)
            pe.wait_ge(gains_loaded, 16 * GAIN_LOADS)
            turn(bank(gains_unit, cols=P), g_in[:, :], P).then_inc(full, 1)
            for t in range(NT):
                pe.wait_ge(x_loaded[t], 16)
                for e, u in enumerate(xt_units[t]):
                    free(u)
                    for j in range(4):
                        c = (4 * e + j) * P
                        if t < PT_:
                            ins = turn(ps[:, u.bank, j * P:(j + 1) * P], x_tm[:, t, c:c + P], P)
                        else:
                            ins = pe.transpose(ps[:, u.bank, j * P:j * P + DEC], x_tm[DEC:P, t, c:c + P],
                                               ident[DEC:P, DEC:P])
                    ins.then_inc(full, 1)
            pe.wait_ge(const_ready, 1)

            def by_token(u, t, k_w, n, cols):
                c = TILE_AT[t]
                for k in range(KT):
                    w = slice(k * cols, (k + 1) * cols)
                    x_hi, x_lo = hs_hi[:, k, c:c + P], hs_lo[:, k, c:c + P]
                    dst = bank(u, cols=cols)
                    pe.matmul(dst, x_hi, w_hi[:, k_w, w], start=(k == 0), stop=False)
                    pe.matmul(dst, x_hi, w_lo[:, k_w, w], start=False, stop=False)
                    ins = pe.matmul(dst, x_lo, w_hi[:, k_w, w], start=False, stop=(k == KT - 1))
                return ins

            def by_feature(units, k_w, at, step, count, x_hi, x_lo, ready=None):
                for k in range(count):
                    if ready:
                        ready(k)
                    w = slice(at + k * step, at + k * step + P)
                    hi, lo = w_hi[:, k_w, w], w_lo[:, k_w, w]
                    for h, u in enumerate(units):
                        cols = slice(h * HALF, (h + 1) * HALF)
                        pe.matmul(bank(u, cols=HALF), hi, x_hi[:, k, cols], start=(k == 0), stop=False)
                        pe.matmul(bank(u, cols=HALF), hi, x_lo[:, k, cols], start=False, stop=False)
                    for h, u in enumerate(units):
                        cols = slice(h * HALF, (h + 1) * HALF)
                        ins = pe.matmul(bank(u, cols=HALF), lo, x_hi[:, k, cols], start=False, stop=(k == count - 1))
                        if k == count - 1:
                            ins.then_inc(full, 1)

            def sums_by_token(u, tiles, dst_cols=1):
                free(u)
                for t, c in enumerate(TILE_AT):
                    for m, src in enumerate(tiles):
                        ins = pe.matmul(ps[:, u.bank, t:t + 1], src[:, c:c + P], ones[:, 0:1], start=(m == 0),
                                        stop=(m == len(tiles) - 1))
                ins.then_inc(full, 1)

            for l, L in enumerate(plan):
                def tokens(units, n, cols):
                    split_ready(n)
                    for t, u in enumerate(units):
                        free(u)
                        by_token(u, t, slots.raw[n] % 2, n, cols).then_inc(full, 1)

                pe.wait_ge(hs_lo_done, (2 * l + 1) * KT)
                tokens(L["kv"], L["w_in"][0], KV_KR)
                pe.wait_ge(summed, (2 * l + 1) * KT)
                sums_by_token(L["ss1"], [sumsq])
                split_ready(L["w_in"][1])
                for m in range(2):
                    for u in L["q"][m]:
                        free(u)
                    by_feature(L["q"][m], slots.raw[L["w_in"][1]] % 2, m * P, COLS, KT, hs_hi, hs_lo)
                tokens(L["v0"], L["w_in"][2], COLS)
                emptied(pe, L["q"][1][1])
                sums_by_token(L["ssq"], [gate[:, 0, :], gate[:, 1, :]])
                for j, name in ((3, "v1"), (4, "u0"), (5, "u1")):
                    tokens(L[name], L["w_in"][j], COLS)

                pe.wait_ge(ckv_normed, l + 1)
                pe.wait_ge(layer_loaded, 16 * SMALL * (l + 1))
                for j, u in enumerate(L["ct"]):
                    free(u)
                    if j == 0:
                        srcs = [ckv_n[:, t, :] for t in range(PT_)]
                    elif j == 1:
                        srcs = [ckv_n[:, PT_, :]]
                    else:
                        srcs = [cache_in[:, 4 * (j - 2) + i, :] for i in range(4)]
                    for i, src in enumerate(srcs):
                        ins = turn(ps[:, u.bank, i * P:(i + 1) * P], src, P)
                    ins.then_inc(full, 1)
                for j, u in enumerate(L["wst"]):
                    free(u)
                    if j < 2:
                        for i in range(4):
                            ins = turn(ps[:, u.bank, i * P:(i + 1) * P], ws_in[:, 4 * j + i, :], P)
                    else:
                        for g in range(GROUPS):
                            ins = pe.matmul(ps[DEC:P, u.bank, g * DEC:(g + 1) * DEC], ws_in[0:DEC, g, 0:DEC],
                                            ident[0:DEC, 0:DEC], start=True, stop=True)
                    ins.then_inc(full, 1)

                def up(b):
                    for jj, j in enumerate(b["tiles"]):
                        for e, u in enumerate(b["up"][jj]):
                            free(u)
                            if b["what"] == "q":
                                c = TILE_AT[j]
                                for m in range(2):
                                    w = m * HEADS * QK + e * 4 * QK
                                    ins = pe.matmul(bank(u, cols=4 * QK), qlatT[:, m, c:c + P],
                                                    raw[:, L["wq"] % 2, w:w + 4 * QK], start=(m == 0), stop=(m == 1))
                            else:
                                c, w = key_tile(j)
                                wkv = raw[:, L["wkv"] % 2, 0:2 * WIDTH].rearrange("p (h c) -> p h c", h=HEADS)
                                ins = pe.matmul(ps[0:w, u.bank, :].rearrange("p (h c) -> p h c", h=HEADS),
                                                ckvT[:, c:c + w], wkv[:, :, e * NOPE:(e + 1) * NOPE],
                                                start=True, stop=True)
                            ins.then_inc(full, 1)

                spread = [(2 * (CACHE_TILES + PT_) // 2) * l]

                def turn_batch(b):
                    seq = b["seq"]
                    if b["what"] == "q":
                        pe.wait_ge(sq_free, NB * l + seq + 1)
                    else:
                        emptied(pe, b["up"][-1][0])
                        if b["tiles"][0] != CACHE_TILES:
                            spread[0] += len(b["tiles"])
                            pe.wait_ge(kr_spread, spread[0])
                    for jj, j in enumerate(b["tiles"]):
                        w = P if b["what"] == "q" else key_tile(j)[1]
                        for e, u in enumerate(b["turn"][jj]):
                            free(u)
                            for i in range(4):
                                ins = turn(ps[0:QK, u.bank, i * P:i * P + w], tm[0:w, seq % 2, jj, 4 * e + i, :], w)
                            ins.then_inc(full, 1)

                def batches_run(todo):
                    for n, b in enumerate(todo):
                        up(b)
                        if n:
                            turn_batch(todo[n - 1])
                    turn_batch(todo[-1])

                for n in (L["wq"], L["wkv"]):
                    pe.wait_ge(raw_loaded[n % 2], 16 * (n // 2 + 1))
                emptied(pe, L["ct"][2])
                emptied(pe, L["ct"][3])
                batches_run(L["s_batches"])

                pe.wait_ge(vn_done, l + 1)
                pe.wait_ge(wsT_masked, l + 1)
                emptied(pe, L["u1"][-1])
                for g2 in range(4):
                    u = L["mix"][g2]
                    free(u)
                    for e in range(2):
                        g = 2 * g2 + e
                        ins = pe.matmul(ps[:, u.bank, e * 256:(e + 1) * 256].rearrange("p (t d) -> p t d", t=PT_),
                                        wsT[:, g, :], gv[:, 0:PT_, g * GDIM:(g + 1) * GDIM], start=True, stop=True)
                    ins.then_inc(full, 1)
                u = L["mix"][4]
                free(u)
                for g in range(GROUPS):
                    ins = pe.matmul(ps[DEC:P, u.bank, g * GDIM:(g + 1) * GDIM], wsT_s[DEC:P, g, :],
                                    gv[DEC:P, PT_, g * GDIM:(g + 1) * GDIM], start=True, stop=True)
                ins.then_inc(full, 1)

                emptied(pe, L["s_batches"][-1]["turn"][-1][0])
                emptied(pe, L["s_batches"][-1]["turn"][-1][1])
                emptied(pe, L["s_batches"][-1]["up"][-1][1])
                for n in range(HEAD_PAIRS + 2):
                    if n < HEAD_PAIRS:
                        for (c, w), u in zip(S_SPANS, L["s_steps"][n]["s"]):
                            free(u)
                            for e in range(2):
                                ins = pe.matmul(ps[e * DEC:(e + 1) * DEC, u.bank, 0:w], qT_s[:, 2 * n + e, :],
                                                kT_s[:, 2 * n + e, c:c + w], start=True, stop=True)
                            ins.then_inc(full, 1)
                    if 1 <= n <= HEAD_PAIRS:
                        m = n - 1
                        emptied(pe, L["s_steps"][m]["s"][-1])
                        for (first, count), u in zip(S_TRANS, L["s_steps"][m]["t"]):
                            free(u)
                            for i in range(count):
                                c = (first + i) * P
                                w = min(P, S_KEYS - c)
                                ins = turn(ps[0:w, u.bank, i * P:(i + 1) * P], p_sb[:, m % 2, c:c + w], P)
                            ins.then_inc(full, 1)
                    if n >= 2:
                        m = n - 2
                        for u in L["s_steps"][m]["t"]:
                            emptied(pe, u)
                        u = L["s_steps"][m]["o"]
                        free(u)
                        for e in range(2):
                            h = 2 * m + e
                            for j in range(CACHE_TILES + 1):
                                w = key_tile(j)[1]
                                ins = pe.matmul(ps[e * DEC:(e + 1) * DEC, u.bank, 0:VDIM],
                                                pT[0:w, m % 2, j, e * DEC:(e + 1) * DEC],
                                                v_s[0:w, j, h * VDIM:(h + 1) * VDIM],
                                                start=(j == 0), stop=(j == CACHE_TILES))
                        ins.then_inc(full, 1)

                batches_run(L["p_batches"])

                emptied(pe, L["p_batches"][-1]["turn"][-1][0])
                emptied(pe, L["p_batches"][-1]["turn"][-1][1])
                emptied(pe, L["p_batches"][-1]["up"][-1][1])
                for n in range(len(P_STEPS) + 2):
                    if n < len(P_STEPS):
                        i, h0, nh = P_STEPS[n]
                        u = L["p_steps"][n]["s"]
                        w = (i + 1) * P
                        free(u)
                        for e in range(nh):
                            ins = pe.matmul(ps[:, u.bank, e * w:(e + 1) * w], qT_p[:, h0 + e, i * P:(i + 1) * P],
                                            kT_p[:, h0 + e, 0:w], start=True, stop=True)
                        ins.then_inc(full, 1)
                    if 1 <= n <= len(P_STEPS):
                        m = n - 1
                        i, h0, nh = P_STEPS[m]
                        emptied(pe, L["p_steps"][m]["s"])
                        u = L["p_steps"][m]["t"]
                        free(u)
                        for e in range(nh * (i + 1)):
                            ins = turn(ps[:, u.bank, e * P:(e + 1) * P], p_sb[:, m % 2, e * P:(e + 1) * P], P)
                        ins.then_inc(full, 1)
                    if n >= 2:
                        m = n - 2
                        i, h0, nh = P_STEPS[m]
                        emptied(pe, L["p_steps"][m]["t"])
                        u = L["p_steps"][m]["o"]
                        free(u)
                        for e in range(nh):
                            for j in range(i + 1):
                                ins = pe.matmul(ps[:, u.bank, e * VDIM:(e + 1) * VDIM], pT[:, m % 2, e * (i + 1) + j, :],
                                                v_p[:, j, (h0 + e) * VDIM:(h0 + e + 1) * VDIM],
                                                start=(j == 0), stop=(j == i))
                        ins.then_inc(full, 1)

                pe.wait_ge(o_normed, l + 1)
                for k in range(KT):
                    u = L["mt"][k]
                    free(u)
                    for t in range(PT_):
                        src = o_tm[:, t * WIDTH + k * P:t * WIDTH + (k + 1) * P] if k < 4 else ug[:, t, (k - 4) * P:(k - 3) * P]
                        ins = turn(ps[:, u.bank, t * P:(t + 1) * P], src, P)
                    ins.then_inc(full, 1)
                u = L["mt"][KT]
                free(u)
                for k in range(KT):
                    if k < 4:
                        for e in range(2):
                            half = slice(e * DEC, (e + 1) * DEC)
                            pe.matmul(ps[half, u.bank, k * DEC:(k + 1) * DEC], o_s[half, k, :], ident[half, half],
                                      start=True, stop=True)
                    else:
                        ins = pe.transpose(ps[:, u.bank, k * DEC:(k + 1) * DEC], ug[DEC:P, PT_, (k - 4) * P:(k - 3) * P],
                                           ident[DEC:P, DEC:P])
                ins.then_inc(full, 1)

                pe.wait_ge(m_lo, l + 1)
                for j, n in enumerate(L["w_o"]):
                    split_ready(n)
                    for e in range(2):
                        units = L["wo"][2 * j + e]
                        for u in units:
                            free(u)
                        by_feature(units, slots.raw[n] % 2, e * P, COLS, KT, hs_hi, hs_lo)

                def gate_or_up(pair, k_w):
                    for f in range(2):
                        by_feature(pair[f], k_w, f * P, COLS, KT, hs_hi, hs_lo)

                n = L["ffn_in"][0]
                split_ready(n)
                for f in range(2):
                    for u in L["g0"][f]:
                        free(u)
                    by_feature(L["g0"][f], slots.raw[n] % 2, f * P, COLS, KT, hs_hi, hs_lo,
                               ready=lambda k: pe.wait_ge(hs_lo_done, (2 * l + 1) * KT + k + 1))
                pe.wait_ge(summed, (2 * l + 2) * KT)
                sums_by_token(L["ss2"], [sumsq])
                pe.wait_ge(r_ready, 2 * l + 2)
                for j, u in enumerate(L["rb"]):
                    free(u)
                    for t in (range(PT_) if j == 0 else [PT_]):
                        ins = pe.matmul(ps[:, u.bank, (t % PT_) * P:(t % PT_ + 1) * P],
                                        r_tok[:, t:t + 1].to_broadcast([P, P]), ident[:, :], start=True, stop=True)
                    ins.then_inc(full, 1)
                n = L["ffn_in"][1]
                split_ready(n)
                for f in range(2):
                    for u in L["u0f"][f]:
                        free(u)
                    by_feature(L["u0f"][f], slots.raw[n] % 2, f * P, COLS, KT, hs_hi, hs_lo)
                emptied(pe, L["rb"][1])
                n0 = L["body_slots"][0]
                pairs = 2 * FPAIRS * l
                with pe.Fori(0, BODIES) as i:
                    for s in range(2):
                        for j, groups in enumerate(L["body"][s]):
                            n = n0 + 3 * s + j
                            pe.wait_ge(lo_split, i * 6 + (slots.raw[n] + 1))
                            if j == 1:
                                pe.wait_ge(act_lo_done, i * 4 + (pairs + 2 * s + 2))
                            for m, units in enumerate(groups):
                                pe.wait_ge(S["ffn_out"], i * L["body_per"] + units[1].before[1])
                                if j == 1:
                                    by_feature(units, slots.raw[n] % 2, m * P, D_MODEL, 2, act_hi, act_lo)
                                else:
                                    by_feature(units, slots.raw[n] % 2, m * P, COLS, KT, hs_hi, hs_lo)
                n = L["last_slot"]
                split_ready(n)
                pe.wait_ge(act_lo_done, pairs + 2 * FPAIRS)
                for m, units in enumerate(L["last"]):
                    for u in units:
                        free(u)
                    by_feature(units, slots.raw[n] % 2, m * P, D_MODEL, 2, act_hi, act_lo)

            emptied(pe, plan[-1]["last"][-1][0])
            for t in range(NT):
                w = P if t < PT_ else DEC
                for e, u in enumerate(y_units[t]):
                    free(u)
                    for j in range(4):
                        ins = turn(ps[0:w, u.bank, j * P:(j + 1) * P], xT[:, 4 * e + j, t * P:t * P + w], P)
                    ins.then_inc(full, 1)


OUTS = [("y_prompt", (1, SEQ, D_MODEL)), ("y_sample", (1, DEC, D_MODEL)), ("ckv_prompt", (DEPTH, 1, SEQ, KV_LORA)),
        ("krope_prompt", (DEPTH, 1, SEQ, ROPE)), ("ckv_sample", (DEPTH, 1, DEC, KV_LORA)),
        ("krope_sample", (DEPTH, 1, DEC, ROPE)), ("gmlp_v_sample", (DEPTH, 1, DEC, WIDTH))]


def kernel(**inputs):
    import concourse.bacc as bacc
    from concourse.bass_utils import run_bass_kernel_spmd

    pos = np.concatenate([np.arange(SEQ), PAST + np.arange(DEC)]).astype(np.float32)
    half = ROPE // 2
    inv = np.float32(THETA) ** (-np.arange(half, dtype=np.float32) / np.float32(half))
    ang = pos[:, None] * inv[None, :]
    arrays = {name: np.ascontiguousarray(x) for name, x in inputs.items()}
    arrays["trig"] = np.concatenate([np.cos(ang), np.sin(ang)], axis=1).astype(np.float32)

    nc = bacc.Bacc("TRN2", target_bir_lowering=False, num_devices=1)
    a = {name: nc.dram_tensor("in_" + name, x.shape, F32, kind="ExternalInput").ap() for name, x in arrays.items()}
    out = {name: nc.dram_tensor("out_" + name, shape, F32, kind="ExternalOutput").ap() for name, shape in OUTS}
    trunk(nc, a, out)
    r = run_bass_kernel_spmd(nc, [{"in_" + name: x for name, x in arrays.items()}], core_ids=[0])
    return tuple(r.results[0]["out_" + name] for name, _ in OUTS)
```

```python
from contextlib import ExitStack

import numpy as np

import concourse.bass as bass
from concourse import mybir

D_MODEL, SEQ, DEC, DEPTH, PAST = 1024, 512, 64, 2, 1024
HEADS, NOPE, ROPE, VDIM = 8, 64, 32, 64
QK = NOPE + ROPE
Q_LORA, KV_LORA = 256, 128
GROUPS, GDIM = 8, 64
WIDTH = GROUPS * GDIM
D_FF = 2816
CHUNK = 64
EPS = 1e-6
SCALE = float(QK) ** -0.5
NEG_INF = -1e30
THETA = 10000.0

P = 128
TOK = SEQ + DEC
HALF = TOK // 2
KT = D_MODEL // P
TILE_AT = [0, 128, 256, 384, TOK - P]
NT = len(TILE_AT)
PT_ = SEQ // P
CACHE_TILES = PAST // P
S_KEYS = PAST + DEC
ALL_KEYS = S_KEYS + SEQ
KV_KR = KV_LORA + ROPE
BLOCK = 2048
COLS = BLOCK // KT
FPAIRS = D_FF // COLS
BODIES = (FPAIRS - 1) // 2
assert FPAIRS == 1 + 2 * BODIES

F32 = mybir.dt.float32
F32R = mybir.dt.float32r
ALU = mybir.AluOpType
ACT = mybir.ActivationFunctionType
AX = mybir.AxisListType

G_MIX, G_FFN, G_QL, G_BS, G_OUT = 0, 16, 32, 36, 52
G_QN, G_KN = 68, 70
G_BS_S = 72
G_ROWS = 88


class Unit:

    def __init__(self, n, done, before, freed):
        self.n, self.bank, self.done, self.before, self.freed = n, n % 8, done, before, freed


class Ring:

    def __init__(self):
        self.units, self.values, self.done = [], {}, 0

    def before(self):
        return self.units[-8].freed if len(self.units) >= 8 else None

    def add(self, sem, with_last=False):
        if not with_last:
            self.values[sem] = self.values.get(sem, 0) + 1
        self.done += 1
        u = Unit(len(self.units), self.done, self.before(), (sem, self.values[sem]))
        self.units.append(u)
        return u

    def skip(self):
        self.units.append(Unit(len(self.units), self.done, None, self.before()))

    def repeat(self, first, times):
        body = self.units[first:]
        size = len(body)
        sem = body[0].freed[0]
        assert size % 8 == 0 and all(u.freed[0] == sem for u in body)
        per = len({u.freed[1] for u in body})
        for t in range(1, times):
            for u in body:
                self.units.append(Unit(len(self.units), u.done + size * t, self.before(),
                                       (sem, u.freed[1] + per * t)))
        self.done += size * (times - 1)
        self.values[sem] += per * (times - 1)
        for j, u in enumerate(body):
            steady = self.units[first + size + j].before
            u.before = (sem, steady[1] - per)
            assert u.before[1] > 0
        return size, per


class Slots:

    def __init__(self):
        self.raw, self.n_split, self.last = [], 0, {}

    def load(self, split=True):
        self.raw.append(self.n_split if split else None)
        self.n_split += split
        return len(self.raw) - 1

    def used(self, n, unit):
        self.last[n] = unit


def prep_tiles():
    own = CACHE_TILES
    sample = [("q", PT_)] + [("k", j) for j in range(own + 1)]
    k = own + 1
    prompt = [("q", 0), ("q", 1), ("k", k), ("q", 2), ("k", k + 1), ("q", 3), ("k", k + 2), ("k", k + 3)]
    return sample, prompt


def key_tile(j):
    if j < CACHE_TILES:
        return j * P, P
    if j == CACHE_TILES:
        return PAST, DEC
    return S_KEYS + (j - CACHE_TILES - 1) * P, P


S_TILES, P_TILES = prep_tiles()
PREPS = len(S_TILES) + len(P_TILES)
SPREADS = CACHE_TILES + PT_
S_SPANS = [(0, 512), (512, 512), (1024, 64)]
S_TRANS = [(0, 4), (4, 4), (8, 1)]
HEAD_PAIRS = HEADS // 2
P_STEPS = [(i, h, n) for i, n in ((0, 4), (1, 2), (2, 1), (3, 1)) for h in range(0, HEADS, n)]
STEPS = HEAD_PAIRS + len(P_STEPS)
O_PARTS = [(PT_ * WIDTH, HEAD_PAIRS)] + [(i * WIDTH, HEADS) for i in range(PT_)]
O_SQUARED, O_ASKED, O_APPLIED = (0, 4, 8, 16), (0, 5, 9, 17), (4, 11, 13, 20)
GM_ASKED = 2
MERGED = [KT, 4, 5, 6, 7, 0, 1, 2, 3]
SMALL, GAIN_LOADS = 8, 11
ROOTS = (["r1", "kv", "q", "ln"] + [f"b{n}" for n in range(PREPS)]
         + ["o0", "gm", "o1", "o2", "o3", "o4", "r2"])


def root_no(l, name):
    return l * len(ROOTS) + ROOTS.index(name) + 1


def build_plan():
    ring, slots, plan = Ring(), Slots(), []
    gains = ring.add("gains_turned")
    xt = [[ring.add("x_turned_dve"), ring.add("x_turned_act")] for _ in range(NT)]
    for l in range(DEPTH):
        L = {}
        L["w_in"] = w = [slots.load() for _ in range(6)]
        L["q"] = [[ring.add("qlat_out") for _ in range(2)] for _ in range(2)]
        slots.used(w[0], L["q"][-1][-1])
        L["ss1"] = ring.add("sumsq_out")
        L["kv"] = [ring.add("kv_out") for _ in range(NT)]
        slots.used(w[1], L["kv"][-1])
        L["v0"] = [ring.add("gelu_out") for _ in range(NT)]
        L["ssq"] = ring.add("sumsq_out")
        L["v1"] = [ring.add("gelu_out") for _ in range(NT)]
        L["ct"] = [ring.add("ckvt_act" if j % 2 else "ckvt_dve") for j in range(4)]
        L["wst"] = [ring.add("wst_out") for _ in range(3)]
        L["u0"] = [ring.add("gelu_out") for _ in range(NT)]
        L["wq"], L["wkv"] = slots.load(False), slots.load(False)
        L["preps"] = []
        spreads = SPREADS * l

        def prep(out, todo, steps):
            nonlocal spreads
            for n in steps:
                if n < len(todo):
                    what, tile = todo[n]
                    spreads += what == "k" and tile != CACHE_TILES
                    out.append({"what": what, "tile": tile, "seq": len(L["preps"]), "spreads": spreads,
                                "up": (ring.add("qz_out" if what == "q" else "k_out"),
                                       ring.add("qz_out" if what == "q" else "v_out"))})
                    L["preps"].append(out[-1])
                if n >= 2:
                    out[n - 2]["turn"] = (ring.add("qkt_dve"), ring.add("qkt_act"))

        L["s_preps"], L["p_preps"] = [], []
        prep(L["s_preps"], S_TILES, [0])
        L["u1"] = [ring.add("gelu_out") for _ in range(NT)]
        for j, name in enumerate(("v0", "v1", "u0", "u1")):
            slots.used(w[2 + j], L[name][-1])
        prep(L["s_preps"], S_TILES, range(1, len(S_TILES) + 2))
        L["mix"] = [ring.add("mix_out") for _ in range(5)]
        L["s_steps"] = steps = [{} for _ in range(HEAD_PAIRS)]
        for n in range(HEAD_PAIRS + 2):
            if n >= HEAD_PAIRS:
                prep(L["p_preps"], P_TILES, [n - HEAD_PAIRS])
            if n < HEAD_PAIRS:
                steps[n]["s"] = [ring.add("s_exp") for _ in S_SPANS]
            if 1 <= n <= HEAD_PAIRS:
                steps[n - 1]["t"] = [ring.add("pt_dve"), ring.add("pt_act"), ring.add("pt_dve")]
            if n >= 2:
                steps[n - 2]["o"] = ring.add("o_out")
        prep(L["p_preps"], P_TILES, range(2, len(P_TILES) + 2))
        slots.used(L["wq"], L["p_preps"][-3]["up"][1])
        slots.used(L["wkv"], L["p_preps"][-1]["up"][1])
        L["p_steps"] = steps = [{} for _ in P_STEPS]
        for n in range(len(P_STEPS) + 2):
            if n < len(P_STEPS):
                steps[n]["s"] = ring.add("s_exp")
            if 1 <= n <= len(P_STEPS):
                steps[n - 1]["t"] = ring.add("pt_act" if (n - 1) % 2 == 0 else "pt_dve")
            if n >= 2:
                steps[n - 2]["o"] = ring.add("o_out")
        L["mt"] = {k: ring.add("merged_out") for k in MERGED}
        L["w_o"] = [slots.load() for _ in range(4)]
        if len(ring.units) % 2:
            ring.skip()
        L["wo"] = [[ring.add("wo_added", with_last=h > 0) for h in range(2)] for _ in range(KT)]
        for j, n in enumerate(L["w_o"]):
            slots.used(n, L["wo"][2 * j + 1][1])

        def pair_units(n, between=lambda: None):
            out = []
            for f in range(2):
                out.append([ring.add("ffn_out", with_last=h > 0) for h in range(2)])
                if f == 0:
                    between()
            slots.used(n, out[1][1])
            return out

        def down_units(n):
            out = [[ring.add("ffn_out", with_last=h > 0) for h in range(2)] for _ in range(KT)]
            slots.used(n, out[-1][1])
            return out

        L["ffn_in"] = [slots.load() for _ in range(2)]

        def sums():
            L["ss2"] = ring.add("sumsq_out")
            ring.skip()

        L["g0"] = pair_units(L["ffn_in"][0], between=sums)
        L["rb"] = [ring.add("rb_out") for _ in range(2)]
        L["u0f"] = pair_units(L["ffn_in"][1])
        first = len(ring.units)
        L["body_slots"] = n = [slots.load() for _ in range(6)]
        L["body"] = [(pair_units(n[3 * s]), down_units(n[3 * s + 1]), pair_units(n[3 * s + 2]))
                     for s in range(2)]
        size, per = L["body_size"], L["body_per"] = ring.repeat(first, BODIES)
        for j in range(6 * (BODIES - 1)):
            m = slots.load()
            slots.used(m, ring.units[slots.last[m - 6].n + size])
        L["last_u"] = [ring.units[u[0].n + size * (BODIES - 1)] for u in L["body"][1][2]]
        L["last_slot"] = slots.load()
        L["last"] = down_units(L["last_slot"])
        plan.append(L)
    y = [[ring.add("y_dve"), ring.add("y_act")] for _ in range(NT)]
    return ring, slots, gains, xt, plan, y


def trunk(nc, a, out):
    ring, slots, gains_unit, xt_units, plan, y_units = build_plan()
    sems = ExitStack()
    with sems:
        place_at = {}

        def place(name, shape, dtype, at):
            size = 4 * int(np.prod(shape[1:]))
            place_at[name] = (at, at + size)
            assert at % 32 == 0 and at + size <= nc.sbuf_top, (name, at, size)
            return nc.alloc_sbuf_tensor_at(name, shape, dtype, offset=at)

        at = -(-nc.sbuf_base // 32) * 32
        xT = place("xT", [P, KT, TOK], F32, at)
        at += 4 * KT * TOK
        r0 = at
        hs_hi = place("hs_hi", [P, KT, TOK], F32R, at)
        at += 4 * KT * TOK
        hs_lo = place("hs_lo", [P, KT, TOK], F32R, at)
        at += 4 * KT * TOK
        act_hi = place("act_hi", [P, 2, TOK], F32R, at)
        at += 8 * TOK
        act_lo = place("act_lo", [P, 2, TOK], F32R, at)
        at += 8 * TOK
        gate = place("gate", [P, 2, TOK], F32, at)
        at += 8 * TOK
        hid = place("hid", [P, 2, TOK], F32, at)
        at += 8 * TOK
        kT_s = place("kT_s", [QK, HEADS, S_KEYS], F32, r0)
        v_s = place("v_s", [P, CACHE_TILES + 1, WIDTH], F32, r0 + 4 * HEADS * S_KEYS)
        qT_s = place("qT_s", [QK, HEADS, DEC], F32, at - 4 * HEADS * DEC)
        assert r0 + 4 * HEADS * S_KEYS + 4 * (CACHE_TILES + 1) * WIDTH <= at - 4 * HEADS * DEC
        kT_p = place("kT_p", [QK, HEADS, SEQ], F32, r0)
        v_p = place("v_p", [P, PT_, WIDTH], F32, r0 + 4 * HEADS * SEQ)
        qT_p = place("qT_p", [QK, HEADS, SEQ], F32, r0 + 4 * HEADS * SEQ + 4 * PT_ * WIDTH)
        raw = place("raw", [P, 2, BLOCK], F32, at)
        at += 8 * BLOCK
        w_hi = place("w_hi", [P, 2, BLOCK], F32R, at)
        at += 8 * BLOCK
        w_lo = place("w_lo", [P, 2, BLOCK], F32R, at)
        at += 8 * BLOCK
        qlatT = place("qlatT", [P, 2, TOK], F32, at)
        sumsq = place("sumsq", [P, TOK], F32, at)
        rb = place("rb", [P, TOK], F32, at + 4 * TOK)
        at += 8 * TOK
        ug = place("ug", [P, NT, WIDTH], F32, at)
        x_tm = place("x_tm", [P, NT, D_MODEL], F32, at)
        at += 4 * NT * WIDTH
        gv = place("gv", [P, NT, WIDTH], F32, at)
        o_tm = place("o_tm", [P, PT_ * WIDTH + HEAD_PAIRS * VDIM], F32, at)
        o_s = o_tm[:, PT_ * WIDTH:].rearrange("p (m d) -> p m d", d=VDIM)
        at += 4 * NT * WIDTH
        ckv_n = place("ckv_n", [P, NT, KV_LORA], F32, at)
        at += 4 * NT * KV_LORA
        kr_n = place("kr_n", [P, NT, ROPE], F32, at)
        at += 4 * NT * ROPE
        ckvT = place("ckvT", [P, ALL_KEYS], F32, at)
        at += 4 * ALL_KEYS
        wsT = place("wsT", [P, GROUPS, P], F32, at)
        at += 4 * GROUPS * P
        wsT_s = place("wsT_s", [P, GROUPS, DEC], F32, at)
        at += 4 * GROUPS * DEC
        tm = place("tm", [P, 4, HEADS, QK], F32, at)
        wide = place("wide", [P, 5 * WIDTH], F32, at)
        at += 16 * HEADS * QK
        sq = place("sq", [P, 2, HEADS, QK], F32, at)
        at += 8 * HEADS * QK
        wide_g = place("wide_g", [P, NT * WIDTH], F32, at - 24 * HEADS * QK)
        wide_o = place("wide_o", [P, 2, WIDTH], F32, at - 24 * HEADS * QK + 4 * NT * WIDTH)
        p_sb = place("p_sb", [P, 2, S_KEYS], F32, at)
        ws_in = place("ws_in", [P, GROUPS, P], F32, at)
        cache_in = place("cache_in", [P, CACHE_TILES, KV_LORA], F32, at + 4 * GROUPS * P)
        at += 8 * S_KEYS
        pT = place("pT", [P, 2, CACHE_TILES + 1, P], F32, at)
        kvz = place("kvz", [P, NT, KV_KR], F32, at)
        kvsq = place("kvsq", [P, NT, KV_KR], F32, at + 4 * NT * KV_KR)
        ms_sb = place("ms_sb", [P, KT, DEC], F32, at)
        at += 8 * (CACHE_TILES + 1) * P
        cache_kr = place("cache_kr", [P, CACHE_TILES, ROPE], F32, at)
        at += 4 * CACHE_TILES * ROPE
        ln_gb = place("ln_gb", [P, 2, WIDTH], F32, at)
        at += 8 * WIDTH
        g_tm = place("g_tm", [P, KV_LORA + 2 * ROPE], F32, at)
        at += 4 * (KV_LORA + 2 * ROPE)
        trig = place("trig", [P, NT, ROPE], F32, at)
        at += 4 * NT * ROPE
        trig_q = place("trig_q", [P, NT, 2, ROPE], F32, at)
        at += 8 * NT * ROPE
        rot = place("rot", [P, HEADS, ROPE], F32, at)
        at += 4 * HEADS * ROPE
        gT = place("gT", [P, G_ROWS], F32, at)
        at += 4 * G_ROWS
        gq = place("gq", [P, 8], F32, at)
        at += 32
        ident = place("ident", [P, P], F32, at)
        g_in = place("g_in", [P, P], F32, at + 512)
        at += 1024
        ones = place("ones", [P, 8], F32, at)
        at += 32
        mhalf = place("mhalf", [P, 64], F32, at)
        at += 256
        ms = place("ms", [P, 176], F32, at)
        at += 704
        rs = place("rs", [P, 176], F32, at)
        at += 704
        mu = place("mu", [P, 64], F32, at)
        at += 256
        r_tok = place("r_tok", [P, 8], F32, at)
        at += 32
        r_q = place("r_q", [P, 8], F32, at)
        at += 32
        mx = place("mx", [P, 8], F32, at)
        at += 32
        nm = place("nm", [P, 2, 8], F32, at)
        at += 64
        lsum = place("lsum", [P, 4, 8], F32, at)
        at += 128
        linv = place("linv", [P, 2, 8], F32, at)
        at += 64

        ps = sems.enter_context(nc.psum_tensor("ps", [P, 8, 512], F32))

        S = {}

        def sem(name):
            S[name] = sems.enter_context(nc.semaphore(name))
            return S[name]

        full = sem("full")
        for name in ring.values:
            sem(name)
        g_zeroed, ident_ready, const_ready = sem("g_zeroed"), sem("ident_ready"), sem("const_ready")
        gains_loaded, trig_loaded = sem("gains_loaded"), sem("trig_loaded")
        x_loaded = [sem(f"x_loaded{t}") for t in range(NT)]
        raw_loaded = [sem(f"raw_loaded{s}") for s in range(2)]
        layer_loaded = sem("layer_loaded")
        hi_split, lo_split = sem("hi_split"), sem("lo_split")
        gq_ready = sem("gq_ready")
        hs_hi_done, hs_lo_done = sem("hs_hi_done"), sem("hs_lo_done")
        squared, summed = sem("squared"), sem("summed")
        ms_ready, rs_ready = sem("ms_ready"), sem("rs_ready")
        r_ready, rq_ready = sem("r_ready"), sem("rq_ready")
        ckv_normed, kr_turned = sem("ckv_normed"), sem("kr_turned")
        v_centred, v_squared, vn_done = sem("v_centred"), sem("v_squared"), sem("vn_done")
        sq_free, tile_normed, kr_spread = sem("sq_free"), sem("tile_normed"), sem("kr_spread")
        nm_ready, wsT_masked = sem("nm_ready"), sem("wsT_masked")
        gm_squared, gm_normed = sem("gm_squared"), sem("gm_normed")
        o_squared, o_normed = sem("o_squared"), sem("o_normed")
        m_hi, m_lo = sem("m_hi"), sem("m_lo")
        silu_done, gate_done = sem("silu_done"), sem("gate_done")
        act_hi_done, act_lo_done = sem("act_hi_done"), sem("act_lo_done")
        dve_chain, pool_chain = sem("dve_chain"), sem("pool_chain")
        rows_stored, v_stored, y_stored = sem("rows_stored"), sem("v_stored"), sem("y_stored")

        def bank(u, rows=slice(0, P), cols=512):
            return ps[rows, u.bank, 0:cols]

        def halves(t):
            return t.rearrange("p (h c) -> p h c", h=2)

        def in_cols(l, c0, c1):
            return a["w_in"][l][:, c0:c1].rearrange("(k p) n -> p k n", p=P)

        w_in_cols = [(0, Q_LORA), (Q_LORA, Q_LORA + KV_KR)]
        for c in (Q_LORA + KV_KR + WIDTH, Q_LORA + KV_KR):
            w_in_cols += [(c, c + COLS), (c + COLS, c + 2 * COLS)]

        raw_of = [n for n, k in enumerate(slots.raw) if k is not None]

        def part_cols(g):
            return slice(128 + HEADS * g, 128 + HEADS * g + O_PARTS[g][1])

        def prep_cols(t):
            c = 64 + 16 * (t["seq"] % 4)
            return slice(c, c + HEADS), slice(c + HEADS, c + 2 * HEADS)

        def emptied(eng, u):
            eng.wait_ge(S[u.freed[0]], u.freed[1])

        def filled(eng, u):
            eng.wait_ge(full, u.done)

        block = sems.enter_context(nc.Block())

        @block.sync
        def _(sp):
            def load(n, dst, src):
                if n >= 2:
                    k = slots.raw[n - 2]
                    if k is None:
                        filled(sp, slots.last[n - 2])
                    else:
                        sp.wait_ge(lo_split, k + 1)
                sp.dma_start(dst, src).then_inc(raw_loaded[n % 2], 16)

            def by_k(n, cols):
                return raw[:, n % 2, 0:KT * cols].rearrange("p (k n) -> p k n", k=KT)

            def by_f(n):
                return raw[:, n % 2, :].rearrange("p (f n) -> p f n", f=2)

            def small(l):
                if l:
                    sp.wait_ge(m_lo, l)
                loads = [(ws_in[:, :, :], a["gm_w_s"][l].rearrange("g i j -> i g j")),
                         (cache_in[:, :, :], a["cache_ckv"][l, 0].rearrange("(j p) c -> p j c", p=P)),
                         (cache_kr[:, :, :], a["cache_krope"][l, 0].rearrange("(j p) c -> p j c", p=P)),
                         (ln_gb[:, 0, :], a["gm_ln_g"][l].rearrange("g d -> (g d)").partition_broadcast(P)),
                         (ln_gb[:, 1, :], a["gm_ln_b"][l].rearrange("g d -> (g d)").partition_broadcast(P))]
                c = 0
                for name, n in (("g_kv_lora", KV_LORA), ("g_kr", ROPE), ("g_qr", ROPE)):
                    loads.append((g_tm[:, c:c + n], a[name][l].partition_broadcast(P)))
                    c += n
                assert len(loads) == SMALL
                for dst, src in loads:
                    sp.dma_start(dst, src).then_inc(layer_loaded, 16)

            for t, c in enumerate(TILE_AT[:PT_]):
                sp.dma_start(x_tm[:, t, :], a["x_prompt"][0, c:c + P, :]).then_inc(x_loaded[t], 16)
            sp.dma_start(x_tm[DEC:P, PT_, :], a["x_sample"][0]).then_inc(x_loaded[PT_], 16)
            for l, L in enumerate(plan):
                for n, (c0, c1) in zip(L["w_in"], w_in_cols):
                    load(n, by_k(n, c1 - c0), in_cols(l, c0, c1))
                    if l == 0 and n == L["w_in"][1]:
                        small(0)
                n = L["wq"]
                load(n, raw[:, n % 2, 0:2 * HEADS * QK].rearrange("p (m n) -> p m n", m=2),
                     a["w_q_up"][l].rearrange("(m p) n -> p m n", p=P))
                n = L["wkv"]
                load(n, raw[:, n % 2, 0:2 * WIDTH], a["w_kv_up"][l])
                for j, n in enumerate(L["w_o"]):
                    load(n, by_k(n, COLS), a["w_o"][l][:, j * COLS:(j + 1) * COLS].rearrange("(k p) n -> p k n", p=P))
                gate_src = a["w_gate"][l].rearrange("(k p) (g n) -> g p k n", p=P, n=COLS)
                up_src = a["w_up"][l].rearrange("(k p) (g n) -> g p k n", p=P, n=COLS)
                down_src = a["w_down"][l].rearrange("(g f p) n -> g p f n", p=P, f=2)
                for n, src in zip(L["ffn_in"], (gate_src, up_src)):
                    load(n, by_k(n, COLS), src[0])
                if l + 1 < DEPTH:
                    small(l + 1)
                n0 = L["body_slots"][0]
                with sp.Fori(0, BODIES) as b:
                    for s in range(2):
                        for j, src in enumerate((gate_src, down_src, up_src)):
                            n = n0 + 3 * s + j
                            sp.wait_ge(lo_split, b * 6 + (slots.raw[n - 2] + 1))
                            sp.dma_start(by_f(n) if j == 1 else by_k(n, COLS),
                                         src[b * 2 + (s if j == 1 else s + 1)]).then_inc(raw_loaded[n % 2], 16)
                n = L["last_slot"]
                load(n, by_f(n), down_src[FPAIRS - 1])
            for t in range(NT):
                for u in y_units[t]:
                    emptied(sp, u)
                if t < PT_:
                    sp.dma_start(out["y_prompt"][0, t * P:(t + 1) * P, :], x_tm[:, t, :]).then_inc(y_stored, 16)
                else:
                    sp.dma_start(out["y_sample"][0], x_tm[0:DEC, t, :]).then_inc(y_stored, 16)
            sp.wait_ge(y_stored, 16 * NT)
            sp.wait_ge(rows_stored, 16 * 4 * DEPTH)
            sp.wait_ge(v_stored, 16 * DEPTH)

        @block.gpsimd
        def _(pool):
            chain = [0]

            def link(ins):
                chain[0] += 1
                ins.then_inc(pool_chain, 1)
                pool.wait_ge(pool_chain, chain[0])

            def w_low(n, size=BLOCK):
                k = slots.raw[n]
                pool.wait_ge(hi_split, k + 1)
                pool.tensor_tensor(w_lo[:, k % 2, 0:size], raw[:, n % 2, 0:size],
                                   w_hi[:, k % 2, 0:size].bitcast(F32), ALU.subtract).then_inc(lo_split, 1)

            def root(l, name, n, c=0):
                no = root_no(l, name)
                pool.wait_ge(ms_ready, no)
                pool.tensor_tensor(rs[:, c:c + n], ms[:, c:c + n], mhalf[:, 0:n], ALU.pow).then_inc(rs_ready, 1)

            def sum_squares(m, tiles):
                for k in tiles:
                    n = m * KT + k + 1
                    pool.wait_ge(squared, n)
                    if k:
                        pool.wait_ge(summed, n - 1)
                        ins = pool.tensor_tensor(sumsq[:, :], sumsq[:, :], gate[:, k % 2, :], ALU.add)
                    else:
                        ins = pool.tensor_copy(sumsq[:, :], gate[:, 0, :])
                    ins.then_inc(summed, 1)

            pool.memset(g_in[:, :], 0.0).then_inc(g_zeroed, 1)
            link(pool.memset(ident[:, :], 0.0))
            pool.affine_select(out=ident[:, :], in_=ident[:, :], compare_op=ALU.not_equal, fill=1.0, base=0,
                               pattern=[[-1, P]], channel_multiplier=1).then_inc(ident_ready, 1)
            pool.memset(ones[:, :], 1.0)
            pool.memset(ms[:, :], 1.0)
            pool.memset(mhalf[:, :], -0.5)
            pool.memset(gq[:, :], 1.0).then_inc(const_ready, 1)
            pool.wait_ge(const_ready, 1)
            for l, L in enumerate(plan):
                w_low(L["w_in"][0])
                sum_squares(2 * l, range(KT))
                w_low(L["w_in"][1], KT * KV_KR)
                root(l, "r1", NT)
                w_low(L["w_in"][2])
                root(l, "kv", 2 * NT)
                pool.wait_ge(ckv_normed, l + 1)
                if l == 0:
                    pool.wait_ge(trig_loaded, 16 * NT)
                h = ROPE // 2
                x1, x2 = kvz[:, :, KV_LORA:KV_LORA + h], kvz[:, :, KV_LORA + h:KV_KR]
                c, s = trig[:, :, 0:h], trig[:, :, h:ROPE]
                t1, t2 = kvsq[:, :, 0:h], kvsq[:, :, h:2 * h]
                link(pool.tensor_tensor(t1, x1, c, ALU.mult))
                link(pool.tensor_tensor(t2, x2, s, ALU.mult))
                link(pool.tensor_tensor(kr_n[:, :, 0:h], t1, t2, ALU.subtract))
                link(pool.tensor_tensor(t1, x1, s, ALU.mult))
                link(pool.tensor_tensor(t2, x2, c, ALU.mult))
                pool.tensor_tensor(kr_n[:, :, h:ROPE], t1, t2, ALU.add).then_inc(kr_turned, 1)
                w_low(L["w_in"][3])
                root(l, "q", NT)
                w_low(L["w_in"][4])
                w_low(L["w_in"][5])
                root(l, "ln", NT * GROUPS)
                pool.wait_ge(layer_loaded, 16 * SMALL * (l + 1))

                def prep(t):
                    seq, tile = t["seq"], t["tile"]
                    nope, rope = prep_cols(t)
                    if t["what"] == "q":
                        root(l, f"b{seq}", 2 * HEADS, nope.start)
                        return
                    if tile != CACHE_TILES:
                        if seq >= 4:
                            filled(pool, L["preps"][seq - 4]["turn"][1])
                        src = cache_kr[:, tile, :] if tile < CACHE_TILES else kr_n[:, tile - CACHE_TILES - 1, :]
                        pool.tensor_copy(tm[:, seq % 4, :, NOPE:QK],
                                         src.unsqueeze(1).to_broadcast([P, HEADS, ROPE])).then_inc(kr_spread, 1)
                    root(l, f"b{seq}", HEADS, nope.start)

                for t in L["s_preps"]:
                    prep(t)
                for t in L["p_preps"]:
                    prep(t)

                def part(g):
                    c = part_cols(g)
                    root(l, f"o{g}", c.stop - c.start, c.start)

                part(0)
                n = NT * GROUPS
                root(l, "gm", n)
                pool.wait_ge(rs_ready, root_no(l, "gm"))
                ugg = ug[:, :, :].rearrange("p t (g d) -> p (t g) d", d=GDIM)
                pool.tensor_tensor(ugg, ugg, rs[:, 0:n].unsqueeze(2).to_broadcast([P, n, GDIM]), ALU.mult
                                   ).then_inc(gm_normed, 1)
                part(1)
                w_low(L["w_o"][0])
                part(2)
                w_low(L["w_o"][1])
                part(3)
                part(4)
                for j, n in enumerate(L["w_o"][2:] + L["ffn_in"][:1]):
                    sum_squares(2 * l + 1, range(2 * j, 2 * j + 2))
                    w_low(n)
                sum_squares(2 * l + 1, range(6, KT))
                root(l, "r2", NT)
                w_low(L["ffn_in"][1])

                def scale_gate(no, f):
                    pool.wait_ge(silu_done, no)
                    pool.tensor_tensor(gate[:, f, :], gate[:, f, :], rb[:, :], ALU.mult).then_inc(gate_done, 1)

                pairs = 2 * FPAIRS * l
                for f in range(2):
                    scale_gate(pairs + f + 1, f)
                n0 = L["body_slots"][0]
                with pool.Fori(0, BODIES) as i:
                    for s in range(2):
                        for j in range(3):
                            n = n0 + 3 * s + j
                            k = slots.raw[n]
                            pool.wait_ge(hi_split, i * 6 + (k + 1))
                            pool.tensor_tensor(w_lo[:, k % 2, :], raw[:, n % 2, :], w_hi[:, k % 2, :].bitcast(F32),
                                               ALU.subtract).then_inc(lo_split, 1)
                            if j == 1:
                                for f in range(2):
                                    scale_gate(i * 4 + (pairs + 3 + 2 * s + f), f)
                w_low(L["last_slot"])

        @block.scalar
        def _(act):
            def w_high(n, size=BLOCK):
                k = slots.raw[n]
                act.wait_ge(raw_loaded[n % 2], 16 * (n // 2 + 1))
                if k >= 2:
                    filled(act, slots.last[raw_of[k - 2]])
                act.activation(w_hi[:, k % 2, 0:size], raw[:, n % 2, 0:size], ACT.Copy).then_inc(hi_split, 1)

            act.wait_ge(g_zeroed, 1)
            loads = [(row, slice(0, P), a[name].rearrange("l (k p) -> (l k) p", p=P))
                     for row, name in ((G_MIX, "g_mix"), (G_FFN, "g_ffn"), (G_QL, "g_q_lora"))]
            loads.append((G_BS, slice(0, P), a["gm_b_s"].rearrange("l g i -> (l g) i")))
            loads.append((G_BS_S, slice(DEC, P), a["gm_b_s"][:, :, 0:DEC].rearrange("l g i -> (l g) i")))
            for l in range(DEPTH):
                for j, name in enumerate(("g_out_att", "g_out_gm")):
                    loads.append((G_OUT + 8 * l + 4 * j, slice(0, P), a[name][l].rearrange("(k e) d -> k (e d)", e=2)))
            loads += [(G_QN, slice(0, NOPE), a["g_qn"]), (G_KN, slice(0, NOPE), a["g_kn"])]
            assert len(loads) == GAIN_LOADS
            for row, cols, src in loads:
                act.dma_start(g_in[row:row + src.shape[0], cols], src).then_inc(gains_loaded, 16)
            for t, c in enumerate(TILE_AT):
                act.dma_start(trig[:, t, :], a["trig"][c:c + P, :]).then_inc(trig_loaded, 16)
            for t in range(NT):
                u = xt_units[t][1]
                filled(act, u)
                w = P if t < PT_ else DEC
                act.activation(xT[:, 4:8, t * P:t * P + w], bank(u).rearrange("p (k c) -> p k c", k=4)[:, :, 0:w],
                               ACT.Copy).then_inc(S["x_turned_act"], 1)

            def high_part(k, gcol):
                act.activation(hs_hi[:, k, :], xT[:, k, :], ACT.Copy, scale=gT[:, gcol + k:gcol + k + 1]
                               ).then_inc(hs_hi_done, 1)

            def square(m, k):
                if k >= 2:
                    act.wait_ge(summed, m * KT + k - 1)
                act.activation(gate[:, k % 2, :], xT[:, k, :], ACT.Square).then_inc(squared, 1)

            for l, L in enumerate(plan):
                w_high(L["w_in"][0])
                if l == 0:
                    emptied(act, gains_unit)
                    emptied(act, xt_units[-1][0])
                    emptied(act, xt_units[-1][1])
                for k in range(KT):
                    if l:
                        emptied(act, plan[l - 1]["last"][k][0])
                    high_part(k, G_MIX + KT * l)
                    square(2 * l, k)
                w_high(L["w_in"][1], KT * KV_KR)
                def prep_first(t):
                    seq, tile = t["seq"], t["tile"]
                    if seq >= 2 or l:
                        act.wait_ge(sq_free, PREPS * l + seq - 1)
                    if seq >= 4:
                        filled(act, L["preps"][seq - 4]["turn"][1])
                    elif seq == 0:
                        act.wait_ge(ms_ready, root_no(l, "ln"))
                    if t["what"] == "q":
                        if seq == 0:
                            act.wait_ge(rq_ready, l + 1)
                        elif L["preps"][seq - 2]["what"] == "q":
                            act.wait_ge(tile_normed, PREPS * l + seq - 1)
                        for e, u in enumerate(t["up"]):
                            filled(act, u)
                            src = bank(u, cols=4 * QK).rearrange("p (h c) -> p h c", c=QK)
                            act.activation(sq[:, seq % 2, 4 * e:4 * e + 4, :], src, ACT.Square,
                                           scale=r_q[:, tile:tile + 1])
                            act.activation(tm[:, seq % 4, 4 * e:4 * e + 4, :], src, ACT.Copy,
                                           scale=r_q[:, tile:tile + 1]).then_inc(S["qz_out"], 1)
                        return
                    uk, uv = t["up"]
                    rows = slice(0, key_tile(tile)[1])
                    src = bank(uk, rows).rearrange("p (h c) -> p h c", c=NOPE)
                    filled(act, uk)
                    act.activation(sq[rows, seq % 2, :, 0:NOPE], src, ACT.Square)
                    act.activation(tm[rows, seq % 4, :, 0:NOPE], src, ACT.Copy).then_inc(S["k_out"], 1)
                    filled(act, uv)
                    dst = v_s[rows, tile, :] if tile <= CACHE_TILES else v_p[:, tile - CACHE_TILES - 1, :]
                    act.activation(dst, bank(uv, rows), ACT.Copy).then_inc(S["v_out"], 1)

                def prep_turned(t):
                    tile, u = t["tile"], t["turn"][1]
                    filled(act, u)
                    src = ps[0:QK, u.bank, :].rearrange("p (h c) -> p h c", h=4)
                    if t["what"] == "q":
                        act.wait_ge(gq_ready, 2)
                        scale = gq[0:QK, l:l + 1]
                        if tile == PT_:
                            dst, src = qT_s[:, 4:8, :], src[:, :, DEC:P]
                        else:
                            dst = qT_p[:, 4:8, tile * P:(tile + 1) * P]
                    else:
                        scale = 1.0
                        c, w = key_tile(tile)
                        src = src[:, :, 0:w]
                        dst = kT_s[:, 4:8, c:c + w] if tile <= CACHE_TILES else kT_p[:, 4:8, c - S_KEYS:c - S_KEYS + w]
                    act.activation(dst, src, ACT.Copy, scale=scale).then_inc(S["qkt_act"], 1)

                def preps_run(todo, steps):
                    for n in steps:
                        if n < len(todo):
                            prep_first(todo[n])
                        if n >= 2:
                            prep_turned(todo[n - 2])

                act.wait_ge(summed, (2 * l + 1) * KT)
                filled(act, L["ss1"])
                for m in range(2):
                    for h in range(2):
                        u = L["q"][m][h]
                        filled(act, u)
                        cols = slice(h * HALF, (h + 1) * HALF)
                        act.activation(gate[:, m, cols], bank(u, cols=HALF), ACT.Square)
                        act.activation(qlatT[:, m, cols], bank(u, cols=HALF), ACT.Copy,
                                       scale=gT[:, G_QL + 2 * l + m:G_QL + 2 * l + m + 1]).then_inc(S["qlat_out"], 1)
                w_high(L["w_in"][2])
                w_high(L["w_in"][3])
                act.wait_ge(r_ready, 2 * l + 1)
                for j, (name, dst) in enumerate((("v0", gv), ("v1", gv), ("u0", ug), ("u1", ug))):
                    if j == 3:
                        act.wait_ge(v_centred, l + 1)
                        act.activation(wide[:, :], gv[:, :, :].rearrange("p t c -> p (t c)"), ACT.Square
                                       ).then_inc(v_squared, 1)
                        preps_run(L["s_preps"], [0])
                    for t in range(NT):
                        u = L[name][t]
                        filled(act, u)
                        act.activation(dst[:, t, (j % 2) * COLS:(j % 2 + 1) * COLS], bank(u, cols=COLS),
                                       ACT.Gelu_apprx_tanh, scale=r_tok[:, t:t + 1]).then_inc(S["gelu_out"], 1)
                    if j < 2:
                        w_high(L["w_in"][4 + j])
                    if j == 1:
                        filled(act, L["ct"][1])
                        act.activation(ckvT[:, PAST:S_KEYS], ps[:, L["ct"][1].bank, DEC:P], ACT.Copy
                                       ).then_inc(S["ckvt_act"], 1)
                        filled(act, L["ct"][3])
                        act.activation(ckvT[:, PAST // 2:PAST], bank(L["ct"][3]), ACT.Copy).then_inc(S["ckvt_act"], 1)
                act.wait_ge(ckv_normed, l + 1)
                act.dma_start(out["ckv_prompt"][l, 0].rearrange("(t p) c -> p t c", p=P), ckv_n[:, 0:PT_, :]
                              ).then_inc(rows_stored, 16)
                act.dma_start(out["ckv_sample"][l, 0], ckv_n[DEC:P, PT_, :]).then_inc(rows_stored, 16)
                act.wait_ge(kr_turned, l + 1)
                act.dma_start(out["krope_prompt"][l, 0].rearrange("(t p) c -> p t c", p=P), kr_n[:, 0:PT_, :]
                              ).then_inc(rows_stored, 16)
                act.dma_start(out["krope_sample"][l, 0], kr_n[DEC:P, PT_, :]).then_inc(rows_stored, 16)

                preps_run(L["s_preps"], range(1, len(S_TILES) + 2))
                act.wait_ge(vn_done, l + 1)
                act.dma_start(out["gmlp_v_sample"][l, 0], gv[DEC:P, PT_, :]).then_inc(v_stored, 16)

                def sample_pt(n):
                    u = L["s_steps"][n]["t"][1]
                    filled(act, u)
                    if n >= 2:
                        filled(act, L["s_steps"][n - 2]["o"])
                    act.activation(pT[:, n % 2, 4:8, :], bank(u).rearrange("p (j c) -> p j c", j=4),
                                   ACT.Copy).then_inc(S["pt_act"], 1)

                for n, st in enumerate(L["s_steps"]):
                    act.wait_ge(nm_ready, STEPS * l + n + 1)
                    if n >= 2:
                        filled(act, L["s_steps"][n - 2]["t"][-1])
                    for e, ((c, w), u) in enumerate(zip(S_SPANS, st["s"])):
                        act.activation(p_sb[:, n % 2, c:c + w], bank(u, cols=w), ACT.Exp, bias=nm[:, n % 2, 0:1],
                                       scale=SCALE, accum_out=lsum[:, n % 4, e:e + 1]).then_inc(S["s_exp"], 1)
                    if n >= 1:
                        sample_pt(n - 1)
                preps_run(L["p_preps"], [0])
                sample_pt(HEAD_PAIRS - 1)
                preps_run(L["p_preps"], range(1, len(P_TILES) + 2))
                w_high(L["w_o"][0])
                w_high(L["w_o"][1])
                filled(act, L["p_preps"][-1]["turn"][1])
                act.wait_ge(tile_normed, PREPS * (l + 1))
                emptied(act, L["mix"][-1])
                act.activation(wide_g[:, :], ug[:, :, :].rearrange("p t c -> p (t c)"), ACT.Square).then_inc(gm_squared, 1)

                def part_square(g):
                    if g == 0:
                        emptied(act, L["s_steps"][-1]["o"])
                    else:
                        last = max(m for m, step in enumerate(P_STEPS) if step[0] == g - 1)
                        emptied(act, L["p_steps"][last]["o"])
                    if g >= 2:
                        act.wait_ge(ms_ready, root_no(l, f"o{g - 2}"))
                    c, n = O_PARTS[g]
                    act.activation(wide_o[:, g % 2, 0:n * VDIM], o_tm[:, c:c + n * VDIM], ACT.Square
                                   ).then_inc(o_squared, 1)

                def prompt_pt(m):
                    if m % 2:
                        return
                    i, _, nh = P_STEPS[m]
                    u = L["p_steps"][m]["t"]
                    filled(act, u)
                    if m >= 2:
                        filled(act, L["p_steps"][m - 2]["o"])
                    w = nh * (i + 1)
                    act.activation(pT[:, 0, 0:w, :], bank(u, cols=w * P).rearrange("p (j c) -> p j c", j=w),
                                   ACT.Copy).then_inc(S["pt_act"], 1)

                for m, (i, _, nh) in enumerate(P_STEPS):
                    st = L["p_steps"][m]
                    act.wait_ge(nm_ready, STEPS * l + HEAD_PAIRS + m + 1)
                    if m >= 2:
                        filled(act, L["p_steps"][m - 2]["t"])
                    w = (i + 1) * P
                    for e in range(nh):
                        ins = act.activation(p_sb[:, m % 2, e * w:(e + 1) * w], ps[:, st["s"].bank, e * w:(e + 1) * w],
                                             ACT.Exp, bias=nm[:, m % 2, e:e + 1], scale=SCALE,
                                             accum_out=lsum[:, m % 4, e:e + 1])
                    ins.then_inc(S["s_exp"], 1)
                    if m >= 1:
                        prompt_pt(m - 1)
                    if m in O_SQUARED:
                        part_square(O_SQUARED.index(m))
                prompt_pt(len(P_STEPS) - 1)
                part_square(PT_)
                for k in MERGED:
                    if k == KT:
                        emptied(act, L["mt"][KT])
                        act.activation(hs_hi[:, :, SEQ:TOK], ms_sb[:, :, :], ACT.Copy).then_inc(m_hi, 1)
                        continue
                    u = L["mt"][k]
                    filled(act, u)
                    g = G_OUT + 8 * l + k
                    act.activation(hs_hi[:, k, 0:SEQ], bank(u), ACT.Copy, scale=gT[:, g:g + 1]).then_inc(m_hi, 1)
                for k in range(KT):
                    if k in (2, 4, 6):
                        w_high((L["w_o"][2:] + L["ffn_in"][:1])[k // 2 - 1])
                    emptied(act, L["wo"][k][0])
                    square(2 * l + 1, k)
                filled(act, L["wo"][-1][1])
                for k in range(KT):
                    high_part(k, G_FFN + KT * l)
                w_high(L["ffn_in"][1])

                def silu(f, no):
                    act.wait_ge(S["ffn_out"], no)
                    act.activation(gate[:, f, :], gate[:, f, :], ACT.Silu).then_inc(silu_done, 1)

                def hidden_high(f, no):
                    act.wait_ge(S["ffn_out"], no)
                    act.activation(act_hi[:, f, :], hid[:, f, :], ACT.Copy).then_inc(act_hi_done, 1)

                for f in range(2):
                    silu(f, L["g0"][f][0].freed[1])
                n0 = L["body_slots"][0]
                size, per = L["body_size"], L["body_per"]
                with act.Fori(0, BODIES) as i:
                    def high(n):
                        k = slots.raw[n]
                        act.wait_ge(raw_loaded[n % 2], i * 48 + 16 * (n // 2 + 1))
                        act.wait_ge(full, i * size + (slots.last[raw_of[k - 2] + 6].done - size))
                        act.activation(w_hi[:, k % 2, :], raw[:, n % 2, :], ACT.Copy).then_inc(hi_split, 1)

                    for s in range(2):
                        before = L["u0f"] if s == 0 else L["body"][0][2]
                        high(n0 + 3 * s)
                        for f in range(2):
                            hidden_high(f, i * per + before[f][0].freed[1])
                        high(n0 + 3 * s + 1)
                        for f in range(2):
                            silu(f, i * per + L["body"][s][0][f][0].freed[1])
                        high(n0 + 3 * s + 2)
                w_high(L["last_slot"])
                for f in range(2):
                    hidden_high(f, L["last_u"][f].freed[1])
            for t in range(NT):
                u = y_units[t][1]
                rows = slice(0, P if t < PT_ else DEC)
                filled(act, u)
                act.activation(x_tm[rows, t, WIDTH:2 * WIDTH], bank(u, rows), ACT.Copy).then_inc(S["y_act"], 1)

        @block.vector
        def _(dve):
            chain = [0]

            def link(ins):
                chain[0] += 1
                ins.then_inc(dve_chain, 1)
                dve.wait_ge(dve_chain, chain[0])

            def root(l, name, n, rows, scale, ins_in=None):
                src = ms[rows, 0:n] if ins_in is None else ins_in
                dve.tensor_scalar(ms[rows, 0:n], src, scale, EPS, ALU.mult, ALU.add).then_inc(ms_ready, 1)
                dve.wait_ge(rs_ready, root_no(l, name))

            def low(dst, src, gain, hi):
                return dve.scalar_tensor_tensor(out=dst, in0=src, scalar=gain, in1=hi.bitcast(F32), op0=ALU.mult,
                                                op1=ALU.subtract)

            ALL = slice(0, P)
            filled(dve, gains_unit)
            dve.tensor_copy(gT[:, :], bank(gains_unit, cols=G_ROWS)).then_inc(S["gains_turned"], 1)
            emptied(dve, gains_unit)
            dve.wait_ge(const_ready, 1)
            dve.tensor_tensor(gq[0:NOPE, 0:DEPTH], gT[0:NOPE, G_QN:G_QN + DEPTH], gT[0:NOPE, G_KN:G_KN + DEPTH],
                              ALU.mult).then_inc(gq_ready, 2)
            for t in range(NT):
                u = xt_units[t][0]
                filled(dve, u)
                w = P if t < PT_ else DEC
                dve.tensor_copy(xT[:, 0:4, t * P:t * P + w], bank(u).rearrange("p (k c) -> p k c", k=4)[:, :, 0:w]
                                ).then_inc(S["x_turned_dve"], 1)

            def low_part(m, k, gcol):
                dve.wait_ge(hs_hi_done, m * KT + k + 1)
                low(hs_lo[:, k, :], xT[:, k, :], gT[:, gcol + k:gcol + k + 1], hs_hi[:, k, :]).then_inc(hs_lo_done, 1)

            def r_by_token(l, name, u, no):
                filled(dve, u)
                dve.tensor_scalar(ms[:, 0:NT], bank(u, cols=NT), 1.0 / D_MODEL, EPS, ALU.mult, ALU.add
                                  ).then_inc(S["sumsq_out"], 1)
                emptied(dve, u)
                dve.tensor_copy(ms[:, 0:NT], ms[:, 0:NT]).then_inc(ms_ready, 1)
                dve.wait_ge(rs_ready, root_no(l, name))
                dve.tensor_copy(r_tok[:, 0:NT], rs[:, 0:NT]).then_inc(r_ready, 1)
                dve.wait_ge(r_ready, no)

            for l, L in enumerate(plan):
                if l == 0:
                    for k in range(KT):
                        low_part(0, k, G_MIX)
                r_by_token(l, "r1", L["ss1"], 2 * l + 1)
                for t in range(NT):
                    u = L["kv"][t]
                    filled(dve, u)
                    dve.tensor_scalar(kvz[:, t, :], bank(u, cols=KV_KR), r_tok[:, t:t + 1], None, ALU.mult
                                      ).then_inc(S["kv_out"], 1)
                emptied(dve, L["kv"][-1])
                link(dve.tensor_tensor(kvsq[:, :, :], kvz[:, :, :], kvz[:, :, :], ALU.mult))
                dve.tensor_reduce(ms[:, 0:NT], kvsq[:, :, 0:KV_LORA], AX.X, ALU.add)
                link(dve.tensor_reduce(ms[:, NT:2 * NT], kvsq[:, :, KV_LORA:KV_KR], AX.X, ALU.add))
                link(dve.tensor_scalar(ms[:, 0:NT], ms[:, 0:NT], ROPE / KV_LORA, None, ALU.mult))
                root(l, "kv", 2 * NT, ALL, 1.0 / ROPE)
                link(dve.tensor_tensor(kvz[:, :, 0:KV_LORA], kvz[:, :, 0:KV_LORA],
                                       rs[:, 0:NT].unsqueeze(2).to_broadcast([P, NT, KV_LORA]), ALU.mult))
                link(dve.tensor_tensor(kvz[:, :, KV_LORA:KV_KR], kvz[:, :, KV_LORA:KV_KR],
                                       rs[:, NT:2 * NT].unsqueeze(2).to_broadcast([P, NT, ROPE]), ALU.mult))
                dve.wait_ge(layer_loaded, 16 * SMALL * (l + 1))
                if l:
                    dve.wait_ge(rows_stored, 64 * l)
                dve.tensor_tensor(ckv_n[:, :, :], kvz[:, :, 0:KV_LORA],
                                  g_tm[:, 0:KV_LORA].unsqueeze(1).to_broadcast([P, NT, KV_LORA]), ALU.mult)
                dve.tensor_tensor(kvz[:, :, KV_LORA:KV_KR], kvz[:, :, KV_LORA:KV_KR],
                                  g_tm[:, KV_LORA:KV_KR].unsqueeze(1).to_broadcast([P, NT, ROPE]), ALU.mult
                                  ).then_inc(ckv_normed, 1)
                if l == 0:
                    dve.wait_ge(trig_loaded, 16 * NT)
                h = ROPE // 2
                g = g_tm[:, KV_KR:KV_KR + ROPE]
                dve.tensor_tensor(trig_q[:, :, 0, :], trig[:, :, :], g.unsqueeze(1).to_broadcast([P, NT, ROPE]), ALU.mult)
                dve.tensor_tensor(trig_q[:, :, 1, 0:h], trig[:, :, h:ROPE], g[:, 0:h].unsqueeze(1).to_broadcast([P, NT, h]),
                                  ALU.mult)
                dve.tensor_tensor(trig_q[:, :, 1, h:ROPE], trig[:, :, 0:h],
                                  g[:, h:ROPE].unsqueeze(1).to_broadcast([P, NT, h]), ALU.mult)
                link(dve.tensor_tensor(r_q[:, 0:NT], r_tok[:, 0:NT], r_tok[:, 0:NT], ALU.mult))
                filled(dve, L["ssq"])
                dve.tensor_tensor(ms[:, 0:NT], bank(L["ssq"], cols=NT), r_q[:, 0:NT], ALU.mult).then_inc(S["sumsq_out"], 1)
                emptied(dve, L["ssq"])
                root(l, "q", NT, ALL, 1.0 / Q_LORA)
                dve.tensor_tensor(r_q[:, 0:NT], r_tok[:, 0:NT], rs[:, 0:NT], ALU.mult).then_inc(rq_ready, 1)
                filled(dve, L["ct"][0])
                dve.tensor_copy(ckvT[:, S_KEYS:ALL_KEYS], bank(L["ct"][0])).then_inc(S["ckvt_dve"], 1)
                filled(dve, L["ct"][2])
                dve.tensor_copy(ckvT[:, 0:PAST // 2], bank(L["ct"][2])).then_inc(S["ckvt_dve"], 1)
                for j in range(2):
                    filled(dve, L["wst"][j])
                    dve.tensor_copy(wsT[:, 4 * j:4 * j + 4, :], bank(L["wst"][j]).rearrange("p (g i) -> p g i", g=4)
                                    ).then_inc(S["wst_out"], 1)
                filled(dve, L["wst"][2])
                dve.tensor_copy(wsT_s[DEC:P, :, :], bank(L["wst"][2], slice(DEC, P)).rearrange("p (g i) -> p g i", g=GROUPS)
                                ).then_inc(S["wst_out"], 1)
                emptied(dve, L["wst"][1])
                dve.memset(wsT[CHUNK:P, :, 0:CHUNK], 0.0).then_inc(wsT_masked, 1)

                emptied(dve, L["v1"][-1])
                gvg = gv[:, :, :].rearrange("p t (g d) -> p (t g) d", d=GDIM)
                n = NT * GROUPS
                link(dve.tensor_reduce(mu[:, 0:n], gvg, AX.X, ALU.add))
                link(dve.tensor_scalar(mu[:, 0:n], mu[:, 0:n], 1.0 / GDIM, None, ALU.mult))
                dve.tensor_tensor(gvg, gvg, mu[:, 0:n].unsqueeze(2).to_broadcast([P, n, GDIM]), ALU.subtract
                                  ).then_inc(v_centred, 1)
                dve.wait_ge(v_squared, l + 1)
                link(dve.tensor_reduce(ms[:, 0:n], wide[:, :].rearrange("p (n d) -> p n d", d=GDIM), AX.X, ALU.add))
                root(l, "ln", n, ALL, 1.0 / GDIM)
                dve.tensor_tensor(gvg, gvg, rs[:, 0:n].unsqueeze(2).to_broadcast([P, n, GDIM]), ALU.mult)

                def prep_asked(t):
                    seq, tile = t["seq"], t["tile"]
                    nope, rope = prep_cols(t)
                    if t["what"] == "q":
                        emptied(dve, t["up"][1])
                        dve.tensor_reduce(ms[:, rope], sq[:, seq % 2, :, NOPE:QK], AX.X, ALU.add)
                        dve.tensor_reduce(ms[:, nope], sq[:, seq % 2, :, 0:NOPE], AX.X, ALU.add).then_inc(sq_free, 1)
                        dve.wait_ge(sq_free, PREPS * l + seq + 1)
                        dve.tensor_scalar(ms[:, nope], ms[:, nope], 1.0 / NOPE, EPS, ALU.mult, ALU.add)
                        dve.tensor_scalar(ms[:, rope], ms[:, rope], 1.0 / ROPE, EPS, ALU.mult, ALU.add
                                          ).then_inc(ms_ready, 1)
                        return
                    emptied(dve, t["up"][0])
                    rows = slice(0, key_tile(tile)[1])
                    dve.tensor_reduce(ms[rows, nope], sq[rows, seq % 2, :, 0:NOPE], AX.X, ALU.add).then_inc(sq_free, 1)
                    if tile == CACHE_TILES:
                        filled(dve, L["preps"][seq - 4]["turn"][1])
                        dve.wait_ge(kr_turned, l + 1)
                        dve.tensor_copy(tm[rows, seq % 4, :, NOPE:QK],
                                        kr_n[DEC:P, PT_:PT_ + 1, :].to_broadcast([DEC, HEADS, ROPE]))
                    dve.wait_ge(sq_free, PREPS * l + seq + 1)
                    dve.tensor_scalar(ms[rows, nope], ms[rows, nope], 1.0 / NOPE, EPS, ALU.mult, ALU.add
                                      ).then_inc(ms_ready, 1)

                def prep_normed(t):
                    seq, tile = t["seq"], t["tile"]
                    nope, rope = prep_cols(t)
                    rows = slice(0, P if t["what"] == "q" else key_tile(tile)[1])
                    x = tm[rows, seq % 4, :, :]
                    dve.wait_ge(rs_ready, root_no(l, f"b{seq}"))
                    ins = dve.tensor_tensor(x[:, :, 0:NOPE], x[:, :, 0:NOPE],
                                            rs[rows, nope].unsqueeze(2).to_broadcast([rows.stop, HEADS, NOPE]), ALU.mult)
                    if t["what"] == "q":
                        xr = x[:, :, NOPE:QK]
                        link(dve.tensor_tensor(xr, xr, rs[:, rope].unsqueeze(2).to_broadcast([P, HEADS, ROPE]), ALU.mult))
                        parts = (sq[:, seq % 2, :, NOPE:QK], rot[:, :, :])
                        for e in range(2):
                            ins = dve.tensor_tensor(parts[e], xr,
                                                    trig_q[:, tile, e, :].unsqueeze(1).to_broadcast([P, HEADS, ROPE]), ALU.mult)
                        link(ins)
                        h = ROPE // 2
                        dve.tensor_tensor(xr[:, :, 0:h], parts[0][:, :, 0:h], parts[0][:, :, h:ROPE], ALU.subtract)
                        ins = dve.tensor_tensor(xr[:, :, h:ROPE], parts[1][:, :, 0:h], parts[1][:, :, h:ROPE], ALU.add)
                    ins.then_inc(tile_normed, 1)

                def prep_turned(t):
                    tile, u = t["tile"], t["turn"][0]
                    filled(dve, u)
                    src = ps[0:QK, u.bank, :].rearrange("p (h c) -> p h c", h=4)
                    if t["what"] == "q":
                        if tile == PT_:
                            dst, src = qT_s[:, 0:4, :], src[:, :, DEC:P]
                        else:
                            dst = qT_p[:, 0:4, tile * P:(tile + 1) * P]
                        dve.tensor_scalar(dst, src, gq[0:QK, l:l + 1], None, ALU.mult).then_inc(S["qkt_dve"], 1)
                    else:
                        c, w = key_tile(tile)
                        src = src[:, :, 0:w]
                        dst = kT_s[:, 0:4, c:c + w] if tile <= CACHE_TILES else kT_p[:, 0:4, c - S_KEYS:c - S_KEYS + w]
                        dve.tensor_copy(dst, src).then_inc(S["qkt_dve"], 1)

                def preps_run(todo, steps, between=lambda n: None):
                    for n in steps:
                        if n < len(todo):
                            prep_asked(todo[n])
                        if 1 <= n <= len(todo):
                            prep_normed(todo[n - 1])
                        if n >= 2:
                            prep_turned(todo[n - 2])
                        between(n)

                def v_affine(n):
                    row = {3: 0, 6: 1}.get(n)
                    if row is None:
                        return
                    ins = dve.tensor_tensor(gv[:, :, :], gv[:, :, :], ln_gb[:, row:row + 1, :].to_broadcast([P, NT, WIDTH]),
                                            ALU.add if row else ALU.mult)
                    if row:
                        ins.then_inc(vn_done, 1)

                preps_run(L["s_preps"], range(len(S_TILES) + 2), v_affine)

                for g2 in range(4):
                    u = L["mix"][g2]
                    filled(dve, u)
                    for e in range(2):
                        g = 2 * g2 + e
                        dst = ug[:, 0:PT_, g * GDIM:(g + 1) * GDIM]
                        ins = dve.scalar_tensor_tensor(
                            out=dst, in0=ps[:, u.bank, e * 256:(e + 1) * 256].rearrange("p (t d) -> p t d", t=PT_),
                            scalar=gT[:, G_BS + GROUPS * l + g:G_BS + GROUPS * l + g + 1], in1=dst, op0=ALU.add, op1=ALU.mult)
                    ins.then_inc(S["mix_out"], 1)
                u = L["mix"][4]
                filled(dve, u)
                for g in range(GROUPS):
                    dst = ug[DEC:P, PT_, g * GDIM:(g + 1) * GDIM]
                    ins = dve.scalar_tensor_tensor(
                        out=dst, in0=ps[DEC:P, u.bank, g * GDIM:(g + 1) * GDIM],
                        scalar=gT[DEC:P, G_BS_S + GROUPS * l + g:G_BS_S + GROUPS * l + g + 1], in1=dst,
                        op0=ALU.add, op1=ALU.mult)
                ins.then_inc(S["mix_out"], 1)
                dve.wait_ge(v_stored, 16 * (l + 1))
                for n in range(HEAD_PAIRS + 2):
                    if n >= HEAD_PAIRS:
                        preps_run(L["p_preps"], [n - HEAD_PAIRS])
                    if n < HEAD_PAIRS:
                        st = L["s_steps"][n]
                        for e, ((c, w), u) in enumerate(zip(S_SPANS, st["s"])):
                            filled(dve, u)
                            ins = dve.tensor_reduce(mx[:, e:e + 1], bank(u, cols=w), AX.X, ALU.max)
                        link(ins)
                        link(dve.tensor_reduce(mx[:, 3:4], mx[:, 0:3], AX.X, ALU.max))
                        dve.tensor_scalar(nm[:, n % 2, 0:1], mx[:, 3:4], -SCALE, None, ALU.mult).then_inc(nm_ready, 1)
                    if 1 <= n <= HEAD_PAIRS:
                        m = n - 1
                        for j in (0, 2):
                            u = L["s_steps"][m]["t"][j]
                            filled(dve, u)
                            if m >= 2 and not j:
                                filled(dve, L["s_steps"][m - 2]["o"])
                            first, count = S_TRANS[j]
                            rows = slice(0, P if j < 2 else DEC)
                            dve.tensor_copy(pT[rows, m % 2, first:first + count, :],
                                            bank(u, rows, count * P).rearrange("p (j c) -> p j c", j=count)
                                            ).then_inc(S["pt_dve"], 1)
                    if n >= 2:
                        m = n - 2
                        emptied(dve, L["s_steps"][m]["s"][-1])
                        link(dve.tensor_reduce(linv[:, m % 2, 0:1], lsum[:, m % 4, 0:3], AX.X, ALU.add))
                        link(dve.reciprocal(linv[:, m % 2, 0:1], linv[:, m % 2, 0:1]))
                        u = L["s_steps"][m]["o"]
                        filled(dve, u)
                        dve.tensor_scalar(o_s[:, m, :], bank(u, cols=VDIM), linv[:, m % 2, 0:1], None, ALU.mult
                                          ).then_inc(S["o_out"], 1)
                preps_run(L["p_preps"], range(2, len(P_TILES) + 2))

                def part_asked(g):
                    c, n = part_cols(g), O_PARTS[g][1]
                    dve.wait_ge(o_squared, (PT_ + 1) * l + g + 1)
                    link(dve.tensor_reduce(ms[:, c], wide_o[:, g % 2, 0:n * VDIM].rearrange("p (n d) -> p n d", d=VDIM),
                                           AX.X, ALU.add))
                    dve.tensor_scalar(ms[:, c], ms[:, c], 1.0 / VDIM, EPS, ALU.mult, ALU.add).then_inc(ms_ready, 1)

                def part_applied(g):
                    dve.wait_ge(rs_ready, root_no(l, f"o{g}"))
                    c, n = O_PARTS[g]
                    o = o_tm[:, c:c + n * VDIM].rearrange("p (n d) -> p n d", d=VDIM)
                    dve.tensor_tensor(o, o, rs[:, part_cols(g)].unsqueeze(2).to_broadcast([P, n, VDIM]), ALU.mult
                                      ).then_inc(o_normed, 1)

                def gm_asked():
                    dve.wait_ge(gm_squared, l + 1)
                    n = NT * GROUPS
                    link(dve.tensor_reduce(ms[:, 0:n], wide_g[:, :].rearrange("p (n d) -> p n d", d=GDIM), AX.X, ALU.add))
                    dve.tensor_scalar(ms[:, 0:n], ms[:, 0:n], 1.0 / GDIM, EPS, ALU.mult, ALU.add).then_inc(ms_ready, 1)

                for n in range(len(P_STEPS) + 2):
                    if n < len(P_STEPS):
                        i, _, nh = P_STEPS[n]
                        u = L["p_steps"][n]["s"]
                        w = (i + 1) * P
                        sc = ps[:, u.bank, 0:nh * w].rearrange("p (h c) -> p h c", h=nh)
                        filled(dve, u)
                        link(dve.memset(ps[0:CHUNK, u.bank, 0:nh * w].rearrange("p (h c) -> p h c", h=nh)[:, :, w - CHUNK:w],
                                        NEG_INF))
                        link(dve.tensor_reduce(mx[:, 0:nh], sc, AX.X, ALU.max))
                        dve.tensor_scalar(nm[:, n % 2, 0:nh], mx[:, 0:nh], -SCALE, None, ALU.mult).then_inc(nm_ready, 1)
                    if 1 <= n <= len(P_STEPS) and (n - 1) % 2:
                        m = n - 1
                        i, _, nh = P_STEPS[m]
                        u = L["p_steps"][m]["t"]
                        filled(dve, u)
                        if m >= 2:
                            filled(dve, L["p_steps"][m - 2]["o"])
                        w = nh * (i + 1)
                        dve.tensor_copy(pT[:, 1, 0:w, :], bank(u, cols=w * P).rearrange("p (j c) -> p j c", j=w)
                                        ).then_inc(S["pt_dve"], 1)
                    if n >= 2:
                        m = n - 2
                        i, h0, nh = P_STEPS[m]
                        emptied(dve, L["p_steps"][m]["s"])
                        link(dve.reciprocal(linv[:, m % 2, 0:nh], lsum[:, m % 4, 0:nh]))
                        u = L["p_steps"][m]["o"]
                        filled(dve, u)
                        c = i * WIDTH + h0 * VDIM
                        dve.tensor_tensor(o_tm[:, c:c + nh * VDIM].rearrange("p (h d) -> p h d", h=nh),
                                          bank(u, cols=nh * VDIM).rearrange("p (h d) -> p h d", h=nh),
                                          linv[:, m % 2, 0:nh].unsqueeze(2).to_broadcast([P, nh, VDIM]), ALU.mult
                                          ).then_inc(S["o_out"], 1)
                    if n in O_ASKED:
                        part_asked(O_ASKED.index(n))
                    if n == GM_ASKED:
                        gm_asked()
                    if n in O_APPLIED:
                        part_applied(O_APPLIED.index(n))
                part_asked(PT_)
                part_applied(PT_)
                for j, k in enumerate(MERGED):
                    u = L["mt"][k]
                    if k == KT:
                        g = G_OUT + 8 * l
                        filled(dve, u)
                        dve.tensor_tensor(ms_sb[:, :, :], bank(u).rearrange("p (k c) -> p k c", k=KT),
                                          gT[:, g:g + KT].unsqueeze(2).to_broadcast([P, KT, DEC]), ALU.mult
                                          ).then_inc(S["merged_out"], 1)
                        dve.wait_ge(m_hi, (KT + 1) * l + j + 1)
                        dve.tensor_tensor(hs_lo[:, :, SEQ:TOK], ms_sb[:, :, :], hs_hi[:, :, SEQ:TOK].bitcast(F32),
                                          ALU.subtract).then_inc(m_lo, 1)
                        continue
                    g = G_OUT + 8 * l + k
                    dve.wait_ge(m_hi, (KT + 1) * l + j + 1)
                    low(hs_lo[:, k, 0:SEQ], bank(u), gT[:, g:g + 1], hs_hi[:, k, 0:SEQ]).then_inc(S["merged_out"], 1)

                def add_to_x(m, u):
                    x = halves(xT[:, m, :])
                    return dve.tensor_tensor(x, ps[:, u.bank:u.bank + 2, 0:HALF], x, ALU.add)

                for m in range(KT):
                    filled(dve, L["wo"][m][1])
                    add_to_x(m, L["wo"][m][0]).then_inc(S["wo_added"], 1)
                for k in range(KT):
                    low_part(2 * l + 1, k, G_FFN + KT * l)
                r_by_token(l, "r2", L["ss2"], 2 * l + 2)
                filled(dve, L["rb"][0])
                dve.tensor_copy(rb[:, 0:SEQ], bank(L["rb"][0])).then_inc(S["rb_out"], 1)
                filled(dve, L["rb"][1])
                dve.tensor_copy(rb[:, SEQ:TOK], ps[:, L["rb"][1].bank, DEC:P]).then_inc(S["rb_out"], 1)
                emptied(dve, L["rb"][1])

                def gate_in(f, u, off):
                    dve.wait_ge(full, off[0] + u[1].done)
                    dve.tensor_tensor(halves(gate[:, f, :]), ps[:, u[0].bank:u[0].bank + 2, 0:HALF], halves(rb[:, :]),
                                      ALU.mult).then_inc(S["ffn_out"], 1)

                def hidden(f, u, off, no):
                    dve.wait_ge(full, off[0] + u[1].done)
                    dve.wait_ge(gate_done, no)
                    dve.tensor_tensor(halves(hid[:, f, :]), ps[:, u[0].bank:u[0].bank + 2, 0:HALF], halves(gate[:, f, :]),
                                      ALU.mult).then_inc(S["ffn_out"], 1)
                    dve.wait_ge(act_hi_done, no)
                    dve.tensor_tensor(act_lo[:, f, :], hid[:, f, :], act_hi[:, f, :].bitcast(F32), ALU.subtract
                                      ).then_inc(act_lo_done, 1)

                def down(units, off, first=0):
                    for m, u in enumerate(units):
                        dve.wait_ge(full, off[0] + u[1].done)
                        add_to_x(first + m, u[0]).then_inc(S["ffn_out"], 1)

                pairs = 2 * FPAIRS * l
                for f in range(2):
                    gate_in(f, L["g0"][f], (0, 0))
                for f in range(2):
                    hidden(f, L["u0f"][f], (0, 0), pairs + f + 1)
                with dve.Fori(0, BODIES) as i:
                    off = (i * L["body_size"], i * L["body_per"])
                    for s in range(2):
                        g, d, u = L["body"][s]
                        for f in range(2):
                            gate_in(f, g[f], off)
                        dve.wait_ge(S["ffn_out"], off[1] + g[1][0].freed[1])
                        down(d, off)
                        for f in range(2):
                            hidden(f, u[f], off, i * 4 + (pairs + 3 + 2 * s + f))
                dve.wait_ge(S["ffn_out"], L["last_u"][1].freed[1])
                for m in range(KT + 1):
                    if m < KT:
                        down(L["last"][m:m + 1], (0, 0), m)
                    if m and l + 1 < DEPTH:
                        low_part(2 * l + 2, m - 1, G_MIX + KT * (l + 1))
            for t in range(NT):
                u = y_units[t][0]
                rows = slice(0, P if t < PT_ else DEC)
                filled(dve, u)
                dve.tensor_copy(x_tm[rows, t, 0:WIDTH], bank(u, rows)).then_inc(S["y_dve"], 1)

        @block.tensor
        def _(pe):
            def free(u):
                if u.before:
                    pe.wait_ge(S[u.before[0]], u.before[1])

            def split_ready(n):
                pe.wait_ge(lo_split, slots.raw[n] + 1)

            def turn(dst, src, n):
                return pe.transpose(dst, src, ident[0:n, 0:n])

            pe.wait_ge(ident_ready, 1)
            pe.wait_ge(gains_loaded, 16 * GAIN_LOADS)
            turn(bank(gains_unit, cols=P), g_in[:, :], P).then_inc(full, 1)
            for t in range(NT):
                pe.wait_ge(x_loaded[t], 16)
                for e, u in enumerate(xt_units[t]):
                    free(u)
                    for j in range(4):
                        c = (4 * e + j) * P
                        if t < PT_:
                            ins = turn(ps[:, u.bank, j * P:(j + 1) * P], x_tm[:, t, c:c + P], P)
                        else:
                            ins = pe.transpose(ps[:, u.bank, j * P:j * P + DEC], x_tm[DEC:P, t, c:c + P],
                                               ident[DEC:P, DEC:P])
                    ins.then_inc(full, 1)
            pe.wait_ge(const_ready, 1)

            def by_token(u, t, k_w, n, cols):
                c = TILE_AT[t]
                for k in range(KT):
                    w = slice(k * cols, (k + 1) * cols)
                    x_hi, x_lo = hs_hi[:, k, c:c + P], hs_lo[:, k, c:c + P]
                    dst = bank(u, cols=cols)
                    pe.matmul(dst, x_hi, w_hi[:, k_w, w], start=(k == 0), stop=False)
                    pe.matmul(dst, x_hi, w_lo[:, k_w, w], start=False, stop=False)
                    ins = pe.matmul(dst, x_lo, w_hi[:, k_w, w], start=False, stop=(k == KT - 1))
                return ins

            def by_feature(units, k_w, at, step, count, x_hi, x_lo, ready=None, order=None):
                order = order or range(count)
                for k in order:
                    if ready:
                        ready(k)
                    first, last = k == order[0], k == order[-1]
                    w = slice(at + k * step, at + k * step + P)
                    hi, lo = w_hi[:, k_w, w], w_lo[:, k_w, w]
                    for h, u in enumerate(units):
                        cols = slice(h * HALF, (h + 1) * HALF)
                        pe.matmul(bank(u, cols=HALF), hi, x_hi[:, k, cols], start=first, stop=False)
                        pe.matmul(bank(u, cols=HALF), hi, x_lo[:, k, cols], start=False, stop=False)
                    for h, u in enumerate(units):
                        cols = slice(h * HALF, (h + 1) * HALF)
                        ins = pe.matmul(bank(u, cols=HALF), lo, x_hi[:, k, cols], start=False, stop=last)
                        if last:
                            ins.then_inc(full, 1)

            def sums_by_token(u, tiles, dst_cols=1):
                free(u)
                for t, c in enumerate(TILE_AT):
                    for m, src in enumerate(tiles):
                        ins = pe.matmul(ps[:, u.bank, t:t + 1], src[:, c:c + P], ones[:, 0:1], start=(m == 0),
                                        stop=(m == len(tiles) - 1))
                ins.then_inc(full, 1)

            for l, L in enumerate(plan):
                def tokens(units, n, cols):
                    split_ready(n)
                    for t, u in enumerate(units):
                        free(u)
                        by_token(u, t, slots.raw[n] % 2, n, cols).then_inc(full, 1)

                split_ready(L["w_in"][0])
                for m in range(2):
                    for u in L["q"][m]:
                        free(u)
                    by_feature(L["q"][m], slots.raw[L["w_in"][0]] % 2, m * P, COLS, KT, hs_hi, hs_lo,
                               ready=lambda k: pe.wait_ge(hs_lo_done, 2 * l * KT + k + 1))
                pe.wait_ge(summed, (2 * l + 1) * KT)
                sums_by_token(L["ss1"], [sumsq])
                tokens(L["kv"], L["w_in"][1], KV_KR)
                tokens(L["v0"], L["w_in"][2], COLS)
                emptied(pe, L["q"][1][1])
                sums_by_token(L["ssq"], [gate[:, 0, :], gate[:, 1, :]])
                tokens(L["v1"], L["w_in"][3], COLS)

                pe.wait_ge(ckv_normed, l + 1)
                pe.wait_ge(layer_loaded, 16 * SMALL * (l + 1))
                for j, u in enumerate(L["ct"]):
                    free(u)
                    if j == 0:
                        srcs = [ckv_n[:, t, :] for t in range(PT_)]
                    elif j == 1:
                        srcs = [ckv_n[:, PT_, :]]
                    else:
                        srcs = [cache_in[:, 4 * (j - 2) + i, :] for i in range(4)]
                    for i, src in enumerate(srcs):
                        ins = turn(ps[:, u.bank, i * P:(i + 1) * P], src, P)
                    ins.then_inc(full, 1)
                for j, u in enumerate(L["wst"]):
                    free(u)
                    if j < 2:
                        for i in range(4):
                            ins = turn(ps[:, u.bank, i * P:(i + 1) * P], ws_in[:, 4 * j + i, :], P)
                    else:
                        for g in range(GROUPS):
                            ins = pe.matmul(ps[DEC:P, u.bank, g * DEC:(g + 1) * DEC], ws_in[0:DEC, g, 0:DEC],
                                            ident[0:DEC, 0:DEC], start=True, stop=True)
                    ins.then_inc(full, 1)

                def prep_up(t):
                    tile = t["tile"]
                    for e, u in enumerate(t["up"]):
                        free(u)
                        if t["what"] == "q":
                            c = TILE_AT[tile]
                            for m in range(2):
                                w = m * HEADS * QK + e * 4 * QK
                                ins = pe.matmul(bank(u, cols=4 * QK), qlatT[:, m, c:c + P],
                                                raw[:, L["wq"] % 2, w:w + 4 * QK], start=(m == 0), stop=(m == 1))
                        else:
                            c, w = key_tile(tile)
                            wkv = raw[:, L["wkv"] % 2, 0:2 * WIDTH].rearrange("p (h c) -> p h c", h=HEADS)
                            ins = pe.matmul(ps[0:w, u.bank, :].rearrange("p (h c) -> p h c", h=HEADS),
                                            ckvT[:, c:c + w], wkv[:, :, e * NOPE:(e + 1) * NOPE],
                                            start=True, stop=True)
                        ins.then_inc(full, 1)

                def prep_turn(t):
                    seq, tile = t["seq"], t["tile"]
                    pe.wait_ge(tile_normed, PREPS * l + seq + 1)
                    if t["what"] == "k" and tile != CACHE_TILES:
                        pe.wait_ge(kr_spread, t["spreads"])
                    w = P if t["what"] == "q" else key_tile(tile)[1]
                    for e, u in enumerate(t["turn"]):
                        free(u)
                        for i in range(4):
                            ins = turn(ps[0:QK, u.bank, i * P:i * P + w], tm[0:w, seq % 4, 4 * e + i, :], w)
                        ins.then_inc(full, 1)

                def preps_run(todo, steps):
                    for n in steps:
                        if n < len(todo):
                            prep_up(todo[n])
                        if n >= 2:
                            prep_turn(todo[n - 2])

                tokens(L["u0"], L["w_in"][4], COLS)
                pe.wait_ge(raw_loaded[L["wq"] % 2], 16 * (L["wq"] // 2 + 1))
                preps_run(L["s_preps"], [0])
                tokens(L["u1"], L["w_in"][5], COLS)

                pe.wait_ge(raw_loaded[L["wkv"] % 2], 16 * (L["wkv"] // 2 + 1))
                emptied(pe, L["ct"][2])
                emptied(pe, L["ct"][3])
                preps_run(L["s_preps"], range(1, len(S_TILES) + 2))

                pe.wait_ge(vn_done, l + 1)
                pe.wait_ge(wsT_masked, l + 1)
                emptied(pe, L["u1"][-1])
                for g2 in range(4):
                    u = L["mix"][g2]
                    free(u)
                    for e in range(2):
                        g = 2 * g2 + e
                        ins = pe.matmul(ps[:, u.bank, e * 256:(e + 1) * 256].rearrange("p (t d) -> p t d", t=PT_),
                                        wsT[:, g, :], gv[:, 0:PT_, g * GDIM:(g + 1) * GDIM], start=True, stop=True)
                    ins.then_inc(full, 1)
                u = L["mix"][4]
                free(u)
                for g in range(GROUPS):
                    ins = pe.matmul(ps[DEC:P, u.bank, g * GDIM:(g + 1) * GDIM], wsT_s[DEC:P, g, :],
                                    gv[DEC:P, PT_, g * GDIM:(g + 1) * GDIM], start=True, stop=True)
                ins.then_inc(full, 1)

                emptied(pe, L["s_preps"][-1]["turn"][0])
                emptied(pe, L["s_preps"][-1]["turn"][1])
                emptied(pe, L["s_preps"][-1]["up"][1])
                for n in range(HEAD_PAIRS + 2):
                    if n >= HEAD_PAIRS:
                        preps_run(L["p_preps"], [n - HEAD_PAIRS])
                    if n < HEAD_PAIRS:
                        for (c, w), u in zip(S_SPANS, L["s_steps"][n]["s"]):
                            free(u)
                            for e in range(2):
                                ins = pe.matmul(ps[e * DEC:(e + 1) * DEC, u.bank, 0:w], qT_s[:, 2 * n + e, :],
                                                kT_s[:, 2 * n + e, c:c + w], start=True, stop=True)
                            ins.then_inc(full, 1)
                    if 1 <= n <= HEAD_PAIRS:
                        m = n - 1
                        emptied(pe, L["s_steps"][m]["s"][-1])
                        for (first, count), u in zip(S_TRANS, L["s_steps"][m]["t"]):
                            free(u)
                            for i in range(count):
                                c = (first + i) * P
                                w = min(P, S_KEYS - c)
                                ins = turn(ps[0:w, u.bank, i * P:(i + 1) * P], p_sb[:, m % 2, c:c + w], P)
                            ins.then_inc(full, 1)
                    if n >= 2:
                        m = n - 2
                        for u in L["s_steps"][m]["t"]:
                            emptied(pe, u)
                        u = L["s_steps"][m]["o"]
                        free(u)
                        for e in range(2):
                            h = 2 * m + e
                            for j in range(CACHE_TILES + 1):
                                w = key_tile(j)[1]
                                ins = pe.matmul(ps[e * DEC:(e + 1) * DEC, u.bank, 0:VDIM],
                                                pT[0:w, m % 2, j, e * DEC:(e + 1) * DEC],
                                                v_s[0:w, j, h * VDIM:(h + 1) * VDIM],
                                                start=(j == 0), stop=(j == CACHE_TILES))
                        ins.then_inc(full, 1)

                preps_run(L["p_preps"], range(2, len(P_TILES) + 2))

                emptied(pe, L["p_preps"][-1]["turn"][0])
                emptied(pe, L["p_preps"][-1]["turn"][1])
                emptied(pe, L["p_preps"][-1]["up"][1])
                for n in range(len(P_STEPS) + 2):
                    if n < len(P_STEPS):
                        i, h0, nh = P_STEPS[n]
                        u = L["p_steps"][n]["s"]
                        w = (i + 1) * P
                        free(u)
                        for e in range(nh):
                            ins = pe.matmul(ps[:, u.bank, e * w:(e + 1) * w], qT_p[:, h0 + e, i * P:(i + 1) * P],
                                            kT_p[:, h0 + e, 0:w], start=True, stop=True)
                        ins.then_inc(full, 1)
                    if 1 <= n <= len(P_STEPS):
                        m = n - 1
                        i, h0, nh = P_STEPS[m]
                        emptied(pe, L["p_steps"][m]["s"])
                        u = L["p_steps"][m]["t"]
                        free(u)
                        for e in range(nh * (i + 1)):
                            ins = turn(ps[:, u.bank, e * P:(e + 1) * P], p_sb[:, m % 2, e * P:(e + 1) * P], P)
                        ins.then_inc(full, 1)
                    if n >= 2:
                        m = n - 2
                        i, h0, nh = P_STEPS[m]
                        emptied(pe, L["p_steps"][m]["t"])
                        u = L["p_steps"][m]["o"]
                        free(u)
                        for e in range(nh):
                            for j in range(i + 1):
                                ins = pe.matmul(ps[:, u.bank, e * VDIM:(e + 1) * VDIM], pT[:, m % 2, e * (i + 1) + j, :],
                                                v_p[:, j, (h0 + e) * VDIM:(h0 + e + 1) * VDIM],
                                                start=(j == 0), stop=(j == i))
                        ins.then_inc(full, 1)

                pe.wait_ge(gm_normed, l + 1)
                for k in MERGED:
                    u = L["mt"][k]
                    free(u)
                    if k == 0:
                        pe.wait_ge(o_normed, (PT_ + 1) * (l + 1))
                    elif k == KT:
                        pe.wait_ge(o_normed, (PT_ + 1) * l + 1)
                        for j in range(KT):
                            if j < 4:
                                for e in range(2):
                                    half = slice(e * DEC, (e + 1) * DEC)
                                    pe.matmul(ps[half, u.bank, j * DEC:(j + 1) * DEC], o_s[half, j, :], ident[half, half],
                                              start=True, stop=True)
                            else:
                                ins = pe.transpose(ps[:, u.bank, j * DEC:(j + 1) * DEC],
                                                   ug[DEC:P, PT_, (j - 4) * P:(j - 3) * P], ident[DEC:P, DEC:P])
                        ins.then_inc(full, 1)
                        continue
                    for t in range(PT_):
                        src = o_tm[:, t * WIDTH + k * P:t * WIDTH + (k + 1) * P] if k < 4 else ug[:, t, (k - 4) * P:(k - 3) * P]
                        ins = turn(ps[:, u.bank, t * P:(t + 1) * P], src, P)
                    ins.then_inc(full, 1)

                pe.wait_ge(m_lo, l + 1)
                for j, n in enumerate(L["w_o"]):
                    split_ready(n)
                    for e in range(2):
                        units = L["wo"][2 * j + e]
                        for u in units:
                            free(u)
                        by_feature(units, slots.raw[n] % 2, e * P, COLS, KT, hs_hi, hs_lo, order=MERGED[1:],
                                   ready=None if j or e else lambda k: emptied(pe, L["mt"][k]))

                def gate_or_up(pair, k_w):
                    for f in range(2):
                        by_feature(pair[f], k_w, f * P, COLS, KT, hs_hi, hs_lo)

                n = L["ffn_in"][0]
                split_ready(n)
                for f in range(2):
                    for u in L["g0"][f]:
                        free(u)
                    by_feature(L["g0"][f], slots.raw[n] % 2, f * P, COLS, KT, hs_hi, hs_lo,
                               ready=lambda k: pe.wait_ge(hs_lo_done, (2 * l + 1) * KT + k + 1))
                    if f == 0:
                        pe.wait_ge(summed, (2 * l + 2) * KT)
                        sums_by_token(L["ss2"], [sumsq])
                pe.wait_ge(r_ready, 2 * l + 2)
                for j, u in enumerate(L["rb"]):
                    free(u)
                    for t in (range(PT_) if j == 0 else [PT_]):
                        ins = pe.matmul(ps[:, u.bank, (t % PT_) * P:(t % PT_ + 1) * P],
                                        r_tok[:, t:t + 1].to_broadcast([P, P]), ident[:, :], start=True, stop=True)
                    ins.then_inc(full, 1)
                n = L["ffn_in"][1]
                split_ready(n)
                for f in range(2):
                    for u in L["u0f"][f]:
                        free(u)
                    by_feature(L["u0f"][f], slots.raw[n] % 2, f * P, COLS, KT, hs_hi, hs_lo)
                emptied(pe, L["rb"][1])
                n0 = L["body_slots"][0]
                pairs = 2 * FPAIRS * l
                with pe.Fori(0, BODIES) as i:
                    for s in range(2):
                        for j, groups in enumerate(L["body"][s]):
                            n = n0 + 3 * s + j
                            pe.wait_ge(lo_split, i * 6 + (slots.raw[n] + 1))
                            if j == 1:
                                pe.wait_ge(act_lo_done, i * 4 + (pairs + 2 * s + 2))
                            for m, units in enumerate(groups):
                                pe.wait_ge(S["ffn_out"], i * L["body_per"] + units[1].before[1])
                                if j == 1:
                                    by_feature(units, slots.raw[n] % 2, m * P, D_MODEL, 2, act_hi, act_lo)
                                else:
                                    by_feature(units, slots.raw[n] % 2, m * P, COLS, KT, hs_hi, hs_lo)
                n = L["last_slot"]
                split_ready(n)
                pe.wait_ge(act_lo_done, pairs + 2 * FPAIRS)
                for m, units in enumerate(L["last"]):
                    for u in units:
                        free(u)
                    by_feature(units, slots.raw[n] % 2, m * P, D_MODEL, 2, act_hi, act_lo)

            emptied(pe, plan[-1]["last"][-1][0])
            for t in range(NT):
                w = P if t < PT_ else DEC
                for e, u in enumerate(y_units[t]):
                    free(u)
                    for j in range(4):
                        ins = turn(ps[0:w, u.bank, j * P:(j + 1) * P], xT[:, 4 * e + j, t * P:t * P + w], P)
                    ins.then_inc(full, 1)


OUTS = [("y_prompt", (1, SEQ, D_MODEL)), ("y_sample", (1, DEC, D_MODEL)), ("ckv_prompt", (DEPTH, 1, SEQ, KV_LORA)),
        ("krope_prompt", (DEPTH, 1, SEQ, ROPE)), ("ckv_sample", (DEPTH, 1, DEC, KV_LORA)),
        ("krope_sample", (DEPTH, 1, DEC, ROPE)), ("gmlp_v_sample", (DEPTH, 1, DEC, WIDTH))]


def kernel(**inputs):
    import concourse.bacc as bacc
    from concourse.bass_utils import run_bass_kernel_spmd

    pos = np.concatenate([np.arange(SEQ), PAST + np.arange(DEC)]).astype(np.float32)
    half = ROPE // 2
    inv = np.float32(THETA) ** (-np.arange(half, dtype=np.float32) / np.float32(half))
    ang = pos[:, None] * inv[None, :]
    arrays = {name: np.ascontiguousarray(x) for name, x in inputs.items()}
    arrays["trig"] = np.concatenate([np.cos(ang), np.sin(ang)], axis=1).astype(np.float32)

    nc = bacc.Bacc("TRN2", target_bir_lowering=False, num_devices=1)
    a = {name: nc.dram_tensor("in_" + name, x.shape, F32, kind="ExternalInput").ap() for name, x in arrays.items()}
    out = {name: nc.dram_tensor("out_" + name, shape, F32, kind="ExternalOutput").ap() for name, shape in OUTS}
    trunk(nc, a, out)
    r = run_bass_kernel_spmd(nc, [{"in_" + name: x for name, x in arrays.items()}], core_ids=[0])
    return tuple(r.results[0]["out_" + name] for name, _ in OUTS)
```

```python
from contextlib import ExitStack

import numpy as np

import concourse.bass as bass
from concourse import mybir

D_MODEL, SEQ, DEC, DEPTH, PAST = 1024, 512, 64, 2, 1024
HEADS, NOPE, ROPE, VDIM = 8, 64, 32, 64
QK = NOPE + ROPE
Q_LORA, KV_LORA = 256, 128
GROUPS, GDIM = 8, 64
WIDTH = GROUPS * GDIM
D_FF = 2816
CHUNK = 64
EPS = 1e-6
SCALE = float(QK) ** -0.5
MASKED = 1e30
THETA = 10000.0

P = 128
TOK = SEQ + DEC
HALF = TOK // 2
KT = D_MODEL // P
TILE_AT = [0, 128, 256, 384, TOK - P]
NT = len(TILE_AT)
PT_ = SEQ // P
CACHE_TILES = PAST // P
S_KEYS = PAST + DEC
ALL_KEYS = S_KEYS + SEQ
KV_KR = KV_LORA + ROPE
BLOCK = 2048
COLS = BLOCK // KT
FPAIRS = D_FF // COLS
BODIES = (FPAIRS - 1) // 2
assert FPAIRS == 1 + 2 * BODIES

F32 = mybir.dt.float32
F32R = mybir.dt.float32r
ALU = mybir.AluOpType
ACT = mybir.ActivationFunctionType
AX = mybir.AxisListType

G_MIX, G_FFN, G_QL, G_BS, G_OUT = 0, 16, 32, 36, 52
G_QN, G_KN = 68, 70
G_BS_S = 72
G_ROWS = 88


class Unit:

    def __init__(self, n, done, before, freed):
        self.n, self.bank, self.done, self.before, self.freed = n, n % 8, done, before, freed


class Ring:

    def __init__(self):
        self.units, self.values, self.done = [], {}, 0

    def before(self):
        return self.units[-8].freed if len(self.units) >= 8 else None

    def add(self, sem, with_last=False):
        if not with_last:
            self.values[sem] = self.values.get(sem, 0) + 1
        self.done += 1
        u = Unit(len(self.units), self.done, self.before(), (sem, self.values[sem]))
        self.units.append(u)
        return u

    def skip(self):
        self.units.append(Unit(len(self.units), self.done, None, self.before()))

    def repeat(self, first, times):
        body = self.units[first:]
        size = len(body)
        sem = body[0].freed[0]
        assert size % 8 == 0 and all(u.freed[0] == sem for u in body)
        per = len({u.freed[1] for u in body})
        for t in range(1, times):
            for u in body:
                self.units.append(Unit(len(self.units), u.done + size * t, self.before(),
                                       (sem, u.freed[1] + per * t)))
        self.done += size * (times - 1)
        self.values[sem] += per * (times - 1)
        for j, u in enumerate(body):
            steady = self.units[first + size + j].before
            u.before = (sem, steady[1] - per)
            assert u.before[1] > 0
        return size, per


class Slots:

    def __init__(self):
        self.raw, self.n_split, self.last = [], 0, {}

    def load(self, split=True):
        self.raw.append(self.n_split if split else None)
        self.n_split += split
        return len(self.raw) - 1

    def used(self, n, unit):
        self.last[n] = unit


def prep_tiles():
    own = CACHE_TILES
    sample = [("q", PT_)] + [("k", j) for j in range(own + 1)]
    k = own + 1
    prompt = [("q", 0), ("q", 1), ("k", k), ("q", 2), ("k", k + 1), ("q", 3), ("k", k + 2), ("k", k + 3)]
    return sample, prompt


def key_tile(j):
    if j < CACHE_TILES:
        return j * P, P
    if j == CACHE_TILES:
        return PAST, DEC
    return S_KEYS + (j - CACHE_TILES - 1) * P, P


S_TILES, P_TILES = prep_tiles()
PREPS = len(S_TILES) + len(P_TILES)
SPREADS = CACHE_TILES + PT_
S_SPANS = [(0, 512), (512, 512), (1024, 64)]
S_TRANS = [(0, 4), (4, 4), (8, 1)]
HEAD_PAIRS = HEADS // 2
P_STEPS = [(i, h, n) for i, n in ((0, 4), (1, 2), (2, 1), (3, 1)) for h in range(0, HEADS, n)]
STEPS = HEAD_PAIRS + len(P_STEPS)
PREP, ATTEND = [("prep", n) for n in range(len(P_TILES) + 2)], [("attend", n) for n in range(len(P_STEPS) + 3)]
P_ORDER = PREP[2:7] + [ATTEND[0], PREP[7], ATTEND[1], PREP[8], ATTEND[2], PREP[9]] + ATTEND[3:]
P_ORDER_READERS = PREP[2:7] + [PREP[7], ATTEND[0], PREP[8], ATTEND[1], PREP[9], ATTEND[2]] + ATTEND[3:]
assert P_ORDER[-len(P_STEPS) - 1] == ("prep", len(P_TILES) + 1)
O_PARTS = [(PT_ * WIDTH, HEAD_PAIRS)] + [(i * WIDTH, HEADS) for i in range(PT_)]
SQUARED = {"o0": 4, "g0": 5, "g1": 6, "g2": 7, "o1": 8, "g3": 9, "o2": 10, "g4": 11, "o3": 17}
ASKED = {"o0": 6, "g0": 7, "g1": 8, "g2": 9, "o1": 10, "g3": 11, "o2": 12, "g4": 13, "o3": 19}
APPLIED = {"o0": 9, "o1": 13, "o2": 15, "o3": 21}
assert list(SQUARED) == list(ASKED) and min(SQUARED.values()) > 3
W_O_HIGH = (13, 15)
Y_AFTER = 5
MERGED = [KT, 4, 5, 6, 7, 0, 1, 2, 3]
SMALL, EARLY_GAINS, LATE_GAINS = 8, 3, 8
ROOTS = (["r1", "kv", "q", "ln"] + [f"b{n}" for n in range(PREPS)]
         + list(ASKED) + ["o4", "r2"])


def root_no(l, name):
    return l * len(ROOTS) + ROOTS.index(name) + 1


def build_plan():
    ring, slots, plan = Ring(), Slots(), []
    xt = [[ring.add("x_turned_dve"), ring.add("x_turned_act")] for _ in range(PT_)]
    gains = [ring.add("gains_turned")]
    xt.append([ring.add("x_turned_dve"), ring.add("x_turned_act")])
    gains.append(ring.add("gains_turned"))
    for l in range(DEPTH):
        L = {}
        L["w_in"] = w = [slots.load() for _ in range(6)]
        L["q"] = [[ring.add("qlat_out") for _ in range(2)] for _ in range(2)]
        slots.used(w[0], L["q"][-1][-1])
        L["kv"] = [ring.add("kv_out") for _ in range(NT)]
        slots.used(w[1], L["kv"][-1])
        L["ss1"] = ring.add("sumsq_out")
        L["v0"] = [ring.add("gelu_out") for _ in range(NT)]
        L["ssq"] = ring.add("sumsq_out")
        L["v1"] = [ring.add("gelu_out") for _ in range(NT)]
        L["ct"] = [ring.add("ckvt_act" if j % 2 else "ckvt_dve") for j in range(4)]
        L["wst"] = [ring.add("wst_out") for _ in range(3)]
        L["u0"] = [ring.add("gelu_out") for _ in range(NT)]
        L["wq"], L["wkv"] = slots.load(False), slots.load(False)
        L["preps"] = []
        spreads = SPREADS * l

        def prep(out, todo, steps):
            nonlocal spreads
            for n in steps:
                if n < len(todo):
                    what, tile = todo[n]
                    spreads += what == "k" and tile != CACHE_TILES
                    out.append({"what": what, "tile": tile, "seq": len(L["preps"]), "spreads": spreads,
                                "up": (ring.add("qz_out" if what == "q" else "k_out"),
                                       ring.add("qz_out" if what == "q" else "v_out"))})
                    L["preps"].append(out[-1])
                if n >= 2:
                    out[n - 2]["turn"] = (ring.add("qkt_dve"), ring.add("qkt_act"))

        L["s_preps"], L["p_preps"] = [], []
        prep(L["s_preps"], S_TILES, [0])
        L["u1"] = [ring.add("gelu_out") for _ in range(NT)]
        for j, name in enumerate(("v0", "v1", "u0", "u1")):
            slots.used(w[2 + j], L[name][-1])
        prep(L["s_preps"], S_TILES, range(1, len(S_TILES) + 2))
        L["mix"] = [ring.add("mix_out") for _ in range(5)]
        L["s_steps"] = steps = [{} for _ in range(HEAD_PAIRS)]
        for n in range(HEAD_PAIRS + 2):
            if n >= HEAD_PAIRS:
                prep(L["p_preps"], P_TILES, [n - HEAD_PAIRS])
            if n < HEAD_PAIRS:
                steps[n]["s"] = [ring.add("s_exp") for _ in S_SPANS]
            if 1 <= n <= HEAD_PAIRS:
                steps[n - 1]["t"] = [ring.add("pt_dve"), ring.add("pt_act"), ring.add("pt_dve")]
            if n >= 2:
                steps[n - 2]["o"] = ring.add("o_out")
        L["p_steps"] = steps = [{} for _ in P_STEPS]
        for what, n in P_ORDER:
            if what == "prep":
                prep(L["p_preps"], P_TILES, [n])
                continue
            if n < len(P_STEPS):
                steps[n]["s"] = ring.add("s_exp")
            if 2 <= n < len(P_STEPS) + 2:
                steps[n - 2]["t"] = ring.add("pt_act")
            if n >= 3:
                steps[n - 3]["o"] = ring.add("o_out")
        slots.used(L["wq"], L["p_preps"][-3]["up"][1])
        slots.used(L["wkv"], L["p_preps"][-1]["up"][1])
        L["mt"] = {k: ring.add("merged_out") for k in MERGED}
        L["w_o"] = [slots.load() for _ in range(4)]
        if len(ring.units) % 2:
            ring.skip()
        L["wo"] = [[ring.add("wo_added", with_last=h > 0) for h in range(2)] for _ in range(KT)]
        for j, n in enumerate(L["w_o"]):
            slots.used(n, L["wo"][2 * j + 1][1])

        def pair_units(n, between=lambda: None):
            out = []
            for f in range(2):
                out.append([ring.add("ffn_out", with_last=h > 0) for h in range(2)])
                if f == 0:
                    between()
            slots.used(n, out[1][1])
            return out

        def down_units(n, y=None):
            out = []
            for m in range(KT):
                out.append([ring.add("ffn_out", with_last=h > 0) for h in range(2)])
                if y is not None and m == Y_AFTER:
                    y.append([ring.add("y_dve") for _ in range(NT)])
                    if NT % 2:
                        ring.skip()
            slots.used(n, out[-1][1])
            return out

        L["ffn_in"] = [slots.load() for _ in range(2)]

        def sums():
            L["ss2"] = ring.add("sumsq_out")
            ring.skip()
            L["rb"] = [ring.add("rb_out") for _ in range(2)]

        L["g0"] = pair_units(L["ffn_in"][0], between=sums)
        L["u0f"] = pair_units(L["ffn_in"][1])
        first = len(ring.units)
        L["body_slots"] = n = [slots.load() for _ in range(6)]
        L["body"] = [(pair_units(n[3 * s]), down_units(n[3 * s + 1]), pair_units(n[3 * s + 2]))
                     for s in range(2)]
        size, per = L["body_size"], L["body_per"] = ring.repeat(first, BODIES)
        for j in range(6 * (BODIES - 1)):
            m = slots.load()
            slots.used(m, ring.units[slots.last[m - 6].n + size])
        L["last_u"] = [ring.units[u[0].n + size * (BODIES - 1)] for u in L["body"][1][2]]
        L["last_slot"] = slots.load()
        y = [] if l == DEPTH - 1 else None
        L["last"] = down_units(L["last_slot"], y)
        plan.append(L)
    y.append([ring.add("y_act") for _ in range(NT)])
    return ring, slots, gains, xt, plan, y


def trunk(nc, a, out):
    ring, slots, gains_units, xt_units, plan, y_units = build_plan()
    sems = ExitStack()
    with sems:
        place_at = {}

        def place(name, shape, dtype, at):
            size = 4 * int(np.prod(shape[1:]))
            place_at[name] = (at, at + size)
            assert at % 32 == 0 and at + size <= nc.sbuf_top, (name, at, size)
            return nc.alloc_sbuf_tensor_at(name, shape, dtype, offset=at)

        at = -(-nc.sbuf_base // 32) * 32
        xT = place("xT", [P, KT, TOK], F32, at)
        at += 4 * KT * TOK
        r0 = at
        hs_hi = place("hs_hi", [P, KT, TOK], F32R, at)
        at += 4 * KT * TOK
        hs_lo = place("hs_lo", [P, KT, TOK], F32R, at)
        at += 4 * KT * TOK
        act_hi = place("act_hi", [P, 2, TOK], F32R, at)
        at += 8 * TOK
        act_lo = place("act_lo", [P, 2, TOK], F32R, at)
        at += 8 * TOK
        gate = place("gate", [P, 2, TOK], F32, at)
        at += 8 * TOK
        hid = place("hid", [P, 2, TOK], F32, at)
        sumsq = place("sumsq", [P, TOK], F32, at)
        at += 8 * TOK
        kT_s = place("kT_s", [QK, HEADS, S_KEYS], F32, r0)
        v_s = place("v_s", [P, CACHE_TILES + 1, WIDTH], F32, r0 + 4 * HEADS * S_KEYS)
        qT_s = place("qT_s", [QK, HEADS, DEC], F32, at - 4 * HEADS * DEC)
        assert r0 + 4 * HEADS * S_KEYS + 4 * (CACHE_TILES + 1) * WIDTH <= at - 4 * HEADS * DEC
        kT_p = place("kT_p", [QK, HEADS, SEQ], F32, r0)
        v_p = place("v_p", [P, PT_, WIDTH], F32, r0 + 4 * HEADS * SEQ)
        qT_p = place("qT_p", [QK, HEADS, SEQ], F32, r0 + 4 * HEADS * SEQ + 4 * PT_ * WIDTH)
        raw = place("raw", [P, 2, BLOCK], F32, at)
        at += 8 * BLOCK
        w_hi = place("w_hi", [P, 2, BLOCK], F32R, at)
        at += 8 * BLOCK
        w_lo = place("w_lo", [P, 2, BLOCK], F32R, at)
        at += 8 * BLOCK
        qlatT = place("qlatT", [P, 2, TOK], F32, at)
        rb = place("rb", [P, TOK], F32, at + 4 * TOK)
        at += 8 * TOK
        ug = place("ug", [P, NT, WIDTH], F32, at)
        x_tm = place("x_tm", [P, NT, D_MODEL], F32, at)
        at += 4 * NT * WIDTH
        gv = place("gv", [P, NT, WIDTH], F32, at)
        o_tm = place("o_tm", [P, PT_ * WIDTH + HEAD_PAIRS * VDIM], F32, at)
        o_s = o_tm[:, PT_ * WIDTH:].rearrange("p (m d) -> p m d", d=VDIM)
        at += 4 * NT * WIDTH
        ckv_n = place("ckv_n", [P, NT, KV_LORA], F32, at)
        at += 4 * NT * KV_LORA
        kr_n = place("kr_n", [P, NT, ROPE], F32, at)
        at += 4 * NT * ROPE
        ckvT = place("ckvT", [P, ALL_KEYS], F32, at)
        at += 4 * ALL_KEYS
        wsT = place("wsT", [P, GROUPS, P], F32, at)
        at += 4 * GROUPS * P
        wsT_s = place("wsT_s", [P, GROUPS, DEC], F32, at)
        at += 4 * GROUPS * DEC
        tm = place("tm", [P, 4, HEADS, QK], F32, at)
        wide = place("wide", [P, 5 * WIDTH], F32, at)
        at += 16 * HEADS * QK
        sq = place("sq", [P, 2, HEADS, QK], F32, at)
        at += 8 * HEADS * QK
        wide_g = place("wide_g", [P, NT * WIDTH], F32, at - 24 * HEADS * QK)
        wide_o = place("wide_o", [P, 2, WIDTH], F32, at - 24 * HEADS * QK + 4 * NT * WIDTH)
        p_sb = place("p_sb", [P, 2, S_KEYS], F32, at)
        ws_in = place("ws_in", [P, GROUPS, P], F32, at)
        cache_in = place("cache_in", [P, CACHE_TILES, KV_LORA], F32, at + 4 * GROUPS * P)
        at += 8 * S_KEYS
        pT = place("pT", [P, 2, CACHE_TILES + 1, P], F32, at)
        kvz = place("kvz", [P, NT, KV_KR], F32, at)
        kvsq = place("kvsq", [P, NT, KV_KR], F32, at + 4 * NT * KV_KR)
        ms_sb = place("ms_sb", [P, KT, DEC], F32, at)
        at += 8 * (CACHE_TILES + 1) * P
        cache_kr = place("cache_kr", [P, CACHE_TILES, ROPE], F32, at)
        at += 4 * CACHE_TILES * ROPE
        ln_gb = place("ln_gb", [P, 2, WIDTH], F32, at)
        at += 8 * WIDTH
        g_tm = place("g_tm", [P, KV_LORA + 2 * ROPE], F32, at)
        at += 4 * (KV_LORA + 2 * ROPE)
        trig = place("trig", [P, NT, ROPE], F32, at)
        at += 4 * NT * ROPE
        trig_q = place("trig_q", [P, NT, 2, ROPE], F32, at)
        at += 8 * NT * ROPE
        rot = place("rot", [P, HEADS, ROPE], F32, at)
        at += 4 * HEADS * ROPE
        gT = place("gT", [P, G_ROWS], F32, at)
        at += 4 * G_ROWS
        gq = place("gq", [P, 8], F32, at)
        at += 32
        ident = place("ident", [P, P], F32, at)
        g_in = place("g_in", [P, P], F32, at + 512)
        at += 1024
        ones = place("ones", [P, 8], F32, at)
        at += 32
        mhalf = place("mhalf", [P, 64], F32, at)
        at += 256
        ms = place("ms", [P, 176], F32, at)
        at += 704
        rs = place("rs", [P, 176], F32, at)
        at += 704
        mu = place("mu", [P, 64], F32, at)
        at += 256
        r_tok = place("r_tok", [P, 8], F32, at)
        at += 32
        r_q = place("r_q", [P, 8], F32, at)
        at += 32
        mx = place("mx", [P, 8], F32, at)
        at += 32
        nm = place("nm", [P, 4, 8], F32, at)
        at += 128
        lsum = place("lsum", [P, 4, 8], F32, at)
        at += 128
        linv = place("linv", [P, 2, 8], F32, at)
        at += 64

        ps = sems.enter_context(nc.psum_tensor("ps", [P, 8, 512], F32))

        S = {}

        def sem(name):
            S[name] = sems.enter_context(nc.semaphore(name))
            return S[name]

        full = sem("full")
        for name in ring.values:
            sem(name)
        g_zeroed, ident_ready, const_ready = sem("g_zeroed"), sem("ident_ready"), sem("const_ready")
        gains_loaded, trig_loaded = [sem("early_gains_loaded"), sem("late_gains_loaded")], sem("trig_loaded")
        x_loaded = [sem(f"x_loaded{t}") for t in range(NT)]
        raw_loaded = [sem(f"raw_loaded{s}") for s in range(2)]
        layer_loaded = sem("layer_loaded")
        hi_split, lo_split = sem("hi_split"), sem("lo_split")
        gq_ready = sem("gq_ready")
        hs_hi_done, hs_lo_done = sem("hs_hi_done"), sem("hs_lo_done")
        squared, summed = sem("squared"), sem("summed")
        ms_ready, rs_ready = sem("ms_ready"), sem("rs_ready")
        r_ready, rq_ready = sem("r_ready"), sem("rq_ready")
        ckv_normed, kr_turned = sem("ckv_normed"), sem("kr_turned")
        v_centred, v_squared, vn_done = sem("v_centred"), sem("v_squared"), sem("vn_done")
        sq_free, tile_normed, kr_spread = sem("sq_free"), sem("tile_normed"), sem("kr_spread")
        nm_ready, wsT_masked = sem("nm_ready"), sem("wsT_masked")
        gm_squared, gm_normed = sem("gm_squared"), sem("gm_normed")
        o_squared, o_normed = sem("o_squared"), sem("o_normed")
        m_hi, m_lo = sem("m_hi"), sem("m_lo")
        silu_done, gate_done = sem("silu_done"), sem("gate_done")
        act_hi_done, act_lo_done = sem("act_hi_done"), sem("act_lo_done")
        dve_chain, pool_chain = sem("dve_chain"), sem("pool_chain")
        rows_stored, v_stored, y_stored = sem("rows_stored"), sem("v_stored"), sem("y_stored")

        def bank(u, rows=slice(0, P), cols=512):
            return ps[rows, u.bank, 0:cols]

        def halves(t):
            return t.rearrange("p (h c) -> p h c", h=2)

        gain_loads = [(row, slice(0, P), a[name].rearrange("l (k p) -> (l k) p", p=P))
                 for row, name in ((G_MIX, "g_mix"), (G_FFN, "g_ffn"), (G_QL, "g_q_lora"))]
        gain_loads.append((G_BS, slice(0, P), a["gm_b_s"].rearrange("l g i -> (l g) i")))
        gain_loads.append((G_BS_S, slice(DEC, P), a["gm_b_s"][:, :, 0:DEC].rearrange("l g i -> (l g) i")))
        for l in range(DEPTH):
            for j, name in enumerate(("g_out_att", "g_out_gm")):
                gain_loads.append((G_OUT + 8 * l + 4 * j, slice(0, P), a[name][l].rearrange("(k e) d -> k (e d)", e=2)))
        gain_loads += [(G_QN, slice(0, NOPE), a["g_qn"]), (G_KN, slice(0, NOPE), a["g_kn"])]
        assert len(gain_loads) == EARLY_GAINS + LATE_GAINS

        def in_cols(l, c0, c1):
            return a["w_in"][l][:, c0:c1].rearrange("(k p) n -> p k n", p=P)

        w_in_cols = [(0, Q_LORA), (Q_LORA, Q_LORA + KV_KR)]
        for c in (Q_LORA + KV_KR + WIDTH, Q_LORA + KV_KR):
            w_in_cols += [(c, c + COLS), (c + COLS, c + 2 * COLS)]

        raw_of = [n for n, k in enumerate(slots.raw) if k is not None]

        def part_cols(g):
            return slice(128 + HEADS * g, 128 + HEADS * g + O_PARTS[g][1])

        def prep_cols(t):
            c = 64 + 16 * (t["seq"] % 4)
            return slice(c, c + HEADS), slice(c + HEADS, c + 2 * HEADS)

        def emptied(eng, u):
            eng.wait_ge(S[u.freed[0]], u.freed[1])

        def filled(eng, u):
            eng.wait_ge(full, u.done)

        block = sems.enter_context(nc.Block())

        @block.sync
        def _(sp):
            def load(n, dst, src):
                if n >= 2:
                    k = slots.raw[n - 2]
                    if k is None:
                        filled(sp, slots.last[n - 2])
                    else:
                        sp.wait_ge(lo_split, k + 1)
                sp.dma_start(dst, src).then_inc(raw_loaded[n % 2], 16)

            def by_k(n, cols):
                return raw[:, n % 2, 0:KT * cols].rearrange("p (k n) -> p k n", k=KT)

            def by_f(n):
                return raw[:, n % 2, :].rearrange("p (f n) -> p f n", f=2)

            def small(l):
                if l:
                    sp.wait_ge(m_lo, l)
                loads = [(ws_in[:, :, :], a["gm_w_s"][l].rearrange("g i j -> i g j")),
                         (cache_in[:, :, :], a["cache_ckv"][l, 0].rearrange("(j p) c -> p j c", p=P)),
                         (cache_kr[:, :, :], a["cache_krope"][l, 0].rearrange("(j p) c -> p j c", p=P)),
                         (ln_gb[:, 0, :], a["gm_ln_g"][l].rearrange("g d -> (g d)").partition_broadcast(P)),
                         (ln_gb[:, 1, :], a["gm_ln_b"][l].rearrange("g d -> (g d)").partition_broadcast(P))]
                c = 0
                for name, n in (("g_kv_lora", KV_LORA), ("g_kr", ROPE), ("g_qr", ROPE)):
                    loads.append((g_tm[:, c:c + n], a[name][l].partition_broadcast(P)))
                    c += n
                assert len(loads) == SMALL
                for dst, src in loads:
                    sp.dma_start(dst, src).then_inc(layer_loaded, 16)

            for t, c in enumerate(TILE_AT[:PT_]):
                sp.dma_start(x_tm[:, t, :], a["x_prompt"][0, c:c + P, :]).then_inc(x_loaded[t], 16)
            sp.dma_start(x_tm[DEC:P, PT_, :], a["x_sample"][0]).then_inc(x_loaded[PT_], 16)
            for l, L in enumerate(plan):
                for n, (c0, c1) in zip(L["w_in"], w_in_cols):
                    load(n, by_k(n, c1 - c0), in_cols(l, c0, c1))
                    if l == 0 and n == L["w_in"][1]:
                        sp.wait_ge(g_zeroed, 1)
                        for row, cols, src in gain_loads[EARLY_GAINS:]:
                            sp.dma_start(g_in[row:row + src.shape[0], cols], src).then_inc(gains_loaded[1], 16)
                        for t, c in enumerate(TILE_AT):
                            sp.dma_start(trig[:, t, :], a["trig"][c:c + P, :]).then_inc(trig_loaded, 16)
                        small(0)
                n = L["wq"]
                load(n, raw[:, n % 2, 0:2 * HEADS * QK].rearrange("p (m n) -> p m n", m=2),
                     a["w_q_up"][l].rearrange("(m p) n -> p m n", p=P))
                n = L["wkv"]
                load(n, raw[:, n % 2, 0:2 * WIDTH], a["w_kv_up"][l])
                for j, n in enumerate(L["w_o"]):
                    load(n, by_k(n, COLS), a["w_o"][l][:, j * COLS:(j + 1) * COLS].rearrange("(k p) n -> p k n", p=P))
                gate_src = a["w_gate"][l].rearrange("(k p) (g n) -> g p k n", p=P, n=COLS)
                up_src = a["w_up"][l].rearrange("(k p) (g n) -> g p k n", p=P, n=COLS)
                down_src = a["w_down"][l].rearrange("(g f p) n -> g p f n", p=P, f=2)
                for n, src in zip(L["ffn_in"], (gate_src, up_src)):
                    load(n, by_k(n, COLS), src[0])
                if l + 1 < DEPTH:
                    small(l + 1)
                n0 = L["body_slots"][0]
                with sp.Fori(0, BODIES) as b:
                    for s in range(2):
                        for j, src in enumerate((gate_src, down_src, up_src)):
                            n = n0 + 3 * s + j
                            sp.wait_ge(lo_split, b * 6 + (slots.raw[n - 2] + 1))
                            sp.dma_start(by_f(n) if j == 1 else by_k(n, COLS),
                                         src[b * 2 + (s if j == 1 else s + 1)]).then_inc(raw_loaded[n % 2], 16)
                n = L["last_slot"]
                load(n, by_f(n), down_src[FPAIRS - 1])
            for e in range(2):
                cols = slice(e * WIDTH, (e + 1) * WIDTH)
                for t in range(NT):
                    emptied(sp, y_units[e][t])
                    if t < PT_:
                        sp.dma_start(out["y_prompt"][0, t * P:(t + 1) * P, cols], x_tm[:, t, cols]).then_inc(y_stored, 16)
                    else:
                        sp.dma_start(out["y_sample"][0, :, cols], x_tm[0:DEC, t, cols]).then_inc(y_stored, 16)
            sp.wait_ge(y_stored, 16 * 2 * NT)
            sp.wait_ge(rows_stored, 16 * 4 * DEPTH)
            sp.wait_ge(v_stored, 16 * DEPTH)

        @block.gpsimd
        def _(pool):
            chain = [0]

            def link(ins):
                chain[0] += 1
                ins.then_inc(pool_chain, 1)
                pool.wait_ge(pool_chain, chain[0])

            def w_low(n, size=BLOCK):
                k = slots.raw[n]
                pool.wait_ge(hi_split, k + 1)
                pool.tensor_tensor(w_lo[:, k % 2, 0:size], raw[:, n % 2, 0:size],
                                   w_hi[:, k % 2, 0:size].bitcast(F32), ALU.subtract).then_inc(lo_split, 1)

            def root(l, name, n, c=0):
                no = root_no(l, name)
                pool.wait_ge(ms_ready, no)
                pool.tensor_tensor(rs[:, c:c + n], ms[:, c:c + n], mhalf[:, 0:n], ALU.pow).then_inc(rs_ready, 1)

            def sum_squares(m, tiles):
                for k in tiles:
                    n = m * KT + k + 1
                    pool.wait_ge(squared, n)
                    if k:
                        pool.wait_ge(summed, n - 1)
                        ins = pool.tensor_tensor(sumsq[:, :], sumsq[:, :], gate[:, k % 2, :], ALU.add)
                    else:
                        ins = pool.tensor_copy(sumsq[:, :], gate[:, 0, :])
                    ins.then_inc(summed, 1)

            pool.memset(g_in[:, :], 0.0).then_inc(g_zeroed, 1)
            link(pool.memset(ident[:, :], 0.0))
            pool.affine_select(out=ident[:, :], in_=ident[:, :], compare_op=ALU.not_equal, fill=1.0, base=0,
                               pattern=[[-1, P]], channel_multiplier=1).then_inc(ident_ready, 1)
            pool.memset(ones[:, :], 1.0)
            pool.memset(ms[:, :], 1.0)
            pool.memset(mhalf[:, :], -0.5)
            pool.memset(gq[:, :], -SCALE).then_inc(const_ready, 1)
            pool.wait_ge(const_ready, 1)
            for l, L in enumerate(plan):
                if l == 0:
                    pool.wait_ge(lo_split, 1)
                    w_low(L["w_in"][1], KT * KV_KR)
                else:
                    w_low(L["w_in"][0])
                sum_squares(2 * l, range(KT))
                if l:
                    w_low(L["w_in"][1], KT * KV_KR)
                w_low(L["w_in"][2])
                root(l, "r1", NT)
                w_low(L["w_in"][3])
                root(l, "kv", 2 * NT)
                pool.wait_ge(ckv_normed, l + 1)
                if l == 0:
                    pool.wait_ge(trig_loaded, 16 * NT)
                h = ROPE // 2
                x1, x2 = kvz[:, :, KV_LORA:KV_LORA + h], kvz[:, :, KV_LORA + h:KV_KR]
                c, s = trig[:, :, 0:h], trig[:, :, h:ROPE]
                t1, t2 = kvsq[:, :, 0:h], kvsq[:, :, h:2 * h]
                link(pool.tensor_tensor(t1, x1, c, ALU.mult))
                link(pool.tensor_tensor(t2, x2, s, ALU.mult))
                link(pool.tensor_tensor(kr_n[:, :, 0:h], t1, t2, ALU.subtract))
                link(pool.tensor_tensor(t1, x1, s, ALU.mult))
                link(pool.tensor_tensor(t2, x2, c, ALU.mult))
                pool.tensor_tensor(kr_n[:, :, h:ROPE], t1, t2, ALU.add).then_inc(kr_turned, 1)
                root(l, "q", NT)
                w_low(L["w_in"][4])
                w_low(L["w_in"][5])
                root(l, "ln", NT * GROUPS)
                pool.wait_ge(layer_loaded, 16 * SMALL * (l + 1))

                def prep(t):
                    seq, tile = t["seq"], t["tile"]
                    nope, rope = prep_cols(t)
                    if t["what"] == "q":
                        root(l, f"b{seq}", 2 * HEADS, nope.start)
                        return
                    if tile != CACHE_TILES:
                        if seq >= 4:
                            filled(pool, L["preps"][seq - 4]["turn"][1])
                        src = cache_kr[:, tile, :] if tile < CACHE_TILES else kr_n[:, tile - CACHE_TILES - 1, :]
                        pool.tensor_copy(tm[:, seq % 4, :, NOPE:QK],
                                         src.unsqueeze(1).to_broadcast([P, HEADS, ROPE])).then_inc(kr_spread, 1)
                    root(l, f"b{seq}", HEADS, nope.start)

                for t in L["s_preps"]:
                    prep(t)
                for t in L["p_preps"]:
                    prep(t)

                def part(name):
                    g = int(name[1])
                    if name[0] == "o":
                        c = part_cols(g)
                        root(l, name, c.stop - c.start, c.start)
                        return
                    root(l, name, GROUPS, g * GROUPS)
                    pool.wait_ge(rs_ready, root_no(l, name))
                    u = ug[:, g, :].rearrange("p (g d) -> p g d", d=GDIM)
                    pool.tensor_tensor(u, u, rs[:, g * GROUPS:(g + 1) * GROUPS].unsqueeze(2).to_broadcast([P, GROUPS, GDIM]),
                                       ALU.mult).then_inc(gm_normed, 1)

                for name in ASKED:
                    if name == "o3":
                        w_low(L["w_o"][0])
                        w_low(L["w_o"][1])
                    part(name)
                part("o4")
                for j, n in enumerate(L["w_o"][2:] + L["ffn_in"][:1]):
                    sum_squares(2 * l + 1, range(2 * j, 2 * j + 2))
                    w_low(n)
                sum_squares(2 * l + 1, range(6, KT))
                root(l, "r2", NT)
                w_low(L["ffn_in"][1])

                def scale_gate(no, f):
                    pool.wait_ge(silu_done, no)
                    pool.tensor_tensor(gate[:, f, :], gate[:, f, :], rb[:, :], ALU.mult).then_inc(gate_done, 1)

                pairs = 2 * FPAIRS * l
                for f in range(2):
                    scale_gate(pairs + f + 1, f)
                n0 = L["body_slots"][0]
                with pool.Fori(0, BODIES) as i:
                    for s in range(2):
                        for j in range(3):
                            n = n0 + 3 * s + j
                            k = slots.raw[n]
                            pool.wait_ge(hi_split, i * 6 + (k + 1))
                            pool.tensor_tensor(w_lo[:, k % 2, :], raw[:, n % 2, :], w_hi[:, k % 2, :].bitcast(F32),
                                               ALU.subtract).then_inc(lo_split, 1)
                            if j == 1:
                                for f in range(2):
                                    scale_gate(i * 4 + (pairs + 3 + 2 * s + f), f)
                w_low(L["last_slot"])

        @block.scalar
        def _(act):
            def w_high(n, size=BLOCK):
                k = slots.raw[n]
                act.wait_ge(raw_loaded[n % 2], 16 * (n // 2 + 1))
                if k >= 2:
                    filled(act, slots.last[raw_of[k - 2]])
                act.activation(w_hi[:, k % 2, 0:size], raw[:, n % 2, 0:size], ACT.Copy).then_inc(hi_split, 1)

            act.wait_ge(g_zeroed, 1)
            for row, cols, src in gain_loads[:EARLY_GAINS]:
                act.dma_start(g_in[row:row + src.shape[0], cols], src).then_inc(gains_loaded[0], 16)
            for t in range(NT):
                u = xt_units[t][1]
                if t == PT_:
                    w_high(plan[0]["w_in"][0])
                filled(act, u)
                w = P if t < PT_ else DEC
                act.activation(xT[:, 4:8, t * P:t * P + w], bank(u).rearrange("p (k c) -> p k c", k=4)[:, :, 0:w],
                               ACT.Copy).then_inc(S["x_turned_act"], 1)

            def high_part(k, gcol):
                act.activation(hs_hi[:, k, :], xT[:, k, :], ACT.Copy, scale=gT[:, gcol + k:gcol + k + 1]
                               ).then_inc(hs_hi_done, 1)

            def square(m, k):
                if k >= 2:
                    act.wait_ge(summed, m * KT + k - 1)
                act.activation(gate[:, k % 2, :], xT[:, k, :], ACT.Square).then_inc(squared, 1)

            for l, L in enumerate(plan):
                if l:
                    w_high(L["w_in"][0])
                if l == 0:
                    emptied(act, gains_units[0])
                    emptied(act, xt_units[-1][0])
                    emptied(act, xt_units[-1][1])
                for k in range(KT):
                    if l:
                        emptied(act, plan[l - 1]["last"][k][0])
                    high_part(k, G_MIX + KT * l)
                    if l:
                        square(2 * l, k)
                w_high(L["w_in"][1], KT * KV_KR)
                if l == 0:
                    for k in range(KT):
                        square(0, k)

                def prep_first(t):
                    seq, tile = t["seq"], t["tile"]
                    if seq >= 2 or l:
                        act.wait_ge(sq_free, PREPS * l + seq - 1)
                    if seq >= 4:
                        filled(act, L["preps"][seq - 4]["turn"][1])
                    elif seq == 0:
                        act.wait_ge(ms_ready, root_no(l, "ln"))
                    if t["what"] == "q":
                        if seq == 0:
                            act.wait_ge(rq_ready, l + 1)
                        elif L["preps"][seq - 2]["what"] == "q":
                            act.wait_ge(tile_normed, PREPS * l + seq - 1)
                        for e, u in enumerate(t["up"]):
                            filled(act, u)
                            src = bank(u, cols=4 * QK).rearrange("p (h c) -> p h c", c=QK)
                            act.activation(sq[:, seq % 2, 4 * e:4 * e + 4, :], src, ACT.Square,
                                           scale=r_q[:, tile:tile + 1])
                            act.activation(tm[:, seq % 4, 4 * e:4 * e + 4, :], src, ACT.Copy,
                                           scale=r_q[:, tile:tile + 1]).then_inc(S["qz_out"], 1)
                        return
                    uk, uv = t["up"]
                    rows = slice(0, key_tile(tile)[1])
                    src = bank(uk, rows).rearrange("p (h c) -> p h c", c=NOPE)
                    filled(act, uk)
                    act.activation(sq[rows, seq % 2, :, 0:NOPE], src, ACT.Square)
                    act.activation(tm[rows, seq % 4, :, 0:NOPE], src, ACT.Copy).then_inc(S["k_out"], 1)
                    filled(act, uv)
                    dst = v_s[rows, tile, :] if tile <= CACHE_TILES else v_p[:, tile - CACHE_TILES - 1, :]
                    act.activation(dst, bank(uv, rows), ACT.Copy).then_inc(S["v_out"], 1)

                def prep_turned(t):
                    tile, u = t["tile"], t["turn"][1]
                    filled(act, u)
                    src = ps[0:QK, u.bank, :].rearrange("p (h c) -> p h c", h=4)
                    if t["what"] == "q":
                        act.wait_ge(gq_ready, 1)
                        scale = gq[0:QK, l:l + 1]
                        if tile == PT_:
                            dst, src = qT_s[:, 4:8, :], src[:, :, DEC:P]
                        else:
                            dst = qT_p[:, 4:8, tile * P:(tile + 1) * P]
                    else:
                        scale = 1.0
                        c, w = key_tile(tile)
                        src = src[:, :, 0:w]
                        dst = kT_s[:, 4:8, c:c + w] if tile <= CACHE_TILES else kT_p[:, 4:8, c - S_KEYS:c - S_KEYS + w]
                    act.activation(dst, src, ACT.Copy, scale=scale).then_inc(S["qkt_act"], 1)

                def preps_run(todo, steps):
                    for n in steps:
                        if n < len(todo):
                            prep_first(todo[n])
                        if n >= 2:
                            prep_turned(todo[n - 2])

                act.wait_ge(summed, (2 * l + 1) * KT)
                for m in range(2):
                    for h in range(2):
                        u = L["q"][m][h]
                        filled(act, u)
                        cols = slice(h * HALF, (h + 1) * HALF)
                        act.activation(gate[:, m, cols], bank(u, cols=HALF), ACT.Square)
                        act.activation(qlatT[:, m, cols], bank(u, cols=HALF), ACT.Copy,
                                       scale=gT[:, G_QL + 2 * l + m:G_QL + 2 * l + m + 1]).then_inc(S["qlat_out"], 1)
                w_high(L["w_in"][2])
                w_high(L["w_in"][3])
                act.wait_ge(r_ready, 2 * l + 1)
                for j, (name, dst) in enumerate((("v0", gv), ("v1", gv), ("u0", ug), ("u1", ug))):
                    if j == 3:
                        act.wait_ge(v_centred, l + 1)
                        act.activation(wide[:, :], gv[:, :, :].rearrange("p t c -> p (t c)"), ACT.Square
                                       ).then_inc(v_squared, 1)
                        preps_run(L["s_preps"], [0])
                    for t in range(NT):
                        u = L[name][t]
                        filled(act, u)
                        act.activation(dst[:, t, (j % 2) * COLS:(j % 2 + 1) * COLS], bank(u, cols=COLS),
                                       ACT.Gelu_apprx_tanh, scale=r_tok[:, t:t + 1]).then_inc(S["gelu_out"], 1)
                    if j < 2:
                        w_high(L["w_in"][4 + j])
                    if j == 1:
                        filled(act, L["ct"][1])
                        act.activation(ckvT[:, PAST:S_KEYS], ps[:, L["ct"][1].bank, DEC:P], ACT.Copy
                                       ).then_inc(S["ckvt_act"], 1)
                        filled(act, L["ct"][3])
                        act.activation(ckvT[:, PAST // 2:PAST], bank(L["ct"][3]), ACT.Copy).then_inc(S["ckvt_act"], 1)
                act.wait_ge(ckv_normed, l + 1)
                act.dma_start(out["ckv_prompt"][l, 0].rearrange("(t p) c -> p t c", p=P), ckv_n[:, 0:PT_, :]
                              ).then_inc(rows_stored, 16)
                act.dma_start(out["ckv_sample"][l, 0], ckv_n[DEC:P, PT_, :]).then_inc(rows_stored, 16)
                act.wait_ge(kr_turned, l + 1)
                act.dma_start(out["krope_prompt"][l, 0].rearrange("(t p) c -> p t c", p=P), kr_n[:, 0:PT_, :]
                              ).then_inc(rows_stored, 16)
                act.dma_start(out["krope_sample"][l, 0], kr_n[DEC:P, PT_, :]).then_inc(rows_stored, 16)

                preps_run(L["s_preps"], range(1, len(S_TILES) + 2))
                act.wait_ge(vn_done, l + 1)
                act.dma_start(out["gmlp_v_sample"][l, 0], gv[DEC:P, PT_, :]).then_inc(v_stored, 16)

                def sample_pt(n):
                    u = L["s_steps"][n]["t"][1]
                    filled(act, u)
                    if n >= 2:
                        filled(act, L["s_steps"][n - 2]["o"])
                    act.activation(pT[:, n % 2, 4:8, :], bank(u).rearrange("p (j c) -> p j c", j=4),
                                   ACT.Copy).then_inc(S["pt_act"], 1)

                for n, st in enumerate(L["s_steps"]):
                    act.wait_ge(nm_ready, STEPS * l + n + 1)
                    if n >= 2:
                        filled(act, L["s_steps"][n - 2]["t"][-1])
                    for e, ((c, w), u) in enumerate(zip(S_SPANS, st["s"])):
                        act.activation(p_sb[:, n % 2, c:c + w], bank(u, cols=w), ACT.Exp, bias=nm[:, n % 4, 0:1],
                                       scale=-1.0, accum_out=lsum[:, n % 4, e:e + 1]).then_inc(S["s_exp"], 1)
                    if n >= 1:
                        sample_pt(n - 1)
                preps_run(L["p_preps"], [0])
                sample_pt(HEAD_PAIRS - 1)
                preps_run(L["p_preps"], [1])

                def part_square(name):
                    g = int(name[1])
                    if name[0] == "g":
                        if g == 0:
                            emptied(act, L["mix"][-1])
                        act.activation(wide_g[:, g * WIDTH:(g + 1) * WIDTH], ug[:, g, :], ACT.Square).then_inc(gm_squared, 1)
                        return
                    if g == 0:
                        filled(act, L["p_preps"][-1]["turn"][1])
                        act.wait_ge(tile_normed, PREPS * (l + 1))
                        emptied(act, L["s_steps"][-1]["o"])
                    else:
                        last = max(m for m, step in enumerate(P_STEPS) if step[0] == g - 1)
                        emptied(act, L["p_steps"][last]["o"])
                    if g >= 2:
                        act.wait_ge(ms_ready, root_no(l, f"o{g - 2}"))
                    c, n = O_PARTS[g]
                    act.activation(wide_o[:, g % 2, 0:n * VDIM], o_tm[:, c:c + n * VDIM], ACT.Square
                                   ).then_inc(o_squared, 1)

                def prompt_pt(m):
                    i, _, nh = P_STEPS[m]
                    u = L["p_steps"][m]["t"]
                    filled(act, u)
                    if m >= 2:
                        filled(act, L["p_steps"][m - 2]["o"])
                    w = nh * (i + 1)
                    act.activation(pT[:, m % 2, 0:w, :], bank(u, cols=w * P).rearrange("p (j c) -> p j c", j=w),
                                   ACT.Copy).then_inc(S["pt_act"], 1)

                for what, n in P_ORDER_READERS:
                    if what == "prep":
                        preps_run(L["p_preps"], [n])
                        continue
                    if n < len(P_STEPS):
                        i, _, nh = P_STEPS[n]
                        u = L["p_steps"][n]["s"]
                        act.wait_ge(nm_ready, STEPS * l + HEAD_PAIRS + n + 1)
                        if n >= 2:
                            filled(act, L["p_steps"][n - 2]["t"])
                        w = (i + 1) * P
                        for e in range(nh):
                            ins = act.activation(p_sb[:, n % 2, e * w:(e + 1) * w], ps[:, u.bank, e * w:(e + 1) * w],
                                                 ACT.Exp, bias=nm[:, n % 4, e:e + 1], scale=-1.0,
                                                 accum_out=lsum[:, n % 4, e:e + 1])
                        ins.then_inc(S["s_exp"], 1)
                    if 2 <= n < len(P_STEPS) + 2:
                        prompt_pt(n - 2)
                    for name in SQUARED:
                        if SQUARED[name] == n:
                            part_square(name)
                    if n in W_O_HIGH:
                        w_high(L["w_o"][W_O_HIGH.index(n)])
                part_square(f"o{PT_}")
                for k in MERGED:
                    if k == KT:
                        emptied(act, L["mt"][KT])
                        act.activation(hs_hi[:, :, SEQ:TOK], ms_sb[:, :, :], ACT.Copy).then_inc(m_hi, 1)
                        continue
                    u = L["mt"][k]
                    filled(act, u)
                    g = G_OUT + 8 * l + k
                    act.activation(hs_hi[:, k, 0:SEQ], bank(u), ACT.Copy, scale=gT[:, g:g + 1]).then_inc(m_hi, 1)

                def square_output(k):
                    emptied(act, L["wo"][k][0])
                    square(2 * l + 1, k)

                for k in range(KT - 1):
                    if k in (2, 4, 6):
                        w_high((L["w_o"][2:] + L["ffn_in"][:1])[k // 2 - 1])
                    square_output(k)
                filled(act, L["wo"][-1][1])
                for k in range(KT):
                    if k == 2:
                        square_output(KT - 1)
                    high_part(k, G_FFN + KT * l)
                w_high(L["ffn_in"][1])

                def silu(f, no):
                    act.wait_ge(S["ffn_out"], no)
                    act.activation(gate[:, f, :], gate[:, f, :], ACT.Silu).then_inc(silu_done, 1)

                def hidden_high(f, no):
                    act.wait_ge(S["ffn_out"], no)
                    act.activation(act_hi[:, f, :], hid[:, f, :], ACT.Copy).then_inc(act_hi_done, 1)

                for f in range(2):
                    silu(f, L["g0"][f][0].freed[1])
                n0 = L["body_slots"][0]
                size, per = L["body_size"], L["body_per"]
                with act.Fori(0, BODIES) as i:
                    def high(n):
                        k = slots.raw[n]
                        act.wait_ge(raw_loaded[n % 2], i * 48 + 16 * (n // 2 + 1))
                        act.wait_ge(full, i * size + (slots.last[raw_of[k - 2] + 6].done - size))
                        act.activation(w_hi[:, k % 2, :], raw[:, n % 2, :], ACT.Copy).then_inc(hi_split, 1)

                    for s in range(2):
                        before = L["u0f"] if s == 0 else L["body"][0][2]
                        high(n0 + 3 * s)
                        for f in range(2):
                            hidden_high(f, i * per + before[f][0].freed[1])
                        high(n0 + 3 * s + 1)
                        for f in range(2):
                            silu(f, i * per + L["body"][s][0][f][0].freed[1])
                        high(n0 + 3 * s + 2)
                w_high(L["last_slot"])
                for f in range(2):
                    hidden_high(f, L["last_u"][f].freed[1])
            for t, u in enumerate(y_units[1]):
                rows = slice(0, P if t < PT_ else DEC)
                filled(act, u)
                act.activation(x_tm[rows, t, WIDTH:2 * WIDTH], bank(u, rows), ACT.Copy).then_inc(S["y_act"], 1)

        @block.vector
        def _(dve):
            chain = [0]

            def link(ins):
                chain[0] += 1
                ins.then_inc(dve_chain, 1)
                dve.wait_ge(dve_chain, chain[0])

            def root(l, name, n, scale):
                dve.tensor_scalar(ms[:, 0:n], ms[:, 0:n], scale, EPS, ALU.mult, ALU.add).then_inc(ms_ready, 1)
                dve.wait_ge(rs_ready, root_no(l, name))

            def low(dst, src, gain, hi):
                return dve.scalar_tensor_tensor(out=dst, in0=src, scalar=gain, in1=hi.bitcast(F32), op0=ALU.mult,
                                                op1=ALU.subtract)

            def gains(j, c0, c1):
                u = gains_units[j]
                filled(dve, u)
                dve.tensor_copy(gT[:, c0:c1], bank(u)[:, c0:c1]).then_inc(S["gains_turned"], 1)

            for t in range(NT):
                u = xt_units[t][0]
                if t == PT_:
                    gains(0, 0, G_BS)
                filled(dve, u)
                w = P if t < PT_ else DEC
                dve.tensor_copy(xT[:, 0:4, t * P:t * P + w], bank(u).rearrange("p (k c) -> p k c", k=4)[:, :, 0:w]
                                ).then_inc(S["x_turned_dve"], 1)
            dve.wait_ge(hi_split, 1)
            dve.tensor_tensor(w_lo[:, 0, :], raw[:, 0, :], w_hi[:, 0, :].bitcast(F32), ALU.subtract).then_inc(lo_split, 1)
            gains(1, G_BS, G_ROWS)
            emptied(dve, gains_units[1])
            dve.wait_ge(const_ready, 1)
            dve.scalar_tensor_tensor(out=gq[0:NOPE, 0:DEPTH], in0=gT[0:NOPE, G_QN:G_QN + DEPTH], scalar=-SCALE,
                                     in1=gT[0:NOPE, G_KN:G_KN + DEPTH], op0=ALU.mult, op1=ALU.mult).then_inc(gq_ready, 1)

            def low_part(m, k, gcol):
                dve.wait_ge(hs_hi_done, m * KT + k + 1)
                low(hs_lo[:, k, :], xT[:, k, :], gT[:, gcol + k:gcol + k + 1], hs_hi[:, k, :]).then_inc(hs_lo_done, 1)

            def r_by_token(l, name, u, no):
                filled(dve, u)
                dve.tensor_scalar(ms[:, 0:NT], bank(u, cols=NT), 1.0 / D_MODEL, EPS, ALU.mult, ALU.add
                                  ).then_inc(S["sumsq_out"], 1)
                emptied(dve, u)
                dve.tensor_copy(ms[:, 0:NT], ms[:, 0:NT]).then_inc(ms_ready, 1)
                dve.wait_ge(rs_ready, root_no(l, name))
                dve.tensor_copy(r_tok[:, 0:NT], rs[:, 0:NT]).then_inc(r_ready, 1)
                dve.wait_ge(r_ready, no)

            for l, L in enumerate(plan):
                if l == 0:
                    for k in range(KT):
                        low_part(0, k, G_MIX)
                r_by_token(l, "r1", L["ss1"], 2 * l + 1)
                for t in range(NT):
                    u = L["kv"][t]
                    filled(dve, u)
                    dve.tensor_scalar(kvz[:, t, :], bank(u, cols=KV_KR), r_tok[:, t:t + 1], None, ALU.mult
                                      ).then_inc(S["kv_out"], 1)
                emptied(dve, L["kv"][-1])
                link(dve.tensor_tensor(kvsq[:, :, :], kvz[:, :, :], kvz[:, :, :], ALU.mult))
                dve.tensor_reduce(ms[:, 0:NT], kvsq[:, :, 0:KV_LORA], AX.X, ALU.add)
                link(dve.tensor_reduce(ms[:, NT:2 * NT], kvsq[:, :, KV_LORA:KV_KR], AX.X, ALU.add))
                link(dve.tensor_scalar(ms[:, 0:NT], ms[:, 0:NT], ROPE / KV_LORA, None, ALU.mult))
                root(l, "kv", 2 * NT, 1.0 / ROPE)
                link(dve.tensor_tensor(kvz[:, :, 0:KV_LORA], kvz[:, :, 0:KV_LORA],
                                       rs[:, 0:NT].unsqueeze(2).to_broadcast([P, NT, KV_LORA]), ALU.mult))
                link(dve.tensor_tensor(kvz[:, :, KV_LORA:KV_KR], kvz[:, :, KV_LORA:KV_KR],
                                       rs[:, NT:2 * NT].unsqueeze(2).to_broadcast([P, NT, ROPE]), ALU.mult))
                dve.wait_ge(layer_loaded, 16 * SMALL * (l + 1))
                if l:
                    dve.wait_ge(rows_stored, 64 * l)
                dve.tensor_tensor(ckv_n[:, :, :], kvz[:, :, 0:KV_LORA],
                                  g_tm[:, 0:KV_LORA].unsqueeze(1).to_broadcast([P, NT, KV_LORA]), ALU.mult)
                dve.tensor_tensor(kvz[:, :, KV_LORA:KV_KR], kvz[:, :, KV_LORA:KV_KR],
                                  g_tm[:, KV_LORA:KV_KR].unsqueeze(1).to_broadcast([P, NT, ROPE]), ALU.mult
                                  ).then_inc(ckv_normed, 1)
                if l == 0:
                    dve.wait_ge(trig_loaded, 16 * NT)
                h = ROPE // 2
                g = g_tm[:, KV_KR:KV_KR + ROPE]
                dve.tensor_tensor(trig_q[:, :, 0, :], trig[:, :, :], g.unsqueeze(1).to_broadcast([P, NT, ROPE]), ALU.mult)
                dve.tensor_tensor(trig_q[:, :, 1, 0:h], trig[:, :, h:ROPE], g[:, 0:h].unsqueeze(1).to_broadcast([P, NT, h]),
                                  ALU.mult)
                dve.tensor_tensor(trig_q[:, :, 1, h:ROPE], trig[:, :, 0:h],
                                  g[:, h:ROPE].unsqueeze(1).to_broadcast([P, NT, h]), ALU.mult)
                link(dve.tensor_tensor(r_q[:, 0:NT], r_tok[:, 0:NT], r_tok[:, 0:NT], ALU.mult))
                filled(dve, L["ssq"])
                dve.tensor_tensor(ms[:, 0:NT], bank(L["ssq"], cols=NT), r_q[:, 0:NT], ALU.mult).then_inc(S["sumsq_out"], 1)
                emptied(dve, L["ssq"])
                root(l, "q", NT, 1.0 / Q_LORA)
                dve.tensor_tensor(r_q[:, 0:NT], r_tok[:, 0:NT], rs[:, 0:NT], ALU.mult).then_inc(rq_ready, 1)
                filled(dve, L["ct"][0])
                dve.tensor_copy(ckvT[:, S_KEYS:ALL_KEYS], bank(L["ct"][0])).then_inc(S["ckvt_dve"], 1)
                filled(dve, L["ct"][2])
                dve.tensor_copy(ckvT[:, 0:PAST // 2], bank(L["ct"][2])).then_inc(S["ckvt_dve"], 1)
                for j in range(2):
                    filled(dve, L["wst"][j])
                    dve.tensor_copy(wsT[:, 4 * j:4 * j + 4, :], bank(L["wst"][j]).rearrange("p (g i) -> p g i", g=4)
                                    ).then_inc(S["wst_out"], 1)
                filled(dve, L["wst"][2])
                dve.tensor_copy(wsT_s[DEC:P, :, :], bank(L["wst"][2], slice(DEC, P)).rearrange("p (g i) -> p g i", g=GROUPS)
                                ).then_inc(S["wst_out"], 1)
                emptied(dve, L["wst"][1])
                dve.memset(wsT[CHUNK:P, :, 0:CHUNK], 0.0).then_inc(wsT_masked, 1)

                emptied(dve, L["v1"][-1])
                gvg = gv[:, :, :].rearrange("p t (g d) -> p (t g) d", d=GDIM)
                n = NT * GROUPS
                link(dve.tensor_reduce(mu[:, 0:n], gvg, AX.X, ALU.add))
                link(dve.tensor_scalar(mu[:, 0:n], mu[:, 0:n], 1.0 / GDIM, None, ALU.mult))
                dve.tensor_tensor(gvg, gvg, mu[:, 0:n].unsqueeze(2).to_broadcast([P, n, GDIM]), ALU.subtract
                                  ).then_inc(v_centred, 1)
                dve.wait_ge(v_squared, l + 1)
                link(dve.tensor_reduce(ms[:, 0:n], wide[:, :].rearrange("p (n d) -> p n d", d=GDIM), AX.X, ALU.add))
                dve.tensor_scalar(ms[:, 0:n], ms[:, 0:n], 1.0 / GDIM, EPS, ALU.mult, ALU.add).then_inc(ms_ready, 1)

                def prep_asked(t):
                    seq, tile = t["seq"], t["tile"]
                    nope, rope = prep_cols(t)
                    if t["what"] == "q":
                        emptied(dve, t["up"][1])
                        dve.tensor_reduce(ms[:, rope], sq[:, seq % 2, :, NOPE:QK], AX.X, ALU.add)
                        dve.tensor_reduce(ms[:, nope], sq[:, seq % 2, :, 0:NOPE], AX.X, ALU.add).then_inc(sq_free, 1)
                        dve.wait_ge(sq_free, PREPS * l + seq + 1)
                        dve.tensor_scalar(ms[:, nope], ms[:, nope], 1.0 / NOPE, EPS, ALU.mult, ALU.add)
                        dve.tensor_scalar(ms[:, rope], ms[:, rope], 1.0 / ROPE, EPS, ALU.mult, ALU.add
                                          ).then_inc(ms_ready, 1)
                        return
                    emptied(dve, t["up"][0])
                    rows = slice(0, key_tile(tile)[1])
                    dve.tensor_reduce(ms[rows, nope], sq[rows, seq % 2, :, 0:NOPE], AX.X, ALU.add).then_inc(sq_free, 1)
                    if tile == CACHE_TILES:
                        filled(dve, L["preps"][seq - 4]["turn"][1])
                        dve.wait_ge(kr_turned, l + 1)
                        dve.tensor_copy(tm[rows, seq % 4, :, NOPE:QK],
                                        kr_n[DEC:P, PT_:PT_ + 1, :].to_broadcast([DEC, HEADS, ROPE]))
                    dve.wait_ge(sq_free, PREPS * l + seq + 1)
                    dve.tensor_scalar(ms[rows, nope], ms[rows, nope], 1.0 / NOPE, EPS, ALU.mult, ALU.add
                                      ).then_inc(ms_ready, 1)

                def prep_normed(t):
                    seq, tile = t["seq"], t["tile"]
                    nope, rope = prep_cols(t)
                    rows = slice(0, P if t["what"] == "q" else key_tile(tile)[1])
                    x = tm[rows, seq % 4, :, :]
                    dve.wait_ge(rs_ready, root_no(l, f"b{seq}"))
                    ins = dve.tensor_tensor(x[:, :, 0:NOPE], x[:, :, 0:NOPE],
                                            rs[rows, nope].unsqueeze(2).to_broadcast([rows.stop, HEADS, NOPE]), ALU.mult)
                    if t["what"] == "q":
                        xr = x[:, :, NOPE:QK]
                        link(dve.tensor_tensor(xr, xr, rs[:, rope].unsqueeze(2).to_broadcast([P, HEADS, ROPE]), ALU.mult))
                        parts = (sq[:, seq % 2, :, NOPE:QK], rot[:, :, :])
                        for e in range(2):
                            ins = dve.tensor_tensor(parts[e], xr,
                                                    trig_q[:, tile, e, :].unsqueeze(1).to_broadcast([P, HEADS, ROPE]), ALU.mult)
                        link(ins)
                        h = ROPE // 2
                        dve.tensor_tensor(xr[:, :, 0:h], parts[0][:, :, 0:h], parts[0][:, :, h:ROPE], ALU.subtract)
                        ins = dve.tensor_tensor(xr[:, :, h:ROPE], parts[1][:, :, 0:h], parts[1][:, :, h:ROPE], ALU.add)
                    ins.then_inc(tile_normed, 1)

                def prep_turned(t):
                    tile, u = t["tile"], t["turn"][0]
                    filled(dve, u)
                    src = ps[0:QK, u.bank, :].rearrange("p (h c) -> p h c", h=4)
                    if t["what"] == "q":
                        if tile == PT_:
                            dst, src = qT_s[:, 0:4, :], src[:, :, DEC:P]
                        else:
                            dst = qT_p[:, 0:4, tile * P:(tile + 1) * P]
                        dve.tensor_scalar(dst, src, gq[0:QK, l:l + 1], None, ALU.mult).then_inc(S["qkt_dve"], 1)
                    else:
                        c, w = key_tile(tile)
                        src = src[:, :, 0:w]
                        dst = kT_s[:, 0:4, c:c + w] if tile <= CACHE_TILES else kT_p[:, 0:4, c - S_KEYS:c - S_KEYS + w]
                        dve.tensor_copy(dst, src).then_inc(S["qkt_dve"], 1)

                def preps_run(todo, steps, between=lambda n: None):
                    for n in steps:
                        early = n == 1 and todo is L["s_preps"]
                        if early:
                            prep_normed(todo[0])
                        if n < len(todo):
                            prep_asked(todo[n])
                        if 1 <= n <= len(todo) and not early:
                            prep_normed(todo[n - 1])
                        if n >= 2:
                            prep_turned(todo[n - 2])
                        between(n)

                def v_affine(n):
                    for row, t, op in ((0, n - 2, ALU.mult), (1, n - 4, ALU.add)):
                        if 0 <= t < NT:
                            ins = dve.tensor_tensor(gv[:, t, :], gv[:, t, :], ln_gb[:, row, :], op)
                            if row and t == NT - 1:
                                ins.then_inc(vn_done, 1)

                preps_run(L["s_preps"], [0])
                dve.wait_ge(rs_ready, root_no(l, "ln"))
                n = NT * GROUPS
                dve.tensor_tensor(gvg, gvg, rs[:, 0:n].unsqueeze(2).to_broadcast([P, n, GDIM]), ALU.mult)
                preps_run(L["s_preps"], range(1, len(S_TILES) + 2), v_affine)

                for g2 in range(4):
                    u = L["mix"][g2]
                    filled(dve, u)
                    for e in range(2):
                        g = 2 * g2 + e
                        dst = ug[:, 0:PT_, g * GDIM:(g + 1) * GDIM]
                        ins = dve.scalar_tensor_tensor(
                            out=dst, in0=ps[:, u.bank, e * 256:(e + 1) * 256].rearrange("p (t d) -> p t d", t=PT_),
                            scalar=gT[:, G_BS + GROUPS * l + g:G_BS + GROUPS * l + g + 1], in1=dst, op0=ALU.add, op1=ALU.mult)
                    ins.then_inc(S["mix_out"], 1)
                u = L["mix"][4]
                filled(dve, u)
                for g in range(GROUPS):
                    dst = ug[DEC:P, PT_, g * GDIM:(g + 1) * GDIM]
                    ins = dve.scalar_tensor_tensor(
                        out=dst, in0=ps[DEC:P, u.bank, g * GDIM:(g + 1) * GDIM],
                        scalar=gT[DEC:P, G_BS_S + GROUPS * l + g:G_BS_S + GROUPS * l + g + 1], in1=dst,
                        op0=ALU.add, op1=ALU.mult)
                ins.then_inc(S["mix_out"], 1)

                dve.wait_ge(v_stored, 16 * (l + 1))
                for n in range(HEAD_PAIRS + 2):
                    if n >= HEAD_PAIRS:
                        preps_run(L["p_preps"], [n - HEAD_PAIRS])
                    if n < HEAD_PAIRS:
                        st = L["s_steps"][n]
                        for e, ((c, w), u) in enumerate(zip(S_SPANS, st["s"])):
                            filled(dve, u)
                            ins = dve.tensor_reduce(mx[:, 4 * (n % 2) + e:4 * (n % 2) + e + 1], bank(u, cols=w), AX.X, ALU.min)
                        link(ins)
                        dve.tensor_reduce(nm[:, n % 4, 0:1], mx[:, 4 * (n % 2):4 * (n % 2) + 3], AX.X, ALU.min).then_inc(nm_ready, 1)
                    if 1 <= n <= HEAD_PAIRS:
                        m = n - 1
                        for j in (0, 2):
                            u = L["s_steps"][m]["t"][j]
                            filled(dve, u)
                            if m >= 2 and not j:
                                filled(dve, L["s_steps"][m - 2]["o"])
                            first, count = S_TRANS[j]
                            rows = slice(0, P if j < 2 else DEC)
                            dve.tensor_copy(pT[rows, m % 2, first:first + count, :],
                                            bank(u, rows, count * P).rearrange("p (j c) -> p j c", j=count)
                                            ).then_inc(S["pt_dve"], 1)
                    if n >= 2:
                        m = n - 2
                        emptied(dve, L["s_steps"][m]["s"][-1])
                        link(dve.tensor_reduce(linv[:, m % 2, 0:1], lsum[:, m % 4, 0:3], AX.X, ALU.add))
                        link(dve.reciprocal(linv[:, m % 2, 0:1], linv[:, m % 2, 0:1]))
                        u = L["s_steps"][m]["o"]
                        filled(dve, u)
                        dve.tensor_scalar(o_s[:, m, :], bank(u, cols=VDIM), linv[:, m % 2, 0:1], None, ALU.mult
                                          ).then_inc(S["o_out"], 1)

                def part_asked(name):
                    g = int(name[1])
                    if name[0] == "o":
                        c, n = part_cols(g), O_PARTS[g][1]
                        squares = wide_o[:, g % 2, 0:n * VDIM]
                        dve.wait_ge(o_squared, (PT_ + 1) * l + g + 1)
                    else:
                        c, n = slice(g * GROUPS, (g + 1) * GROUPS), GROUPS
                        squares = wide_g[:, g * WIDTH:(g + 1) * WIDTH]
                        dve.wait_ge(gm_squared, NT * l + g + 1)
                    link(dve.tensor_reduce(ms[:, c], squares.rearrange("p (n d) -> p n d", d=VDIM), AX.X, ALU.add))
                    dve.tensor_scalar(ms[:, c], ms[:, c], 1.0 / VDIM, EPS, ALU.mult, ALU.add).then_inc(ms_ready, 1)

                def part_applied(name):
                    dve.wait_ge(rs_ready, root_no(l, name))
                    g = int(name[1])
                    c, n = O_PARTS[g]
                    o = o_tm[:, c:c + n * VDIM].rearrange("p (n d) -> p n d", d=VDIM)
                    dve.tensor_tensor(o, o, rs[:, part_cols(g)].unsqueeze(2).to_broadcast([P, n, VDIM]), ALU.mult
                                      ).then_inc(o_normed, 1)

                for what, n in P_ORDER_READERS:
                    if what == "prep":
                        preps_run(L["p_preps"], [n])
                        continue
                    if n < len(P_STEPS):
                        i, _, nh = P_STEPS[n]
                        u = L["p_steps"][n]["s"]
                        w = (i + 1) * P
                        sc = ps[:, u.bank, 0:nh * w].rearrange("p (h c) -> p h c", h=nh)
                        filled(dve, u)
                        link(dve.memset(ps[0:CHUNK, u.bank, 0:nh * w].rearrange("p (h c) -> p h c", h=nh)[:, :, w - CHUNK:w],
                                        MASKED))
                        dve.tensor_reduce(nm[:, n % 4, 0:nh], sc, AX.X, ALU.min).then_inc(nm_ready, 1)
                    if n >= 3:
                        m = n - 3
                        i, h0, nh = P_STEPS[m]
                        emptied(dve, L["p_steps"][m]["s"])
                        link(dve.reciprocal(linv[:, m % 2, 0:nh], lsum[:, m % 4, 0:nh]))
                        u = L["p_steps"][m]["o"]
                        filled(dve, u)
                        c = i * WIDTH + h0 * VDIM
                        dve.tensor_tensor(o_tm[:, c:c + nh * VDIM].rearrange("p (h d) -> p h d", h=nh),
                                          bank(u, cols=nh * VDIM).rearrange("p (h d) -> p h d", h=nh),
                                          linv[:, m % 2, 0:nh].unsqueeze(2).to_broadcast([P, nh, VDIM]), ALU.mult
                                          ).then_inc(S["o_out"], 1)
                    for name in ASKED:
                        if ASKED[name] == n:
                            part_asked(name)
                        if APPLIED.get(name) == n:
                            part_applied(name)
                for j, k in enumerate(MERGED):
                    u = L["mt"][k]
                    if k == 0:
                        part_applied(f"o{PT_}")
                    if k == KT:
                        g = G_OUT + 8 * l
                        filled(dve, u)
                        dve.tensor_tensor(ms_sb[:, :, :], bank(u).rearrange("p (k c) -> p k c", k=KT),
                                          gT[:, g:g + KT].unsqueeze(2).to_broadcast([P, KT, DEC]), ALU.mult
                                          ).then_inc(S["merged_out"], 1)
                        part_asked(f"o{PT_}")
                        dve.wait_ge(m_hi, (KT + 1) * l + j + 1)
                        dve.tensor_tensor(hs_lo[:, :, SEQ:TOK], ms_sb[:, :, :], hs_hi[:, :, SEQ:TOK].bitcast(F32),
                                          ALU.subtract).then_inc(m_lo, 1)
                        continue
                    g = G_OUT + 8 * l + k
                    dve.wait_ge(m_hi, (KT + 1) * l + j + 1)
                    low(hs_lo[:, k, 0:SEQ], bank(u), gT[:, g:g + 1], hs_hi[:, k, 0:SEQ]).then_inc(S["merged_out"], 1)

                def add_to_x(m, u):
                    x = halves(xT[:, m, :])
                    return dve.tensor_tensor(x, ps[:, u.bank:u.bank + 2, 0:HALF], x, ALU.add)

                for m in range(KT):
                    filled(dve, L["wo"][m][1])
                    add_to_x(m, L["wo"][m][0]).then_inc(S["wo_added"], 1)
                for k in range(KT):
                    low_part(2 * l + 1, k, G_FFN + KT * l)
                r_by_token(l, "r2", L["ss2"], 2 * l + 2)
                filled(dve, L["rb"][0])
                dve.tensor_copy(rb[:, 0:SEQ], bank(L["rb"][0])).then_inc(S["rb_out"], 1)
                filled(dve, L["rb"][1])
                dve.tensor_copy(rb[:, SEQ:TOK], ps[:, L["rb"][1].bank, DEC:P]).then_inc(S["rb_out"], 1)
                emptied(dve, L["rb"][1])

                def gate_in(f, u, off):
                    dve.wait_ge(full, off[0] + u[1].done)
                    dve.tensor_tensor(halves(gate[:, f, :]), ps[:, u[0].bank:u[0].bank + 2, 0:HALF], halves(rb[:, :]),
                                      ALU.mult).then_inc(S["ffn_out"], 1)

                def hidden(f, u, off, no):
                    dve.wait_ge(full, off[0] + u[1].done)
                    dve.wait_ge(gate_done, no)
                    dve.tensor_tensor(halves(hid[:, f, :]), ps[:, u[0].bank:u[0].bank + 2, 0:HALF], halves(gate[:, f, :]),
                                      ALU.mult).then_inc(S["ffn_out"], 1)
                    dve.wait_ge(act_hi_done, no)
                    dve.tensor_tensor(act_lo[:, f, :], hid[:, f, :], act_hi[:, f, :].bitcast(F32), ALU.subtract
                                      ).then_inc(act_lo_done, 1)

                def down(units, off, first=0):
                    for m, u in enumerate(units):
                        dve.wait_ge(full, off[0] + u[1].done)
                        add_to_x(first + m, u[0]).then_inc(S["ffn_out"], 1)

                pairs = 2 * FPAIRS * l
                for f in range(2):
                    gate_in(f, L["g0"][f], (0, 0))
                for f in range(2):
                    hidden(f, L["u0f"][f], (0, 0), pairs + f + 1)
                with dve.Fori(0, BODIES) as i:
                    off = (i * L["body_size"], i * L["body_per"])
                    for s in range(2):
                        g, d, u = L["body"][s]
                        for f in range(2):
                            gate_in(f, g[f], off)
                        dve.wait_ge(S["ffn_out"], off[1] + g[1][0].freed[1])
                        down(d, off)
                        for f in range(2):
                            hidden(f, u[f], off, i * 4 + (pairs + 3 + 2 * s + f))
                dve.wait_ge(S["ffn_out"], L["last_u"][1].freed[1])
                for m in range(KT + 1):
                    if m < KT:
                        down(L["last"][m:m + 1], (0, 0), m)
                    if m == Y_AFTER and l == DEPTH - 1:
                        for t, u in enumerate(y_units[0]):
                            rows = slice(0, P if t < PT_ else DEC)
                            filled(dve, u)
                            dve.tensor_copy(x_tm[rows, t, 0:WIDTH], bank(u, rows)).then_inc(S["y_dve"], 1)
                    if m and l + 1 < DEPTH:
                        low_part(2 * l + 2, m - 1, G_MIX + KT * (l + 1))

        @block.tensor
        def _(pe):
            def free(u):
                if u.before:
                    pe.wait_ge(S[u.before[0]], u.before[1])

            def split_ready(n):
                pe.wait_ge(lo_split, slots.raw[n] + 1)

            def turn(dst, src, n):
                return pe.transpose(dst, src, ident[0:n, 0:n])

            pe.wait_ge(ident_ready, 1)

            def gains(j, rows, loads):
                free(gains_units[j])
                pe.wait_ge(g_zeroed, 1)
                pe.wait_ge(gains_loaded[j], 16 * loads)
                turn(bank(gains_units[j], cols=rows), g_in[0:rows, :], rows).then_inc(full, 1)

            for t in range(NT):
                if t == PT_:
                    gains(0, G_BS, EARLY_GAINS)
                pe.wait_ge(x_loaded[t], 16)
                for e, u in enumerate(xt_units[t]):
                    free(u)
                    for j in range(4):
                        c = (4 * e + j) * P
                        if t < PT_:
                            ins = turn(ps[:, u.bank, j * P:(j + 1) * P], x_tm[:, t, c:c + P], P)
                        else:
                            ins = pe.transpose(ps[:, u.bank, j * P:j * P + DEC], x_tm[DEC:P, t, c:c + P],
                                               ident[DEC:P, DEC:P])
                    ins.then_inc(full, 1)
            gains(1, P, LATE_GAINS)
            pe.wait_ge(const_ready, 1)

            def by_token(u, t, k_w, n, cols):
                c = TILE_AT[t]
                for k in range(KT):
                    w = slice(k * cols, (k + 1) * cols)
                    x_hi, x_lo = hs_hi[:, k, c:c + P], hs_lo[:, k, c:c + P]
                    dst = bank(u, cols=cols)
                    pe.matmul(dst, x_hi, w_hi[:, k_w, w], start=(k == 0), stop=False)
                    pe.matmul(dst, x_hi, w_lo[:, k_w, w], start=False, stop=False)
                    ins = pe.matmul(dst, x_lo, w_hi[:, k_w, w], start=False, stop=(k == KT - 1))
                return ins

            def by_feature(units, k_w, at, step, count, x_hi, x_lo, ready=None, order=None, ks=None):
                order = order or range(count)
                for k in ks or order:
                    if ready:
                        ready(k)
                    first, last = k == order[0], k == order[-1]
                    w = slice(at + k * step, at + k * step + P)
                    hi, lo = w_hi[:, k_w, w], w_lo[:, k_w, w]
                    for h, u in enumerate(units):
                        cols = slice(h * HALF, (h + 1) * HALF)
                        pe.matmul(bank(u, cols=HALF), hi, x_hi[:, k, cols], start=first, stop=False)
                        pe.matmul(bank(u, cols=HALF), hi, x_lo[:, k, cols], start=False, stop=False)
                    for h, u in enumerate(units):
                        cols = slice(h * HALF, (h + 1) * HALF)
                        ins = pe.matmul(bank(u, cols=HALF), lo, x_hi[:, k, cols], start=False, stop=last)
                        if last:
                            ins.then_inc(full, 1)

            def sums_by_token(u, tiles):
                free(u)
                for t, c in enumerate(TILE_AT):
                    for m, src in enumerate(tiles):
                        ins = pe.matmul(ps[:, u.bank, t:t + 1], src[:, c:c + P], ones[:, 0:1], start=(m == 0),
                                        stop=(m == len(tiles) - 1))
                ins.then_inc(full, 1)

            def y_half(e, last):
                emptied(pe, last[4 * e + 3][0])
                for t, u in enumerate(y_units[e]):
                    w = P if t < PT_ else DEC
                    free(u)
                    for j in range(4):
                        ins = turn(ps[0:w, u.bank, j * P:(j + 1) * P], xT[:, 4 * e + j, t * P:t * P + w], P)
                    ins.then_inc(full, 1)

            for l, L in enumerate(plan):
                def tokens(units, n, cols):
                    split_ready(n)
                    for t, u in enumerate(units):
                        free(u)
                        by_token(u, t, slots.raw[n] % 2, n, cols).then_inc(full, 1)

                split_ready(L["w_in"][0])
                for m in range(2):
                    for u in L["q"][m]:
                        free(u)
                    by_feature(L["q"][m], slots.raw[L["w_in"][0]] % 2, m * P, COLS, KT, hs_hi, hs_lo,
                               ready=lambda k: pe.wait_ge(hs_lo_done, 2 * l * KT + k + 1))
                tokens(L["kv"], L["w_in"][1], KV_KR)
                pe.wait_ge(summed, (2 * l + 1) * KT)
                sums_by_token(L["ss1"], [sumsq])
                tokens(L["v0"], L["w_in"][2], COLS)
                emptied(pe, L["q"][1][1])
                sums_by_token(L["ssq"], [gate[:, 0, :], gate[:, 1, :]])
                tokens(L["v1"], L["w_in"][3], COLS)

                pe.wait_ge(ckv_normed, l + 1)
                pe.wait_ge(layer_loaded, 16 * SMALL * (l + 1))
                for j, u in enumerate(L["ct"]):
                    free(u)
                    if j == 0:
                        srcs = [ckv_n[:, t, :] for t in range(PT_)]
                    elif j == 1:
                        srcs = [ckv_n[:, PT_, :]]
                    else:
                        srcs = [cache_in[:, 4 * (j - 2) + i, :] for i in range(4)]
                    for i, src in enumerate(srcs):
                        ins = turn(ps[:, u.bank, i * P:(i + 1) * P], src, P)
                    ins.then_inc(full, 1)
                for j, u in enumerate(L["wst"]):
                    free(u)
                    if j < 2:
                        for i in range(4):
                            ins = turn(ps[:, u.bank, i * P:(i + 1) * P], ws_in[:, 4 * j + i, :], P)
                    else:
                        for g in range(GROUPS):
                            ins = pe.matmul(ps[DEC:P, u.bank, g * DEC:(g + 1) * DEC], ws_in[0:DEC, g, 0:DEC],
                                            ident[0:DEC, 0:DEC], start=True, stop=True)
                    ins.then_inc(full, 1)

                def prep_up(t):
                    tile = t["tile"]
                    for e, u in enumerate(t["up"]):
                        free(u)
                        if t["what"] == "q":
                            c = TILE_AT[tile]
                            for m in range(2):
                                w = m * HEADS * QK + e * 4 * QK
                                ins = pe.matmul(bank(u, cols=4 * QK), qlatT[:, m, c:c + P],
                                                raw[:, L["wq"] % 2, w:w + 4 * QK], start=(m == 0), stop=(m == 1))
                        else:
                            c, w = key_tile(tile)
                            wkv = raw[:, L["wkv"] % 2, 0:2 * WIDTH].rearrange("p (h c) -> p h c", h=HEADS)
                            ins = pe.matmul(ps[0:w, u.bank, :].rearrange("p (h c) -> p h c", h=HEADS),
                                            ckvT[:, c:c + w], wkv[:, :, e * NOPE:(e + 1) * NOPE],
                                            start=True, stop=True)
                        ins.then_inc(full, 1)

                def prep_turn(t):
                    seq, tile = t["seq"], t["tile"]
                    pe.wait_ge(tile_normed, PREPS * l + seq + 1)
                    if t["what"] == "k" and tile != CACHE_TILES:
                        pe.wait_ge(kr_spread, t["spreads"])
                    w = P if t["what"] == "q" else key_tile(tile)[1]
                    for e, u in enumerate(t["turn"]):
                        free(u)
                        for i in range(4):
                            ins = turn(ps[0:QK, u.bank, i * P:i * P + w], tm[0:w, seq % 4, 4 * e + i, :], w)
                        ins.then_inc(full, 1)

                def preps_run(todo, steps):
                    for n in steps:
                        if n < len(todo):
                            prep_up(todo[n])
                        if n >= 2:
                            prep_turn(todo[n - 2])

                tokens(L["u0"], L["w_in"][4], COLS)
                pe.wait_ge(raw_loaded[L["wq"] % 2], 16 * (L["wq"] // 2 + 1))
                preps_run(L["s_preps"], [0])
                tokens(L["u1"], L["w_in"][5], COLS)

                pe.wait_ge(raw_loaded[L["wkv"] % 2], 16 * (L["wkv"] // 2 + 1))
                emptied(pe, L["ct"][2])
                emptied(pe, L["ct"][3])
                preps_run(L["s_preps"], range(1, len(S_TILES) + 2))

                pe.wait_ge(vn_done, l + 1)
                pe.wait_ge(wsT_masked, l + 1)
                emptied(pe, L["u1"][-1])
                for g2 in range(4):
                    u = L["mix"][g2]
                    free(u)
                    for e in range(2):
                        g = 2 * g2 + e
                        ins = pe.matmul(ps[:, u.bank, e * 256:(e + 1) * 256].rearrange("p (t d) -> p t d", t=PT_),
                                        wsT[:, g, :], gv[:, 0:PT_, g * GDIM:(g + 1) * GDIM], start=True, stop=True)
                    ins.then_inc(full, 1)
                u = L["mix"][4]
                free(u)
                for g in range(GROUPS):
                    ins = pe.matmul(ps[DEC:P, u.bank, g * GDIM:(g + 1) * GDIM], wsT_s[DEC:P, g, :],
                                    gv[DEC:P, PT_, g * GDIM:(g + 1) * GDIM], start=True, stop=True)
                ins.then_inc(full, 1)

                emptied(pe, L["s_preps"][-1]["turn"][0])
                emptied(pe, L["s_preps"][-1]["turn"][1])
                emptied(pe, L["s_preps"][-1]["up"][1])
                for n in range(HEAD_PAIRS + 2):
                    if n >= HEAD_PAIRS:
                        preps_run(L["p_preps"], [n - HEAD_PAIRS])
                    if n < HEAD_PAIRS:
                        for (c, w), u in zip(S_SPANS, L["s_steps"][n]["s"]):
                            free(u)
                            for e in range(2):
                                ins = pe.matmul(ps[e * DEC:(e + 1) * DEC, u.bank, 0:w], qT_s[:, 2 * n + e, :],
                                                kT_s[:, 2 * n + e, c:c + w], start=True, stop=True)
                            ins.then_inc(full, 1)
                    if 1 <= n <= HEAD_PAIRS:
                        m = n - 1
                        emptied(pe, L["s_steps"][m]["s"][-1])
                        for (first, count), u in zip(S_TRANS, L["s_steps"][m]["t"]):
                            free(u)
                            for i in range(count):
                                c = (first + i) * P
                                w = min(P, S_KEYS - c)
                                ins = turn(ps[0:w, u.bank, i * P:(i + 1) * P], p_sb[:, m % 2, c:c + w], P)
                            ins.then_inc(full, 1)
                    if n >= 2:
                        m = n - 2
                        for u in L["s_steps"][m]["t"]:
                            emptied(pe, u)
                        u = L["s_steps"][m]["o"]
                        free(u)
                        for e in range(2):
                            h = 2 * m + e
                            for j in range(CACHE_TILES + 1):
                                w = key_tile(j)[1]
                                ins = pe.matmul(ps[e * DEC:(e + 1) * DEC, u.bank, 0:VDIM],
                                                pT[0:w, m % 2, j, e * DEC:(e + 1) * DEC],
                                                v_s[0:w, j, h * VDIM:(h + 1) * VDIM],
                                                start=(j == 0), stop=(j == CACHE_TILES))
                        ins.then_inc(full, 1)

                for what, n in P_ORDER:
                    if what == "prep":
                        preps_run(L["p_preps"], [n])
                        continue
                    if n < len(P_STEPS):
                        i, h0, nh = P_STEPS[n]
                        u = L["p_steps"][n]["s"]
                        w = (i + 1) * P
                        if h0 == 0:
                            for t in L["p_preps"]:
                                if t["tile"] in (i, CACHE_TILES + 1 + i):
                                    emptied(pe, t["turn"][0])
                                    emptied(pe, t["turn"][1])
                                    emptied(pe, t["up"][1])
                        free(u)
                        for e in range(nh):
                            ins = pe.matmul(ps[:, u.bank, e * w:(e + 1) * w], qT_p[:, h0 + e, i * P:(i + 1) * P],
                                            kT_p[:, h0 + e, 0:w], start=True, stop=True)
                        ins.then_inc(full, 1)
                    if 2 <= n < len(P_STEPS) + 2:
                        m = n - 2
                        i, h0, nh = P_STEPS[m]
                        emptied(pe, L["p_steps"][m]["s"])
                        u = L["p_steps"][m]["t"]
                        free(u)
                        for e in range(nh * (i + 1)):
                            ins = turn(ps[:, u.bank, e * P:(e + 1) * P], p_sb[:, m % 2, e * P:(e + 1) * P], P)
                        ins.then_inc(full, 1)
                    if n >= 3:
                        m = n - 3
                        i, h0, nh = P_STEPS[m]
                        emptied(pe, L["p_steps"][m]["t"])
                        u = L["p_steps"][m]["o"]
                        free(u)
                        for e in range(nh):
                            for j in range(i + 1):
                                ins = pe.matmul(ps[:, u.bank, e * VDIM:(e + 1) * VDIM], pT[:, m % 2, e * (i + 1) + j, :],
                                                v_p[:, j, (h0 + e) * VDIM:(h0 + e + 1) * VDIM],
                                                start=(j == 0), stop=(j == i))
                        ins.then_inc(full, 1)

                def out_tile(m, ks=None):
                    by_feature(L["wo"][m], slots.raw[L["w_o"][m // 2]] % 2, m % 2 * P, COLS, KT, hs_hi, hs_lo,
                               order=MERGED[1:], ks=ks, ready=None if m else lambda k: emptied(pe, L["mt"][k]))

                pe.wait_ge(gm_normed, NT * (l + 1))
                for k in MERGED:
                    u = L["mt"][k]
                    free(u)
                    if k == 0:
                        pe.wait_ge(m_lo, l + 1)
                        split_ready(L["w_o"][0])
                        for w in L["wo"][0]:
                            free(w)
                        out_tile(0, MERGED[1:5])
                        pe.wait_ge(o_normed, (PT_ + 1) * (l + 1))
                    elif k == KT:
                        pe.wait_ge(o_normed, (PT_ + 1) * l + 1)
                        for j in range(KT):
                            if j < 4:
                                for e in range(2):
                                    half = slice(e * DEC, (e + 1) * DEC)
                                    pe.matmul(ps[half, u.bank, j * DEC:(j + 1) * DEC], o_s[half, j, :], ident[half, half],
                                              start=True, stop=True)
                            else:
                                ins = pe.transpose(ps[:, u.bank, j * DEC:(j + 1) * DEC],
                                                   ug[DEC:P, PT_, (j - 4) * P:(j - 3) * P], ident[DEC:P, DEC:P])
                        ins.then_inc(full, 1)
                        continue
                    for t in range(PT_):
                        src = o_tm[:, t * WIDTH + k * P:t * WIDTH + (k + 1) * P] if k < 4 else ug[:, t, (k - 4) * P:(k - 3) * P]
                        ins = turn(ps[:, u.bank, t * P:(t + 1) * P], src, P)
                    ins.then_inc(full, 1)

                out_tile(0, MERGED[5:])
                for m in range(1, KT):
                    split_ready(L["w_o"][m // 2])
                    for u in L["wo"][m]:
                        free(u)
                    out_tile(m)

                def gate_or_up(pair, k_w):
                    for f in range(2):
                        by_feature(pair[f], k_w, f * P, COLS, KT, hs_hi, hs_lo)

                def r_along_columns(k):
                    if k != KT // 2 + 1:
                        return
                    pe.wait_ge(r_ready, 2 * l + 2)
                    for j, u in enumerate(L["rb"]):
                        free(u)
                        for t in (range(PT_) if j == 0 else [PT_]):
                            ins = pe.matmul(ps[:, u.bank, (t % PT_) * P:(t % PT_ + 1) * P],
                                            r_tok[:, t:t + 1].to_broadcast([P, P]), ident[:, :], start=True, stop=True)
                        ins.then_inc(full, 1)

                n = L["ffn_in"][0]
                split_ready(n)
                for f in range(2):
                    for u in L["g0"][f]:
                        free(u)
                    by_feature(L["g0"][f], slots.raw[n] % 2, f * P, COLS, KT, hs_hi, hs_lo,
                               ready=r_along_columns if f else
                               lambda k: pe.wait_ge(hs_lo_done, (2 * l + 1) * KT + k + 1))
                    if f == 0:
                        pe.wait_ge(summed, (2 * l + 2) * KT)
                        sums_by_token(L["ss2"], [sumsq])
                n = L["ffn_in"][1]
                split_ready(n)
                for f in range(2):
                    for u in L["u0f"][f]:
                        free(u)
                    by_feature(L["u0f"][f], slots.raw[n] % 2, f * P, COLS, KT, hs_hi, hs_lo)
                emptied(pe, L["rb"][1])
                n0 = L["body_slots"][0]
                pairs = 2 * FPAIRS * l
                with pe.Fori(0, BODIES) as i:
                    for s in range(2):
                        for j, groups in enumerate(L["body"][s]):
                            n = n0 + 3 * s + j
                            pe.wait_ge(lo_split, i * 6 + (slots.raw[n] + 1))
                            if j == 1:
                                pe.wait_ge(act_lo_done, i * 4 + (pairs + 2 * s + 2))
                            for m, units in enumerate(groups):
                                pe.wait_ge(S["ffn_out"], i * L["body_per"] + units[1].before[1])
                                if j == 1:
                                    by_feature(units, slots.raw[n] % 2, m * P, D_MODEL, 2, act_hi, act_lo)
                                else:
                                    by_feature(units, slots.raw[n] % 2, m * P, COLS, KT, hs_hi, hs_lo)
                n = L["last_slot"]
                split_ready(n)
                for f in range(2):
                    pe.wait_ge(act_lo_done, pairs + 2 * FPAIRS - 1 + f)
                    for m, units in enumerate(L["last"][:4]):
                        if f == 0:
                            for u in units:
                                free(u)
                        by_feature(units, slots.raw[n] % 2, m * P, D_MODEL, 2, act_hi, act_lo, ks=[f])
                for m, units in enumerate(L["last"][4:], 4):
                    for u in units:
                        free(u)
                    by_feature(units, slots.raw[n] % 2, m * P, D_MODEL, 2, act_hi, act_lo)
                    if m == Y_AFTER and l == DEPTH - 1:
                        y_half(0, L["last"])

            y_half(1, plan[-1]["last"])


OUTS = [("y_prompt", (1, SEQ, D_MODEL)), ("y_sample", (1, DEC, D_MODEL)), ("ckv_prompt", (DEPTH, 1, SEQ, KV_LORA)),
        ("krope_prompt", (DEPTH, 1, SEQ, ROPE)), ("ckv_sample", (DEPTH, 1, DEC, KV_LORA)),
        ("krope_sample", (DEPTH, 1, DEC, ROPE)), ("gmlp_v_sample", (DEPTH, 1, DEC, WIDTH))]


def kernel(**inputs):
    import concourse.bacc as bacc
    from concourse.bass_utils import run_bass_kernel_spmd

    pos = np.concatenate([np.arange(SEQ), PAST + np.arange(DEC)]).astype(np.float32)
    half = ROPE // 2
    inv = np.float32(THETA) ** (-np.arange(half, dtype=np.float32) / np.float32(half))
    ang = pos[:, None] * inv[None, :]
    arrays = {name: np.ascontiguousarray(x) for name, x in inputs.items()}
    arrays["trig"] = np.concatenate([np.cos(ang), np.sin(ang)], axis=1).astype(np.float32)

    nc = bacc.Bacc("TRN2", target_bir_lowering=False, num_devices=1)
    a = {name: nc.dram_tensor("in_" + name, x.shape, F32, kind="ExternalInput").ap() for name, x in arrays.items()}
    out = {name: nc.dram_tensor("out_" + name, shape, F32, kind="ExternalOutput").ap() for name, shape in OUTS}
    trunk(nc, a, out)
    r = run_bass_kernel_spmd(nc, [{"in_" + name: x for name, x in arrays.items()}], core_ids=[0])
    return tuple(r.results[0]["out_" + name] for name, _ in OUTS)
```
